# Optimizing a Trainium2 kernel written in Bass

```python
import jax, jax.numpy as jnp
from jax import lax
import numpy as np
import math
import jax
import jax.numpy as jnp

D_MODEL = 2048
BATCH = 1
SEQ = 256
DEPTH = 1

D_MIX = D_MODEL
D_FOURIER = D_MIX // 2
N_FOURIER_GROUPS = 4
FOURIER_GROUP = D_FOURIER // N_FOURIER_GROUPS
D_MLSTM = D_MIX - D_FOURIER
N_MLSTM_HEADS = 4
HEAD_V = D_MLSTM // N_MLSTM_HEADS
HEAD_QK = HEAD_V // 2
D_QK = N_MLSTM_HEADS * HEAD_QK
N_GATES = 4 * N_MLSTM_HEADS
D_IN = D_FOURIER + 2 * D_QK + 2 * D_MLSTM + N_GATES
CHUNK = 64
D_FF = 5632
CONV_W = 3
N_MOD = 6
EPS = 1e-6
M_INIT = -1e30


def rms_norm(x, w):
    xf = x.astype(jnp.float32)
    y = xf * lax.rsqrt(jnp.mean(xf * xf, axis=-1, keepdims=True) + EPS)
    return (y * w.astype(jnp.float32)).astype(x.dtype)

def modulate(h, shift, scale):
    return h * (1 + scale[:, None, :]) + shift[:, None, :]

def fourier_mix(u):
    B, S, _ = u.shape
    ug = u.astype(jnp.float32).reshape(B, S, N_FOURIER_GROUPS, FOURIER_GROUP)
    y = jnp.fft.fft2(ug, axes=(1, 3), norm="ortho").real
    return y.reshape(B, S, D_FOURIER).astype(u.dtype)

def mlstm_chunkwise(q, k, v, ig, fg):
    B, H, S, Dk = q.shape
    Dv = v.shape[-1]
    NC = S // CHUNK
    lf = jax.nn.log_sigmoid(fg)
    q = q.reshape(B, H, NC, CHUNK, Dk) * (Dk ** -0.5)
    k = k.reshape(B, H, NC, CHUNK, Dk)
    v = v.reshape(B, H, NC, CHUNK, Dv)
    ig = ig.reshape(B, H, NC, CHUNK)
    lf = lf.reshape(B, H, NC, CHUNK)
    b = jnp.cumsum(lf, axis=-1)
    g = b[..., -1]

    a = g[..., None] - b + ig
    m_loc = jnp.max(a, axis=-1)
    w_loc = jnp.exp(a - m_loc[..., None])
    C_loc = jnp.einsum('bhclv,bhclk->bhcvk', v * w_loc[..., None], k)
    n_loc = jnp.einsum('bhcl,bhclk->bhck', w_loc, k)

    def step(carry, inp):
        C, n, m = carry
        g_c, m_c, C_c, n_c = inp
        m_new = jnp.maximum(g_c + m, m_c)
        s_old = jnp.exp(g_c + m - m_new)
        s_loc = jnp.exp(m_c - m_new)
        C_new = s_old[..., None, None] * C + s_loc[..., None, None] * C_c
        n_new = s_old[..., None] * n + s_loc[..., None] * n_c
        return (C_new, n_new, m_new), (C, n, m)

    init = (jnp.zeros((B, H, Dv, Dk), jnp.float32),
            jnp.zeros((B, H, Dk), jnp.float32),
            jnp.full((B, H), M_INIT, jnp.float32))
    xs = (jnp.moveaxis(g, 2, 0), jnp.moveaxis(m_loc, 2, 0),
          jnp.moveaxis(C_loc, 2, 0), jnp.moveaxis(n_loc, 2, 0))
    _, (C_st, n_st, m_st) = lax.scan(step, init, xs)
    C_st = jnp.moveaxis(C_st, 0, 2)
    n_st = jnp.moveaxis(n_st, 0, 2)
    m_st = jnp.moveaxis(m_st, 0, 2)

    tri = jnp.tril(jnp.ones((CHUNK, CHUNK), dtype=bool))
    Dlog = jnp.where(tri, b[..., :, None] - b[..., None, :] + ig[..., None, :], -jnp.inf)
    inter = b + m_st[..., None]
    m_row = jnp.maximum(jnp.max(Dlog, axis=-1), inter)
    P = jnp.exp(Dlog - m_row[..., None]) * jnp.einsum('bhcjd,bhctd->bhcjt', q, k)
    s_inter = jnp.exp(inter - m_row)
    num = (jnp.einsum('bhcjt,bhctv->bhcjv', P, v)
           + s_inter[..., None] * jnp.einsum('bhcjk,bhcvk->bhcjv', q, C_st))
    den = jnp.sum(P, axis=-1) + s_inter * jnp.einsum('bhcjk,bhck->bhcj', q, n_st)
    h = num / jnp.maximum(jnp.abs(den), jnp.exp(-m_row))[..., None]
    return h.reshape(B, H, S, Dv)

def mlstm_bidirectional(q_in, k_in, v_in, gates, mlstm_norm_w):
    B, S, _ = q_in.shape
    H = N_MLSTM_HEADS
    q = q_in.astype(jnp.float32).reshape(B, S, H, HEAD_QK).transpose(0, 2, 1, 3)
    k = k_in.astype(jnp.float32).reshape(B, S, H, HEAD_QK).transpose(0, 2, 1, 3)
    v = v_in.astype(jnp.float32).reshape(B, S, H, HEAD_V).transpose(0, 2, 1, 3)
    gt = gates.astype(jnp.float32).reshape(B, S, 4, H).transpose(2, 0, 3, 1)
    i_f, f_f, i_b, f_b = gt[0], gt[1], gt[2], gt[3]
    h_fwd = mlstm_chunkwise(q, k, v, i_f, f_f)
    h_bwd = jnp.flip(mlstm_chunkwise(jnp.flip(q, 2), jnp.flip(k, 2), jnp.flip(v, 2),
                                     jnp.flip(i_b, 2), jnp.flip(f_b, 2)), 2)
    h = (h_fwd + h_bwd).transpose(0, 2, 1, 3)
    h = h * lax.rsqrt(jnp.mean(h * h, axis=-1, keepdims=True) + EPS)
    h = h.reshape(B, S, D_MLSTM) * mlstm_norm_w.astype(jnp.float32)
    return h.astype(q_in.dtype)

def depthwise_conv_centred(u, w_conv, b_conv):
    C = u.shape[-1]
    y = lax.conv_general_dilated(u, w_conv[:, None, :].astype(u.dtype), window_strides=(1,),
                                 padding='SAME', dimension_numbers=('NWC', 'WIO', 'NWC'),
                                 feature_group_count=C)
    return y + b_conv

def first_inputs(seed: int = 0) -> dict:
    key = jax.random.key(seed)
    ks = jax.random.split(key, 20)
    f32 = jnp.float32
    H = N_MLSTM_HEADS
    x = jax.random.normal(ks[0], (BATCH, SEQ, D_MODEL), f32)
    c = jax.random.normal(ks[1], (BATCH, D_MODEL), f32)
    w_ada = jax.random.normal(ks[2], (D_MODEL, N_MOD * D_MODEL), f32) * (0.5 * D_MODEL ** -0.5)
    b_ada = 0.02 * jax.random.normal(ks[3], (N_MOD * D_MODEL,), f32)
    norm1_w = 1.0 + 0.02 * jax.random.normal(ks[4], (D_MODEL,), f32)
    w_in = jax.random.normal(ks[5], (D_MODEL, D_IN), f32) * (D_MODEL ** -0.5)
    bi_f = -1.0 + 0.1 * jax.random.normal(ks[6], (H,), f32)
    bf_f = jnp.linspace(3.0, 6.0, H, dtype=f32) + 0.1 * jax.random.normal(ks[7], (H,), f32)
    bi_b = -1.0 + 0.1 * jax.random.normal(ks[8], (H,), f32)
    bf_b = jnp.linspace(3.0, 6.0, H, dtype=f32) + 0.1 * jax.random.normal(ks[9], (H,), f32)
    b_gates = jnp.concatenate([bi_f, bf_f, bi_b, bf_b])
    mlstm_norm_w = 1.0 + 0.02 * jax.random.normal(ks[10], (D_MLSTM,), f32)
    w_out = jax.random.normal(ks[11], (D_MIX, D_MODEL), f32) * (D_MIX ** -0.5)
    norm2_w = 1.0 + 0.02 * jax.random.normal(ks[12], (D_MODEL,), f32)
    w_up = jax.random.normal(ks[13], (D_MODEL, 2 * D_FF), f32) * (D_MODEL ** -0.5)
    w_conv = jax.random.normal(ks[14], (CONV_W, 2 * D_FF), f32) * (CONV_W ** -0.5)
    b_conv = 0.02 * jax.random.normal(ks[15], (2 * D_FF,), f32)
    w_down = jax.random.normal(ks[16], (D_FF, D_MODEL), f32) * (D_FF ** -0.5)
    norm_f_w = 1.0 + 0.02 * jax.random.normal(ks[17], (D_MODEL,), f32)
    return {"x": x, "c": c, "w_ada": w_ada, "b_ada": b_ada, "norm1_w": norm1_w,
            "w_in": w_in, "b_gates": b_gates, "mlstm_norm_w": mlstm_norm_w, "w_out": w_out,
            "norm2_w": norm2_w, "w_up": w_up, "w_conv": w_conv, "b_conv": b_conv,
            "w_down": w_down, "norm_f_w": norm_f_w}

def first_block(x, c, w_ada, b_ada, norm1_w, w_in, b_gates, mlstm_norm_w, w_out,
              norm2_w, w_up, w_conv, b_conv, w_down, norm_f_w):
    mod = jax.nn.silu(c) @ w_ada + b_ada
    shift1, scale1, gate1, shift2, scale2, gate2 = jnp.split(mod, N_MOD, axis=-1)
    o1 = D_FOURIER
    o2 = o1 + D_QK
    o3 = o2 + D_QK
    o4 = o3 + D_MLSTM
    o5 = o4 + D_MLSTM
    for _ in range(DEPTH):
        h = modulate(rms_norm(x, norm1_w), shift1, scale1)
        p = h @ w_in
        u_f = p[..., :o1]
        q_in, k_in, v_in = p[..., o1:o2], p[..., o2:o3], p[..., o3:o4]
        o_gate = jax.nn.sigmoid(p[..., o4:o5])
        gates = p[..., o5:] + b_gates
        y_f = fourier_mix(u_f)
        y_m = mlstm_bidirectional(q_in, k_in, v_in, gates, mlstm_norm_w) * o_gate
        mix = jnp.concatenate([y_f, y_m], axis=-1)
        x = x + gate1[:, None, :] * (mix @ w_out)
        h2 = modulate(rms_norm(x, norm2_w), shift2, scale2)
        u = depthwise_conv_centred(h2 @ w_up, w_conv, b_conv)
        a, v = jnp.split(u, 2, axis=-1)
        x = x + gate2[:, None, :] * ((jax.nn.silu(a) * v) @ w_down)
    return rms_norm(x, norm_f_w)


SSM_WIDTH = 1024
SSM_GROUP = 16
SSM_GROUPS = SSM_WIDTH // SSM_GROUP
SSM_STATE = 64
DT_MIN = 1e-3
DT_MAX = 1e-1
N_HEADS = 16
N_KV = 4
HEADS_PER_KV = N_HEADS // N_KV
HEAD_DIM = 64
CMP_LEN = 32
CMP_STRIDE = 16
CMP_HID = 256
SEL_BLOCK = 64
N_SEL = 16
WINDOW = 512
Q_BLOCK = 128
SEL_FORCE = 1e4
NEG_INF = -1e30
N_BUCKETS = 32
MAX_DIST = 1024
Q_COLS = N_HEADS * HEAD_DIM
KV_COLS = N_KV * HEAD_DIM
NSA_GATE_COLS = 3 * N_HEADS
IN_COLS = SSM_WIDTH + Q_COLS + 6 * KV_COLS + NSA_GATE_COLS + 2 * D_MODEL


def _rmsnorm(x, g):
    xf = x.astype(jnp.float32)
    ms = jnp.mean(xf * xf, axis=-1, keepdims=True)
    return (xf * lax.rsqrt(ms + EPS)).astype(x.dtype) * g

def _swiglu(x, wg, wu, wd):
    return (jax.nn.silu(x @ wg) * (x @ wu)) @ wd

def _rel_bucket(dist):
    dist = jnp.maximum(dist, 0)
    max_exact = N_BUCKETS // 2
    d_f = jnp.maximum(dist, 1).astype(jnp.float32)
    large = max_exact + (jnp.log(d_f / max_exact) / math.log(MAX_DIST / max_exact)
                         * (N_BUCKETS - max_exact)).astype(jnp.int32)
    large = jnp.minimum(large, N_BUCKETS - 1)
    return jnp.where(dist < max_exact, dist, large)

def _masked_softmax(logits_f32, valid):
    return jax.nn.softmax(jnp.where(valid, logits_f32, NEG_INF), axis=-1)

def _ssm_combine(e1, e2):
    a1r, a1i, b1r, b1i = e1
    a2r, a2i, b2r, b2i = e2
    ar = a1r * a2r - a1i * a2i
    ai = a1r * a2i + a1i * a2r
    br = a2r * b1r - a2i * b1i + b2r
    bi = a2r * b1i + a2i * b1r + b2i
    return (ar, ai, br, bi)

def _s5(u, a_re, a_im, log_dt, b_re, b_im, c_re, c_im, d_skip):
    b_, t_, _ = u.shape
    ug = u.reshape(b_, t_, SSM_GROUPS, SSM_GROUP)
    dt = jnp.exp(log_dt)[:, None]
    lam_re = jnp.minimum(a_re, -1e-4)
    lam_im = a_im
    mag = jnp.exp(lam_re * dt)
    ab_re = mag * jnp.cos(lam_im * dt)
    ab_im = mag * jnp.sin(lam_im * dt)
    den = lam_re * lam_re + lam_im * lam_im
    n_re = ab_re - 1.0
    n_im = ab_im
    co_re = (n_re * lam_re + n_im * lam_im) / den
    co_im = (n_im * lam_re - n_re * lam_im) / den
    bb_re = co_re[..., None] * b_re - co_im[..., None] * b_im
    bb_im = co_re[..., None] * b_im + co_im[..., None] * b_re
    bu_re = jnp.einsum('btgc,gpc->tbgp', ug, bb_re)
    bu_im = jnp.einsum('btgc,gpc->tbgp', ug, bb_im)
    a_shape = (t_, 1, SSM_GROUPS, SSM_STATE)
    a_r = jnp.broadcast_to(ab_re[None, None], a_shape)
    a_i = jnp.broadcast_to(ab_im[None, None], a_shape)
    _, _, x_re, x_im = lax.associative_scan(_ssm_combine, (a_r, a_i, bu_re, bu_im), axis=0)
    y = (jnp.einsum('tbgp,gcp->btgc', x_re, c_re)
         - jnp.einsum('tbgp,gcp->btgc', x_im, c_im)
         + d_skip.reshape(SSM_GROUPS, SSM_GROUP) * ug)
    return y.reshape(b_, t_, SSM_WIDTH)

def _compress(raw, pos, w1, w2):
    b_, t_, _ = raw.shape
    n_sub = CMP_LEN // CMP_STRIDE
    nh = t_ // CMP_STRIDE
    nc = nh - n_sub + 1
    kk = raw.reshape(b_, nh, CMP_STRIDE, N_KV, HEAD_DIM)
    blocks = jnp.concatenate([kk[:, i:i + nc] for i in range(n_sub)], axis=2)
    blocks = blocks + pos[None, None, :, None, :]
    flat = blocks.transpose(0, 1, 3, 2, 4).reshape(b_, nc, N_KV, CMP_LEN * HEAD_DIM)
    return jax.nn.gelu(flat @ w1) @ w2

def _nsa(q, kc_raw, vc_raw, ks_raw, vs_raw, kw_raw, vw_raw, g_logits,
         cmp_pos, ck_w1, ck_w2, cv_w1, cv_w2, rel_bias):
    b_, t_, _ = q.shape
    G, HPG, dh = N_KV, HEADS_PER_KV, HEAD_DIM
    scale = dh ** -0.5
    f32 = jnp.float32
    qh = q.reshape(b_, t_, G, HPG, dh)
    gates = jax.nn.sigmoid(g_logits.reshape(b_, t_, G, HPG, 3))
    k_cmp = _compress(kc_raw, cmp_pos, ck_w1, ck_w2)
    v_cmp = _compress(vc_raw, cmp_pos, cv_w1, cv_w2)
    nc = k_cmp.shape[1]
    ns = t_ // SEL_BLOCK
    k_sel = min(N_SEL, ns)
    kblk = ks_raw.reshape(b_, ns, SEL_BLOCK, G, dh).transpose(0, 3, 1, 2, 4)
    vblk = vs_raw.reshape(b_, ns, SEL_BLOCK, G, dh).transpose(0, 3, 1, 2, 4)
    pad = ((0, 0), (WINDOW, 0), (0, 0), (0, 0))
    kwp = jnp.pad(kw_raw.reshape(b_, t_, G, dh), pad)
    vwp = jnp.pad(vw_raw.reshape(b_, t_, G, dh), pad)
    cmp_start = jnp.arange(nc) * CMP_STRIDE
    cmp_end = cmp_start + CMP_LEN - 1
    blk_ids = jnp.arange(ns)
    sel_start = blk_ids * SEL_BLOCK
    overlap = ((cmp_start[:, None] < sel_start[None, :] + SEL_BLOCK)
               & (cmp_start[:, None] + CMP_LEN > sel_start[None, :])).astype(f32)
    table_g = rel_bias.reshape(N_BUCKETS, G, HPG).transpose(1, 0, 2)
    bi = jnp.arange(b_)[:, None, None, None]
    gi = jnp.arange(G)[None, :, None, None]

    def dense_bias(dist):
        bias = rel_bias[_rel_bucket(dist)].reshape(dist.shape + (G, HPG))
        return bias.transpose(2, 3, 0, 1).astype(f32)

    def block(n):
        q0 = n * Q_BLOCK
        t = q0 + jnp.arange(Q_BLOCK)
        qb = lax.dynamic_slice_in_dim(qh, q0, Q_BLOCK, axis=1)
        gb = lax.dynamic_slice_in_dim(gates, q0, Q_BLOCK, axis=1)
        dist_c = t[:, None] - cmp_end[None, :]
        s_c = jnp.einsum('bqghd,bkgd->bghqk', qb, k_cmp).astype(f32) * scale + dense_bias(dist_c)
        p_c = _masked_softmax(s_c, dist_c >= 0) * (t >= CMP_LEN - 1).astype(f32)[:, None]
        o_c = jnp.einsum('bghqk,bkgd->bqghd', p_c.astype(v_cmp.dtype), v_cmp)
        imp = jnp.einsum('bghqk,kj->bgqj', p_c, overlap)
        valid_b = sel_start[None, :] <= t[:, None]
        cur = (t // SEL_BLOCK)[:, None]
        forced = valid_b & ((blk_ids[None, :] == 0) | (blk_ids[None, :] == cur)
                            | (blk_ids[None, :] == cur - 1))
        score = jnp.where(forced, SEL_FORCE, jnp.where(valid_b, imp, -SEL_FORCE))
        _, idx = lax.top_k(score, k_sel)
        ks_len = k_sel * SEL_BLOCK
        kg = kblk[bi, gi, idx].reshape(b_, G, Q_BLOCK, ks_len, dh)
        vg = vblk[bi, gi, idx].reshape(b_, G, Q_BLOCK, ks_len, dh)
        pos_s = (idx[..., None] * SEL_BLOCK + jnp.arange(SEL_BLOCK)).reshape(b_, G, Q_BLOCK, ks_len)
        dist_s = t[None, None, :, None] - pos_s
        bias_s = jnp.moveaxis(table_g[gi, _rel_bucket(dist_s)], -1, 2).astype(f32)
        s_s = jnp.einsum('bqghd,bgqkd->bghqk', qb, kg).astype(f32) * scale + bias_s
        p_s = _masked_softmax(s_s, (dist_s >= 0)[:, :, None])
        o_s = jnp.einsum('bghqk,bgqkd->bqghd', p_s.astype(vg.dtype), vg)
        kwb = lax.dynamic_slice_in_dim(kwp, q0, Q_BLOCK + WINDOW, axis=1)
        vwb = lax.dynamic_slice_in_dim(vwp, q0, Q_BLOCK + WINDOW, axis=1)
        pos_w = q0 - WINDOW + jnp.arange(Q_BLOCK + WINDOW)
        dist_w = t[:, None] - pos_w[None, :]
        valid_w = (dist_w >= 0) & (dist_w < WINDOW) & (pos_w >= 0)[None, :]
        s_w = jnp.einsum('bqghd,bkgd->bghqk', qb, kwb).astype(f32) * scale + dense_bias(dist_w)
        p_w = _masked_softmax(s_w, valid_w)
        o_w = jnp.einsum('bghqk,bkgd->bqghd', p_w.astype(vwb.dtype), vwb)
        return gb[..., 0:1] * o_c + gb[..., 1:2] * o_s + gb[..., 2:3] * o_w

    outs = lax.map(block, jnp.arange(t_ // Q_BLOCK))
    return jnp.moveaxis(outs, 0, 1).reshape(b_, t_, N_HEADS * dh)

def second_inputs(seed: int = 0) -> dict:
    key = jax.random.key(seed)
    ks = iter(jax.random.split(key, 48))
    L = DEPTH

    def nrm(shape, scale):
        return jax.random.normal(next(ks), shape, jnp.float32) * scale

    def gain():
        return 1.0 + nrm((L, D_MODEL), 0.05)

    G, P, C = SSM_GROUPS, SSM_STATE, SSM_GROUP
    return {
        "x": nrm((BATCH, SEQ, D_MODEL), 1.0),
        "ffn1_pre_g": gain(),
        "ffn1_w_gate": nrm((L, D_MODEL, D_FF), D_MODEL ** -0.5),
        "ffn1_w_up": nrm((L, D_MODEL, D_FF), D_MODEL ** -0.5),
        "ffn1_w_down": nrm((L, D_FF, D_MODEL), D_FF ** -0.5),
        "ffn1_post_g": gain(),
        "mix_pre_g": gain(),
        "w_in": nrm((L, D_MODEL, IN_COLS), D_MODEL ** -0.5),
        "ssm_a_re": -0.5 + nrm((L, G, P), 0.01),
        "ssm_a_im": math.pi * jnp.arange(P, dtype=jnp.float32)[None, None, :] + nrm((L, G, P), 0.01),
        "ssm_log_dt": jax.random.uniform(next(ks), (L, G), jnp.float32,
                                         minval=math.log(DT_MIN), maxval=math.log(DT_MAX)),
        "ssm_b_re": nrm((L, G, P, C), (2 * C) ** -0.5),
        "ssm_b_im": nrm((L, G, P, C), (2 * C) ** -0.5),
        "ssm_c_re": nrm((L, G, C, P), (2 * P) ** -0.5),
        "ssm_c_im": nrm((L, G, C, P), (2 * P) ** -0.5),
        "ssm_d": nrm((L, SSM_WIDTH), 1.0),
        "ssm_glu_w1": nrm((L, SSM_WIDTH, D_MODEL), SSM_WIDTH ** -0.5),
        "ssm_glu_w2": nrm((L, SSM_WIDTH, D_MODEL), SSM_WIDTH ** -0.5),
        "cmp_pos": nrm((L, CMP_LEN, HEAD_DIM), 0.02),
        "cmp_k_w1": nrm((L, CMP_LEN * HEAD_DIM, CMP_HID), (CMP_LEN * HEAD_DIM) ** -0.5),
        "cmp_k_w2": nrm((L, CMP_HID, HEAD_DIM), CMP_HID ** -0.5),
        "cmp_v_w1": nrm((L, CMP_LEN * HEAD_DIM, CMP_HID), (CMP_LEN * HEAD_DIM) ** -0.5),
        "cmp_v_w2": nrm((L, CMP_HID, HEAD_DIM), CMP_HID ** -0.5),
        "nsa_w_o": nrm((L, N_HEADS * HEAD_DIM, D_MODEL), (N_HEADS * HEAD_DIM) ** -0.5),
        "w_out": nrm((L, D_MODEL, D_MODEL), D_MODEL ** -0.5),
        "mix_post_g": gain(),
        "ffn2_pre_g": gain(),
        "ffn2_w_gate": nrm((L, D_MODEL, D_FF), D_MODEL ** -0.5),
        "ffn2_w_up": nrm((L, D_MODEL, D_FF), D_MODEL ** -0.5),
        "ffn2_w_down": nrm((L, D_FF, D_MODEL), D_FF ** -0.5),
        "ffn2_post_g": gain(),
        "rel_bias": nrm((N_BUCKETS, N_HEADS), 0.5),
    }

def second_block(x, ffn1_pre_g, ffn1_w_gate, ffn1_w_up, ffn1_w_down, ffn1_post_g,
              mix_pre_g, w_in, ssm_a_re, ssm_a_im, ssm_log_dt, ssm_b_re, ssm_b_im,
              ssm_c_re, ssm_c_im, ssm_d, ssm_glu_w1, ssm_glu_w2, cmp_pos,
              cmp_k_w1, cmp_k_w2, cmp_v_w1, cmp_v_w2, nsa_w_o, w_out, mix_post_g,
              ffn2_pre_g, ffn2_w_gate, ffn2_w_up, ffn2_w_down, ffn2_post_g, rel_bias):
    widths = [SSM_WIDTH, Q_COLS] + [KV_COLS] * 6 + [NSA_GATE_COLS, D_MODEL, D_MODEL]
    split_at = np.cumsum(widths)[:-1].tolist()
    h = x
    for l in range(DEPTH):
        f1 = _swiglu(_rmsnorm(h, ffn1_pre_g[l]), ffn1_w_gate[l], ffn1_w_up[l], ffn1_w_down[l])
        h = h + 0.5 * _rmsnorm(f1, ffn1_post_g[l])
        u = _rmsnorm(h, mix_pre_g[l])
        proj = u @ w_in[l]
        (u_ssm, q, kc, vc, ksl, vsl, kw, vw, g_nsa, g_a, g_b) = jnp.split(proj, split_at, axis=-1)
        y_ssm = jax.nn.gelu(_s5(u_ssm, ssm_a_re[l], ssm_a_im[l], ssm_log_dt[l], ssm_b_re[l],
                                ssm_b_im[l], ssm_c_re[l], ssm_c_im[l], ssm_d[l]))
        y_a = (y_ssm @ ssm_glu_w1[l]) * jax.nn.sigmoid(y_ssm @ ssm_glu_w2[l])
        o_nsa = _nsa(q, kc, vc, ksl, vsl, kw, vw, g_nsa, cmp_pos[l], cmp_k_w1[l], cmp_k_w2[l],
                     cmp_v_w1[l], cmp_v_w2[l], rel_bias)
        y_b = o_nsa @ nsa_w_o[l]
        mixed = (jax.nn.sigmoid(g_a) * y_a + jax.nn.sigmoid(g_b) * y_b) @ w_out[l]
        h = h + _rmsnorm(mixed, mix_post_g[l])
        f2 = _swiglu(_rmsnorm(h, ffn2_pre_g[l]), ffn2_w_gate[l], ffn2_w_up[l], ffn2_w_down[l])
        h = h + 0.5 * _rmsnorm(f2, ffn2_post_g[l])
    return h


def setup_inputs(seed=0):
    out = dict(first_inputs(seed))
    for name, value in second_inputs(seed + 1).items():
        if name != "x":
            out[name + "_2"] = value
    return out


def reference(
    x, c, w_ada, b_ada, norm1_w, w_in, b_gates, mlstm_norm_w, w_out, norm2_w, w_up, w_conv,
    b_conv, w_down, norm_f_w, ffn1_pre_g_2, ffn1_w_gate_2, ffn1_w_up_2, ffn1_w_down_2,
    ffn1_post_g_2, mix_pre_g_2, w_in_2, ssm_a_re_2, ssm_a_im_2, ssm_log_dt_2, ssm_b_re_2,
    ssm_b_im_2, ssm_c_re_2, ssm_c_im_2, ssm_d_2, ssm_glu_w1_2, ssm_glu_w2_2, cmp_pos_2,
    cmp_k_w1_2, cmp_k_w2_2, cmp_v_w1_2, cmp_v_w2_2, nsa_w_o_2, w_out_2, mix_post_g_2,
    ffn2_pre_g_2, ffn2_w_gate_2, ffn2_w_up_2, ffn2_w_down_2, ffn2_post_g_2, rel_bias_2,
):
    x = first_block(
        x, c, w_ada, b_ada, norm1_w, w_in, b_gates, mlstm_norm_w, w_out, norm2_w, w_up, w_conv,
        b_conv, w_down, norm_f_w,
    )
    return second_block(
        x, ffn1_pre_g_2, ffn1_w_gate_2, ffn1_w_up_2, ffn1_w_down_2, ffn1_post_g_2, mix_pre_g_2,
        w_in_2, ssm_a_re_2, ssm_a_im_2, ssm_log_dt_2, ssm_b_re_2, ssm_b_im_2, ssm_c_re_2,
        ssm_c_im_2, ssm_d_2, ssm_glu_w1_2, ssm_glu_w2_2, cmp_pos_2, cmp_k_w1_2, cmp_k_w2_2,
        cmp_v_w1_2, cmp_v_w2_2, nsa_w_o_2, w_out_2, mix_post_g_2, ffn2_pre_g_2, ffn2_w_gate_2,
        ffn2_w_up_2, ffn2_w_down_2, ffn2_post_g_2, rel_bias_2,
    )


_drawn_inputs = setup_inputs


def setup_inputs(seed=0):
    import zlib

    import numpy as np

    out = dict(_drawn_inputs(seed))
    spreads = {}
    factors = {'norm1_w': 6.776,
     'mlstm_norm_w': 8.0,
     'norm2_w': 7.417,
     'b_conv': 7.484,
     'ssm_a_re_2': 200.0,
     'cmp_pos_2': 6.415,
     'ffn2_post_g_2': 3.473,
     'ssm_a_im_2': 31.44,
     'ssm_log_dt_2': 33.72,
     'ssm_b_re_2': 43.624,
     'ssm_b_im_2': 43.52,
     'ssm_c_re_2': 43.784,
     'ssm_c_im_2': 43.64}
    for name, (base, spread) in spreads.items():
        noise = np.random.default_rng([zlib.crc32(name.encode()), seed]).standard_normal(out[name].shape)
        drawn = base * np.exp(spread * noise) if base else spread * noise
        out[name] = jnp.asarray(drawn.astype(out[name].dtype))
    for name, factor in factors.items():
        out[name] = (out[name] * factor).astype(out[name].dtype)
    return out
```

```python
import math
from contextlib import ExitStack

import numpy as np
import concourse.bass as bass
from concourse import mybir

F32 = mybir.dt.float32
F32R = mybir.dt.float32r
ACT = mybir.ActivationFunctionType
ALU = mybir.AluOpType
AX = mybir.AxisListType
ds = bass.ds

P = 128
T = 256
MT = T // P
D = 2048
KC = D // P
FF = 5632
FC = FF // P
PARTS = ((0, 24), (24, 20))
EPS = 1e-6
UNIT = 2048
SLOTS = 4
HALF = 1024
HEADS1, DK, DV = 4, 128, 256
G_IN2 = 3584
GA_IN2 = G_IN2 + 48
GB_IN2 = GA_IN2 + D
NH, NKV, DH = 16, 4, 64
NCMP = 15
NEG = -1e30
ST = 32
TWO_PI = 2 * math.pi
ROUND = 1.5 * 2.0 ** 23


class Steps:

    def __init__(self, eng, sem):
        self.eng, self.sem, self.n = eng, sem, 0

    def then(self, ins):
        self.n += 1
        ins.then_inc(self.sem, 1)
        self.eng.wait_ge(self.sem, self.n)


def stream_plan():
    order = [("ada", 96, True), ("in_tiles", 16, True), ("in_rows", 16, True), ("out1", 16, True)]

    def ffn(n):
        for part, (_, chunks) in enumerate(PARTS):
            order.append((f"up{n}{part}", 2 * chunks, True))
            order.append((f"down{n}{part}", chunks, True))

    ffn(0)
    ffn(1)
    order += [("in2", 28, True), ("cmp", 4, False), ("merge", 64, True),
              ("out2", 16, True)]
    ffn(2)
    plan, unit, split, direct = {}, 0, 0, 0
    for name, n, is_split in order:
        plan[name] = (unit, split, direct, n)
        unit += n
        counts = 2 * n if name == "ada" else n
        split, direct = (split + counts, direct) if is_split else (split, direct + n)
    return plan


def build(nc, I, out, stop=None):
    plan = stream_plan()
    ctx = ExitStack()

    def sem(name):
        return ctx.enter_context(nc.semaphore(name))

    base = 16512
    here = [base]

    def sb(name, cols, dt=F32, at=None, parts=P):
        at = here[0] if at is None else at
        t = nc.alloc_sbuf_tensor_at(name, [parts, cols], dt, offset=at)
        here[0] = max(here[0], at + (4 * cols + 31) // 32 * 32)
        return t

    stage = sb("stage", SLOTS * UNIT)
    w_hi = sb("w_hi", 2 * UNIT, F32R)
    w_lo = sb("w_lo", 2 * UNIT, F32R)
    xt_hi = sb("xt_hi", KC * T, F32R)
    xt_lo = sb("xt_lo", KC * T, F32R)
    x_nat = sb("x_nat", MT * D)
    OV = here[0]
    hid_hi = sb("hid_hi", 24 * T, F32R)
    hid_lo = sb("hid_lo", 24 * T, F32R)
    FN = here[0]
    f_nat = sb("f_nat", MT * D)
    RB = here[0]
    row = sb("row", D)
    ident = sb("ident", P)
    cols = sb("cols", 6 * P)
    mod = sb("mod", 96)
    scale_cols = sb("scale_cols", 2 * KC)
    csilu = sb("csilu", KC)
    bgate = sb("bgate", 4)
    stats = sb("stats", 32)
    TT = here[0]
    turn = sb("turn", 2 * 512)
    conv_a = sb("conv_a", 2 * T)
    conv_v = sb("conv_v", 2 * T)
    hval = sb("hval", 2 * T)
    MISC = here[0]

    projt = sb("projt", 16 * T, at=OV)
    v_one = sb("v_one", MT * HEADS1 * 257, at=OV + 16384)
    o_sig = sb("o_sig", MT * 1024, at=OV + 24640)
    dft1 = sb("dft1", 2 * 512, at=OV + 32832)
    dft2 = sb("dft2", 2 * 512, at=OV + 36928)
    four = sb("four", MT * 512, at=OV + 41024)
    rows1 = sb("rows1", 6 * T, at=OV, parts=4)
    pt1 = sb("pt1", 4 * T, at=OV + 32832)
    ex1 = sb("ex1", 4 * T, at=OV + 36928)
    h_nat = sb("h_nat", MT * 1024, at=FN)
    mask1 = sb("mask1", 4 * T, at=FN + 8192)
    grow = sb("grow", 4 * T, at=TT, parts=4)
    lfrow = sb("lfrow", 2 * T, at=TT + 4096, parts=4)
    crow = sb("crow", 2 * T, at=TT + 6144, parts=4)
    wg_raw = sb("wg_raw", KC * 48)
    wg_hi = sb("wg_hi", KC * 48, F32R, at=FN)
    wg_lo = sb("wg_lo", KC * 48, F32R, at=FN + 3072)
    g_nat = sb("g_nat", MT * 48)
    ecols = sb("ecols", 32)
    dcols = sb("dcols", 64)
    SEL = here[0]
    sel1 = sb("sel1", 4 * P, parts=4)
    ones1 = sb("ones1", T, parts=4)
    mod_row = sb("mod_row", 6 * D, at=OV, parts=64)
    rowtab = sb("rowtab", 6 * P, at=TT)
    pt2 = sb("pt2", 28 * T, at=OV)
    swp = sb("swp", 4 * T, at=OV + 28672)
    v_nat = sb("v_nat", 4 * T, at=OV + 32768)
    o_nat = sb("o_nat", MT * 1024, at=OV + 36864)
    raw_k = sb("raw_k", 16 * 60, at=OV + 36864)
    raw_v = sb("raw_v", 16 * 60, at=OV + 40960)
    soft = sb("soft", 2 * 384, at=OV + 45056)
    strips = sb("strips", NH * T, at=FN)
    ps_hi = sb("ps_hi", 8 * T, F32R, at=FN)
    ps_lo = sb("ps_lo", 8 * T, F32R, at=FN + 8192)
    sgates = sb("sgates", 5 * T, at=OV + 40960)
    po_hi = sb("po_hi", 8 * T, F32R, at=RB)
    po_lo = sb("po_lo", 8 * T, F32R, at=TT)
    turned = sb("turned", 2 * 384, at=TT)
    hid_n = sb("hid_n", 2 * T, at=TT + 4096, parts=60)
    hid_t = sb("hid_t", 2 * 120, at=TT + 6144)
    kc_t = sb("kc_t", 60)
    vc_n = sb("vc_n", T, parts=15)
    w2 = sb("w2", 2 * P + P, at=SEL)
    cmp_s = sb("cmp_s", 2 * 240, at=RB)
    cmp_t = sb("cmp_t", 2 * 512, at=RB + 2048, parts=15)
    biasc = sb("biasc", 2 * 240, at=RB + 6144)
    oh_rev = sb("oh_rev", 384, at=TT, parts=33)
    oh_fwd = sb("oh_fwd", 512, at=TT + 1536, parts=33)
    rev_sb = sb("rev_sb", 384, at=TT + 3584, parts=16)
    relb = sb("relb", 16, parts=33)
    pos2 = sb("pos2", P, at=SEL + 1536, parts=32)
    pos_t = sb("pos_t", 32)
    live = sb("live", 1)
    sm = sb("sm", 256, at=SEL + 2048)
    S5 = OV + 8192
    bc = sb("bc", 2 * ST * 16, at=S5)
    cc = sb("cc", 2 * 8 * P, at=S5 + 4096)
    bn = sb("bn", 2 * 512, at=S5 + 12288)
    bt = sb("bt", 2 * 512, at=S5 + 16384)
    cw = sb("cw", 2 * 3 * 512, at=S5 + 20480)
    ct = sb("ct", 4 * P, at=S5 + 32768)
    par = sb("par", 20 * ST, at=S5 + 34816)
    trow = sb("trow", T, at=S5 + 37376)
    cmask = sb("cmask", 32, at=S5 + 38400)
    WR = base + SLOTS * UNIT * 4
    trig = sb("trig", 2 * 512, at=WR)
    sine = sb("sine", 2 * 512, at=WR + 4096)
    cosine = sb("cosine", 2 * 512, at=WR + 8192)
    rot_r = sb("rot_r", 512, at=WR + 12288)
    rot_i = sb("rot_i", 512, at=WR + 14336)
    z_r = sb("z_r", 2 * 512, at=WR + 16384)
    z_i = sb("z_i", 2 * 512, at=WR + 20480)
    backs = [sb("back_even", 4 * 512, at=WR + 24576), sb("back_odd", 4 * 512, at=base + 3 * UNIT * 4)]
    assert here[0] <= nc.sbuf_usable_end, (here[0], nc.sbuf_usable_end)

    ps = ctx.enter_context(nc.psum_tensor("ps", [P, 8 * 512], F32))
    gates_dram = nc.dram_tensor("gates_scratch", [2, D], F32).ap()
    modrow_dram = nc.dram_tensor("modrow_scratch", [2, 6 * D], F32).ap()
    rev_dram = nc.dram_tensor("rev_scratch", [16, P, 384], F32).ap()

    landed = [sem(f"landed{s}") for s in range(SLOTS)]
    hi_made = sem("hi_made")
    split_made = sem("split_made")
    split_used = sem("split_used")
    direct_used = sem("direct_used")
    act_step = sem("act_step")
    dve_step = sem("dve_step")
    pool_step = sem("pool_step")

    names = """const_in tab_in tab_ready tab_turned cols_made c_in c_turned silu_made mod_made x_in
        ada_taken modrow_out modrow_in mod_turned crep_hi crep_made norm_ssq norm_var norm_std norm_xhat norm_rs piece_made norm_turned norm_scaled norm_hi norm_done
        tile_copied rows_taken wg_in wg_split_hi wg_split g_made g_copied
        dft_in four1 four1_copied four2 four2_copied four2_hi mix_lo
        gt_made grow_made f_exp f_add f_ln rows_made ec_made ec_copied em_made
        bcast_made score_made arg_made exp_made pt_made num_made num_taken h_ssq h_var h_std h_done
        ym_turned ym_copied ym_hi row_in row_used gate_out mask_in
        pair_e1 pair_d1 pair_e2 pair_d2 pair_e3 hid_made conv_step x_made out_done
        q_scaled swapped vt_made vn_copied oh_in rev_made rev_copied rev_out strips_in biasc_made
        biasc_copied small_in pos_made pos_copied raw_made hn_gelu ht_made ht_copied kv_made
        kv_copied cs_made cs_max cs_exp cs_done ct_made ct_copied co_made co_copied sc_made sc_max sc_exp
        pt_turned pt_copied av_made av_taken o_added on_turned on_copied on_hi on_lo
        s5_in p_dt p_x p_mag p_phi p_sin bn_made bt_made bt_copied cw_made
        ang_made ang_sin cos_made bu_made scan_made back_made y_made y_sum y_hi y_lo
        mg_a mg_b mg_2 mg_d mg_sum mg_hi mixed_made
        """.split()
    S = {n: sem(n) for n in names}
    dve_merge = sem("dve_merge")
    N_SMALL, N_S5 = 7, 8

    W = {
        "ada": I["w_ada"], "in_tiles": I["w_in"], "in_rows": I["w_in"], "out1": I["w_out"],
        "in2": I["w_in_2"], "out2": I["w_out_2"],
    }
    ffn_w = [
        dict(up=(I["w_up"], I["w_up"]), off=(0, FF), down=I["w_down"], conv=True),
        dict(up=(I["ffn1_w_gate_2"], I["ffn1_w_up_2"]), off=(0, 0), down=I["ffn1_w_down_2"], conv=False),
        dict(up=(I["ffn2_w_gate_2"], I["ffn2_w_up_2"]), off=(0, 0), down=I["ffn2_w_down_2"], conv=False),
    ]

    def bank(b, a=0, n=512, parts=P):
        return ps[0:parts, b * 512 + a:b * 512 + a + n]

    def chunk(t, k, m=None):
        return t[:, k * T:(k + 1) * T] if m is None else t[:, k * T + m * P:k * T + (m + 1) * P]

    def slot(s):
        return stage[:, s * UNIT:(s + 1) * UNIT]

    stages = ["prep", "ada", "norm0", "in", "four", "mlstm", "out1", "ffn0", "final1", "ffn1",
              "mix2", "cmp", "attn", "s5", "merge", "out2", "ffn2"]
    upto = len(stages) if stop is None else stages.index(stop) + 1
    run = set(stages[:upto])

    TABLE_ROWS = (128, 96, 120, 104, 120, 64)
    C_ADA, C_N1, C_N2 = 0, 96, 112
    C_CONV = (P, 2 * P, 3 * P)
    C_SD = P + 88
    C_F1, C_MP = 2 * P + 88, 2 * P + 104
    C_F2 = 3 * P + 88
    C_CB, C_ARE = 4 * P, 4 * P + 88
    C_AIM, C_LDT = 5 * P, 5 * P + 32

    ctx.enter_context(nc.allow_non_contiguous_dma(reason="small vectors are laid along the partitions"))
    block_scope = nc.Block()
    block = block_scope.__enter__()

    @block.sync
    def _(sp):
        def load(name, body_units, n_iter, fetch):
            first, split, direct, _ = plan[name]
            is_direct = name == "cmp"
            used, before = (direct_used, direct) if is_direct else (split_made, split)

            def body(i, fresh):
                for u in range(body_units):
                    moves = fetch(i, u)
                    if u >= SLOTS or not fresh:
                        step = 2 if name == "ada" else 1
                        sp.wait_ge(used, before + (i * body_units + u - SLOTS + 1) * step)
                    if name == "merge" and fresh and u == 3:
                        sp.wait_ge(S["y_made"], 16)
                    for dst, src in moves:
                        sp.dma_start(dst, src).then_inc(landed[u % SLOTS], 16)

            kind_before = {"cmp": (split_made, plan["cmp"][1]), "merge": (direct_used, 4)}
            if name in kind_before:
                sp.wait_ge(*kind_before[name])
            if name == "ada" or name in kind_before:
                body(0, True)
                start = 1
            else:
                start = 0
            if n_iter - start == 1:
                body(start, False)
            elif n_iter > start:
                with sp.Fori(start, n_iter) as i:
                    body(i, False)

        def tiles(w, off=0):
            view = w.rearrange("(k p) n -> p k n", p=P)
            return lambda i, u: [(slot(u % SLOTS).rearrange("p (k n) -> p k n", n=P),
                                  view[:, :, ds(i * 4 * P + (off + u * P), P)])]

        def rows(w, r0, per_half, off=0):
            view = w[r0:r0 + 2 * P * per_half, :].rearrange("(c k p) n -> c p k n", p=P, k=2)
            return lambda i, u: [(slot(u % SLOTS).rearrange("p (k n) -> p k n", k=2),
                                  view[u % per_half][:, :, ds(i * HALF + (off + u // per_half * HALF), HALF)])]

        def pairs(ws, offs, f0):
            views = [w.rearrange("(k p) n -> p k n", p=P) for w in ws]
            return lambda i, u: [(slot(u % SLOTS).rearrange("p (k n) -> p k n", n=P),
                                  views[u % 2][:, :, ds(i * 2 * P + (offs[u % 2] + (f0 + u // 2) * P), P)])]

        def load_ffn(n):
            f = ffn_w[n]
            for part, (f0, chunks) in enumerate(PARTS):
                load(f"up{n}{part}", 4, chunks // 2, pairs(f["up"], f["off"], f0))
                per_half = chunks // 2
                if per_half % SLOTS == 0:
                    load(f"down{n}{part}", per_half, 2, rows(f["down"], f0 * P, per_half))
                else:
                    load(f"down{n}{part}", 2 * per_half, 1, rows(f["down"], f0 * P, per_half))

        if "ada" in run:
            view = W["ada"].rearrange("(c k p) n -> c p k n", p=P, k=2)
            load("ada", 16, 6, lambda i, u: [(slot(u % SLOTS).rearrange("p (k n) -> p k n", k=2),
                                              view[u % 8][:, :, ds(i * 2 * HALF + u // 8 * HALF, HALF)])])
        if "in" in run:
            load("in_tiles", 4, 4, tiles(W["in_tiles"]))
            load("in_rows", 8, 2, rows(W["in_rows"], 0, 8, off=2048))
        if "out1" in run:
            load("out1", 8, 2, rows(W["out1"], 0, 8))
        if "ffn0" in run:
            load_ffn(0)
        if "ffn1" in run:
            load_ffn(1)
        if "mix2" in run:
            load("in2", 4, 7, tiles(W["in2"]))
        if "cmp" in run:
            def fetch_cmp(i, u):
                w = I["cmp_k_w1_2"] if u < 2 else I["cmp_v_w1_2"]
                view = w.rearrange("(h k p) n -> h p k n", p=P, k=8)
                return [(slot(u).rearrange("p (k n) -> p k n", n=256), view[u % 2])]
            load("cmp", 4, 1, fetch_cmp)
        if "merge" in run:
            in2 = I["w_in_2"].rearrange("(k p) n -> p k n", p=P)
            halves = [I[n].rearrange("(k p) n -> p k n", p=P) for n in ("ssm_glu_w1_2", "ssm_glu_w2_2", "nsa_w_o_2")]

            def fetch_merge(i, u):
                to = slot(u).rearrange("p (k n) -> p k n", n=P)
                if u < 2:
                    return [(to, in2[:, :, ds(i * P + (GA_IN2, GB_IN2)[u], P)])]
                at = i * P if isinstance(i, int) else (i + 1) * P - P
                if u == 2:
                    return [(to[:, 8 * v:8 * v + 8], halves[v][:, :, ds(at, P)]) for v in range(2)]
                return [(to[:, 0:8], halves[2][:, :, ds(at, P)])]
            load("merge", 4, 16, fetch_merge)
        if "out2" in run:
            load("out2", 8, 2, rows(W["out2"], 0, 8))
        if "ffn2" in run:
            load_ffn(2)
        if stop is None:
            sp.wait_ge(S["x_made"], 6)
            sp.dma_start(out.rearrange("b (m p) d -> p (b m) d", p=P),
                         x_nat[:, :].rearrange("p (m d) -> p m d", m=MT)).then_inc(S["out_done"], 16)
            sp.wait_ge(S["out_done"], 16)

    @block.gpsimd
    def _(pool):
        link = Steps(pool, pool_step)
        link.then(pool.memset(ones1[:, :], 1.0))
        link.then(pool.memset(relb[32:33, :], NEG))
        tab = rowtab[:, :].rearrange("q (t p) -> q t p", p=P)

        def vec(name):
            return I[name].rearrange("(q p) -> q p", p=P)

        conv = I["w_conv"].rearrange("t (q p) -> t q p", p=P)
        loads = [
            (tab[0:96, 0, :], vec("b_ada")), (tab[96:112, 0, :], vec("norm1_w")),
            (tab[112:128, 0, :], vec("norm2_w")),
            (tab[0:88, 1, :], conv[0]), (tab[88:96, 1, :], I["ssm_d_2"].rearrange("b (q p) -> (b q) p", p=P)),
            (tab[0:88, 2, :], conv[1]), (tab[88:104, 2, :], I["ffn1_pre_g_2"].rearrange("b (q p) -> (b q) p", p=P)),
            (tab[104:120, 2, :], I["mix_pre_g_2"].rearrange("b (q p) -> (b q) p", p=P)),
            (tab[0:88, 3, :], conv[2]), (tab[88:104, 3, :], I["ffn2_pre_g_2"].rearrange("b (q p) -> (b q) p", p=P)),
            (tab[0:88, 4, :], vec("b_conv")),
            (tab[88:120, 4, :], I["ssm_a_re_2"].rearrange("b (q g) p -> (b q) (g p)", g=2)),
            (tab[0:32, 5, :], I["ssm_a_im_2"].rearrange("b (q g) p -> (b q) (g p)", g=2)),
        ]
        for dst, src in loads:
            pool.dma_start(dst, src).then_inc(S["tab_in"], 16)
        pool.dma_start(hval[32:64, 0:2], I["ssm_log_dt_2"].rearrange("b (q g) -> (b q) g", g=2)).then_inc(S["tab_in"], 16)
        pool.wait_ge(S["tab_in"], 16 * (len(loads) + 1))
        for g in range(2):
            last = pool.tensor_copy(tab[32:64, 5, 64 * g:64 * g + 64],
                                    hval[32:64, g:g + 1].to_broadcast([32, 64]))
        last.then_inc(S["tab_ready"], 1)
        pool.dma_start(x_nat[:, :].rearrange("p (m d) -> p m d", m=MT),
                       I["x"].rearrange("b (m p) d -> p (b m) d", p=P)).then_inc(S["x_in"], 16)
        pool.dma_start(bgate[0:4, :], I["b_gates"].rearrange("(k h) -> h k", h=4)).then_inc(S["const_in"], 16)
        pool.dma_start(sel1[:, :], I["k_sel"]).then_inc(S["const_in"], 16)
        wgv = wg_raw[:, :].rearrange("p (k n) -> p k n", n=48)
        pool.dma_start(wgv[:, :, 0:16], I["w_in"].rearrange("(k p) n -> p k n", p=P)[:, :, 4096:4112]).then_inc(S["wg_in"], 16)
        if "ada" in run:
            pool.wait_ge(S["ada_taken"], 14)
            for v in range(2):
                pool.dma_start(modrow_dram[v:v + 1], mod_row[32 * v:32 * v + 1, :]).then_inc(S["modrow_out"], 16)
            pool.wait_ge(S["modrow_out"], 32)
            for v, t in enumerate((conv_a, conv_v)):
                pool.dma_start(t[0:96, 0:P], modrow_dram[v].rearrange("(q p) -> q p", p=P)).then_inc(S["modrow_in"], 16)
        if "in" in run:
            for dst, src in ((dft1, "k_dft1"), (dft2, "k_dft2")):
                pool.dma_start(dst[:, :].rearrange("p (k n) -> p k n", n=512),
                               I[src].rearrange("(k p) n -> p k n", p=P)).then_inc(S["dft_in"], 16)
            pool.wait_ge(S["mod_made"], 1)
            pool.dma_start(gates_dram[0].rearrange("(k p) -> p k", p=P), mod[:, 32:48]).then_inc(S["gate_out"], 16)
            pool.dma_start(gates_dram[1].rearrange("(k p) -> p k", p=P), mod[:, 80:96]).then_inc(S["gate_out"], 16)
            pool.wait_ge(S["gate_out"], 32)

        rows_in = [0]

        def spread_row(src, n=D):
            if rows_in[0]:
                pool.wait_ge(S["row_used"], rows_in[0])
            rows_in[0] += 1
            pool.dma_start(row[:, 0:n], src.partition_broadcast(P)).then_inc(S["row_in"], 16)

        if "mlstm" in run:
            pool.wait_ge(S["g_made"], 1)
            pool.dma_start(mask1[:, :].rearrange("p (k n) -> p k n", n=T), I["k_mask"]).then_inc(S["mask_in"], 16)
            spread_row(I["mlstm_norm_w"], 1024)
        if "out1" in run:
            spread_row(gates_dram[0])
        if "ffn0" in run:
            spread_row(gates_dram[1])
        if "final1" in run:
            spread_row(I["norm_f_w"])
        if "ffn1" in run:
            spread_row(I["ffn1_post_g_2"][0])
        if "mix2" in run:
            pool.wait_ge(S["g_copied"], 1)
            pool.dma_start(wgv, I["w_in_2"].rearrange("(k p) n -> p k n", p=P)[:, :, G_IN2:G_IN2 + 48]).then_inc(S["wg_in"], 16)
            pool.wait_ge(S["num_taken"], 4)
            pool.wait_ge(S["rows_made"], 1)
            for c in range(2):
                for k in range(2):
                    pool.dma_start(w2[:, c * P + k * DH:c * P + (k + 1) * DH], I["cmp_k_w2_2"][c * P:(c + 1) * P, :]).then_inc(S["small_in"], 16)
            pool.dma_start(w2[:, 2 * P:3 * P].rearrange("p (c n) -> p c n", n=DH),
                           I["cmp_v_w2_2"].rearrange("(c p) n -> p c n", p=P)).then_inc(S["small_in"], 16)
            for k in range(2):
                pool.dma_start(pos2[:, k * DH:(k + 1) * DH], I["cmp_pos_2"]).then_inc(S["small_in"], 16)
            pool.wait_ge(S["norm_done"], 32)
            pool.dma_start(oh_rev[:, :], I["k_oh_rev"]).then_inc(S["oh_in"], 16)
            pool.dma_start(oh_fwd[:, :], I["k_oh_fwd"]).then_inc(S["oh_in"], 16)
            pool.dma_start(relb[0:32, :], I["rel_bias_2"]).then_inc(S["oh_in"], 16)
            pool.dma_start(live[:, :], I["k_live"]).then_inc(S["oh_in"], 16)
            pool.wait_ge(S["rev_copied"], 1)
            pool.dma_start(rev_dram, rev_sb[:, :].unsqueeze(1).to_broadcast([16, P, 384])).then_inc(S["rev_out"], 16)
            pool.wait_ge(S["rev_out"], 16)
            pool.wait_ge(S["g_made"], 2)
            pool.dma_start(strips[:, :].rearrange("p (h x) -> p h x", h=NH),
                           bass.AP(rev_dram.tensor, 127, [[383, P], [P * 384, NH], [1, T]])).then_inc(S["strips_in"], 16)
        if "s5" in run:
            pool.wait_ge(S["on_turned"], 4)
            pool.wait_ge(S["av_made"], 8)
            for v, n in enumerate(("ssm_b_re_2", "ssm_b_im_2")):
                pool.dma_start(bc[:, v * 512:(v + 1) * 512].rearrange("p (j c) -> p j c", c=16),
                               I[n].rearrange("(j g) p c -> (g p) j c", g=2)).then_inc(S["s5_in"], 16)
            for v, n in enumerate(("ssm_c_re_2", "ssm_c_im_2")):
                for k in range(2):
                    pool.dma_start(cc[:, v * 1024:(v + 1) * 1024].rearrange("p (c k n) -> p c k n", k=2, n=64)[:, :, k],
                                   I[n].rearrange("(c g) h p -> (g h) c p", c=8)).then_inc(S["s5_in"], 16)
            pool.dma_start(trow[:, :], I["k_trow"]).then_inc(S["s5_in"], 16)
            pool.dma_start(cmask[:, :], I["k_cmask"]).then_inc(S["s5_in"], 16)
            link.then(pool.memset(bn[:, :], 0.0))
            pool.wait_ge(S["s5_in"], 16 * N_S5)

            def spread_b(c):
                if c:
                    pool.wait_ge(S["bt_made"], c)
                for v in range(2):
                    for jj in range(4):
                        for g in range(2):
                            at = v * 512 + jj * P + 32 * jj + 16 * g
                            last = pool.tensor_copy(bn[64 * g:64 * g + 64, at:at + 16],
                                                    bc[64 * g:64 * g + 64, v * 512 + (4 * c + jj) * 16:v * 512 + (4 * c + jj + 1) * 16])
                last.then_inc(S["bn_made"], 1)
                pool.wait_ge(S["bn_made"], c + 1)

            spread_b(0)
            for pr in range(16):
                at = slice(pr % 2 * 512, (pr % 2 + 1) * 512)
                pool.wait_ge(S["scan_made"], pr + 1)
                if pr >= 2:
                    pool.wait_ge(S["y_made"], pr - 1)
                for k, (w, z) in enumerate(((cosine, z_r), (sine, z_i), (cosine, z_i), (sine, z_r))):
                    last = pool.tensor_tensor(backs[pr % 2][:, k * 512:(k + 1) * 512], w[:, at], z[:, at], ALU.mult)
                last.then_inc(S["back_made"], 1)
                if pr % 2 == 0 and pr < 14:
                    pool.wait_ge(S["back_made"], pr + 1)
                    spread_b(pr // 2 + 1)
        if "out2" in run:
            pool.wait_ge(split_used, plan["merge"][1] + 66)
            spread_row(I["mix_post_g_2"][0])
        if "ffn2" in run:
            spread_row(I["ffn2_post_g_2"][0])


    rows_index = {n: r for r, n in enumerate(["in_rows", "out1", "down00", "down01", "down10", "down11",
                                              "out2", "down20", "down21"])}

    def rows_cols(half, m, n=0, width=HALF):
        return ps[:, ds(half * 2048 + (m * HALF + n * 512), width)]

    def up_body_order(i, split, s2, s3, s1):
        static = isinstance(i, int) and i == 0
        split(0)
        if not static:
            s2(2 * i - 2, 0)
        split(1)
        if not static:
            s3(2 * i - 2, 0)
            s1(2 * i - 1, 1)
        split(2)
        if not static:
            s2(2 * i - 1, 1)
        split(3)
        if not static:
            s3(2 * i - 1, 1)
        s1(2 * i, 0)

    def nothing(*_):
        pass

    def up_phase(eng, split, s2, s3, s1, chunks, pending=nothing):
        def first_split(u):
            split(0, u)
            if u == 1:
                pending()
        up_body_order(0, first_split, s2, s3, s1)
        with eng.Fori(1, chunks // 2) as i:
            up_body_order(i, lambda u: split(i, u), s2, s3, s1)
        last = chunks - 2
        s2(last, 0)
        s3(last, 0)
        s1(last + 1, 1)
        s2(last + 1, 1)
        s3(last + 1, 1)

    PIECES = (2, 4, 4, 2, 4, 2, 4, 2, 4)

    def pieces_before(e):
        return sum(PIECES[:e])
    NORM_OF = (1, 2, 4)
    NUM = (0, 1, 6, 7)

    def take4(dve, link, q):
        br, h0 = q // 4, q % 4 * 4
        dve.wait_ge(S["av_made"], q + 1)
        rs = sm[:, 128 + 8 * q:136 + 8 * q]
        link.then(dve.reciprocal(rs, rs))
        gate = g_nat[:, :].rearrange("p (m h b) -> p h m b", h=NH, b=3)[:, h0:h0 + 4, :, 1 + br]
        link.then(dve.tensor_tensor(rs.rearrange("p (h m) -> p h m", m=2), rs.rearrange("p (h m) -> p h m", m=2),
                                    gate, ALU.mult))
        part = hval[:, :].rearrange("p (x d) -> p x d", d=DH)
        dve.tensor_tensor(part, bank(4 + q % 2).rearrange("p (x d) -> p x d", d=DH),
                          rs.unsqueeze(2).to_broadcast([P, 8, DH]), ALU.mult).then_inc(S["av_taken"], 1)
        dve.wait_ge(S["av_taken"], q + 1)
        dst = o_nat[:, :].rearrange("p (m h d) -> p h m d", m=2, d=DH)[:, h0:h0 + 4]
        dve.tensor_tensor(dst, dst, hval[:, :].rearrange("p (h m d) -> p h m d", m=2, d=DH), ALU.add).then_inc(S["o_added"], 1)
        dve.wait_ge(S["o_added"], q + 1)

    def half_done(eng, name, half):
        eng.wait_ge(split_used, plan[name][1] + plan[name][3] // 2 * (half + 1) + 2)

    def head_squares(act, h):
        act.wait_ge(S["num_taken"], h + 1)
        for m in range(MT):
            if h + m:
                act.wait_ge(S["h_ssq"], 2 * h + m)
            act.activation(bank(2, 0, 256), h_nat[:, m * 1024 + h * 256:m * 1024 + (h + 1) * 256], ACT.Square,
                           accum_out=stats[:, 8 + m * 4 + h:9 + m * 4 + h]).then_inc(S["h_ssq"], 1)

    def gates(pe, n, made):
        for m in range(MT):
            for k in range(KC):
                wh, wl = (w[:, k * n:(k + 1) * n] for w in (wg_hi, wg_lo))
                pe.matmul(bank(0, m * n, n), chunk(xt_hi, k, m), wh, start=k == 0, stop=False)
                pe.matmul(bank(0, m * n, n), chunk(xt_hi, k, m), wl, start=False, stop=False)
                last = pe.matmul(bank(0, m * n, n), chunk(xt_lo, k, m), wh, start=False, stop=k == KC - 1)
        last.then_inc(S["g_made"], 1)

    @block.scalar
    def _(act):
        link = Steps(act, act_step)
        act.sem_inc(S["ada_taken"], 2)
        act.sem_inc(S["tile_copied"], 4)

        def split(name, per_body, i, u):
            first, before, _, _ = plan[name]
            loads = 2 if name == "merge" and u == 2 else 1
            earlier = first // SLOTS
            if first > plan["merge"][0] and u % SLOTS == 2:
                earlier += 16
            act.wait_ge(landed[u % SLOTS], (earlier + loads * (u // SLOTS + 1 + i * (per_body // SLOTS))) * 16)
            act.wait_ge(split_used, before + u + 1 + i * per_body)
            n = HALF if name == "merge" and u == 3 else UNIT
            act.activation(w_hi[:, u % 2 * UNIT:u % 2 * UNIT + n], stage[:, u % SLOTS * UNIT:u % SLOTS * UNIT + n],
                           ACT.Copy).then_inc(hi_made, 1)

        def squares(e, src, k):
            n = pieces_before(e) + k
            if e:
                act.wait_ge(S["piece_made"], n - 1)
            if n:
                act.wait_ge(S["norm_ssq"], n)
            if PIECES[e] == 4:
                half, m = divmod(k, 2)
                part, to = src[:, m * D + half * HALF:m * D + (half + 1) * HALF], ps[:, 0:HALF]
            else:
                part, to = src[:, k * D:(k + 1) * D], ps[:, 2048:4096]
            act.activation(to, part, ACT.Square, accum_out=stats[:, k:k + 1]).then_inc(S["norm_ssq"], 1)

        def root(e):
            act.wait_ge(S["norm_var"], e + 1)
            act.activation(stats[:, 6:8], stats[:, 4:6], ACT.Sqrt).then_inc(S["norm_std"], 1)

        def square_sum(e, src, first=0):
            for k in range(first, PIECES[e]):
                squares(e, src, k)
            root(e)

        def second_tile(n, e):
            act.wait_ge(S["norm_rs"], e + 1)
            act.activation(f_nat[:, D:2 * D], x_nat[:, D:2 * D], ACT.Copy, scale=stats[:, 9:10]).then_inc(S["norm_xhat"], 1)

        def norm(e, n, first=0):
            square_sum(e, x_nat, first)
            second_tile(n, e)
            norm_split(n)

        def norm_split(n):
            for g in range(8):
                act.wait_ge(S["norm_scaled"], 8 * n + g + 1)
                act.activation(xt_hi[:, g * 512:(g + 1) * 512], turn[:, g % 2 * 512:(g % 2 + 1) * 512],
                               ACT.Copy).then_inc(S["norm_hi"], 1)

        def ffn(n, e_post):
            conv = ffn_w[n]["conv"]
            for part, (f0, chunks) in enumerate(PARTS):
                name, q0 = f"up{n}{part}", n * FC + f0
                before = plan[name][1]

                def e1(j, s):
                    act.wait_ge(split_used, 2 * j + (before + 4))
                    if conv:
                        act.activation(conv_a[:, s * T:(s + 1) * T], bank(s, 0, T), ACT.Identity,
                                       scale=cols[:, ds(j + (C_CONV[1] + f0), 1)],
                                       bias=cols[:, ds(j + (C_CB + f0), 1)])
                        act.activation(conv_v[:, s * T:(s + 1) * T], bank(s, T, T), ACT.Identity,
                                       scale=cols[:, ds(j + (C_CONV[1] + FC + f0), 1)],
                                       bias=cols[:, ds(j + (C_CB + FC + f0), 1)]).then_inc(S["pair_e1"], 1)
                    else:
                        act.activation(conv_a[:, s * T:(s + 1) * T], bank(s, 0, T),
                                       ACT.Silu).then_inc(S["pair_e1"], 1)

                def e2(j, s):
                    act.wait_ge(S["pair_d1"], j + (q0 + 3))
                    act.activation(conv_a[:, s * T:(s + 1) * T], conv_a[:, s * T:(s + 1) * T],
                                   ACT.Silu).then_inc(S["pair_e2"], 1)

                def e3(j, s):
                    if conv:
                        act.wait_ge(S["pair_d2"], j + (q0 + 1))
                    else:
                        act.wait_ge(S["pair_d1"], j + (q0 + 3))
                    act.activation(hid_hi[:, ds(j * T, T)], hval[:, s * T:(s + 1) * T],
                                   ACT.Copy).then_inc(S["pair_e3"], 1)

                up_phase(act, lambda i, u: split(name, 4, i, u), e2 if conv else e3,
                         e3 if conv else nothing, e1, chunks)
                for u in range(chunks):
                    split(f"down{n}{part}", chunks, 0, u)
                    if part and u == chunks // 2 + (3 if n else 7):
                        squares(e_post, x_nat if n == 0 else f_nat, 0)
                        squares(e_post, x_nat if n == 0 else f_nat, 1)

        act.dma_start(conv_a[0:16, 0:P], I["c"].rearrange("b (q p) -> (b q) p", p=P)).then_inc(S["c_in"], 16)
        act.dma_start(ident[:, :], I["k_ident"]).then_inc(S["c_in"], 16)
        act.wait_ge(S["c_turned"], 1)
        act.activation(csilu[:, :], bank(4, 0, KC), ACT.Silu).then_inc(S["silu_made"], 1)
        act.wait_ge(S["silu_made"], 1)
        crep = xt_hi[:, :].rearrange("p (k n) -> p k n", n=T)
        act.activation(crep[:, :, 0:32], csilu[:, :].unsqueeze(2).to_broadcast([P, KC, 32]),
                       ACT.Copy).then_inc(S["crep_hi"], 1)

        def take_ada(b, h):
            act.wait_ge(split_used, 16 * b + 18)
            act.activation(mod_row[0:64, ds(b * HALF, HALF)], ps[0:64, h * HALF:(h + 1) * HALF],
                           ACT.Copy).then_inc(S["ada_taken"], 1)

        def ada(i):
            for u in range(16):
                act.wait_ge(landed[u % SLOTS], (u // SLOTS + 1 + i * (16 // SLOTS)) * 16)
                for s in range(2):
                    used = 32 * i + (2 * u + s - 1)
                    if not isinstance(i, int) or used > 0:
                        act.wait_ge(split_used, used)
                    at = slice(u % 2 * UNIT + s * HALF, u % 2 * UNIT + (s + 1) * HALF)
                    act.activation(w_hi[:, at], stage[:, u % SLOTS * UNIT + s * HALF:u % SLOTS * UNIT + (s + 1) * HALF],
                                   ACT.Copy).then_inc(hi_made, 1)
                if u == 1 and not isinstance(i, int):
                    take_ada(2 * i - 1, 1)
                if u == 9:
                    take_ada(2 * i, 0)
        ada(0)
        act.wait_ge(S["x_in"], 16)
        square_sum(0, x_nat)
        second_tile(0, 0)
        with act.Fori(1, 6) as i:
            ada(i)
        take_ada(11, 1)
        norm_split(0)
        if "in" in run:
            def copy_tile(i, s):
                act.activation(projt[:, ds(i * 4 * T + s * T, T)], bank(s, 0, T),
                               ACT.Copy).then_inc(S["tile_copied"], 1)

            split("in_tiles", 4, 0, 0)
            split("in_tiles", 4, 0, 1)
            split("in_tiles", 4, 0, 2)
            copy_tile(0, 0)
            split("in_tiles", 4, 0, 3)
            copy_tile(0, 1)
            with act.Fori(1, 4) as i:
                for u in range(4):
                    split("in_tiles", 4, i, u)
                    if u < 2:
                        copy_tile(i - 1, u + 2)
                    else:
                        copy_tile(i, u - 2)
            for u in range(2):
                split("in_rows", 16, 0, u)
                copy_tile(3, u + 2)
            for u in range(2, 16):
                split("in_rows", 16, 0, u)
                if u == 9:
                    half_done(act, "in_rows", 0)
                    for m in range(MT):
                        dst = v_one[:, m * 1028:(m + 1) * 1028].rearrange("p (h n) -> p h n", n=257)
                        last = act.activation(dst[:, :, 0:256], rows_cols(0, m).rearrange("p (h n) -> p h n", n=256),
                                       ACT.Copy)
                    last.then_inc(S["rows_taken"], 1)
            act.wait_ge(S["wg_in"], 16)
            act.wait_ge(S["norm_turned"], 8)
            act.activation(wg_hi[:, 0:KC * 16].rearrange("p (k n) -> p k n", n=16),
                           wg_raw[:, :].rearrange("p (k n) -> p k n", n=48)[:, :, 0:16],
                           ACT.Copy).then_inc(S["wg_split_hi"], 1)
            half_done(act, "in_rows", 1)
            for m in range(MT):
                last = act.activation(o_sig[:, m * 1024:(m + 1) * 1024], rows_cols(1, m),
                               ACT.Sigmoid)
            last.then_inc(S["rows_taken"], 1)
        if "four" in run:
            for g in range(4):
                act.wait_ge(S["four1"], g + 1)
                if g:
                    act.wait_ge(S["four2"], g)
                for m in range(MT):
                    act.activation(four[:, m * 512:(m + 1) * 512], bank(2 * (g % 2) + m),
                                   ACT.Copy).then_inc(S["four1_copied"], 1)
                act.wait_ge(S["four2_copied"], g + 1)
                act.activation(xt_hi[:, g * 512:(g + 1) * 512], turn[:, g % 2 * 512:(g % 2 + 1) * 512],
                               ACT.Copy).then_inc(S["four2_hi"], 1)
        if "mlstm" in run:
            act.wait_ge(S["grow_made"], 1)
            link.then(act.activation(crow[:, :].rearrange("h (d t) -> h d t", d=2),
                                     grow[:, :].rearrange("h (d k t) -> h k d t", d=2, k=2)[:, 1], ACT.Abs))
            act.activation(crow[:, :], crow[:, :], ACT.Exp, scale=-1.0).then_inc(S["f_exp"], 1)
            act.wait_ge(S["f_add"], 1)
            act.activation(crow[:, :], crow[:, :], ACT.Ln).then_inc(S["f_ln"], 1)
            act.wait_ge(S["ec_copied"], 1)
            act.activation(ecols[:, 16:32], ecols[:, 16:32], ACT.Exp, scale=-1.0).then_inc(S["em_made"], 1)
            for h in range(HEADS1):
                act.wait_ge(S["arg_made"], h + 1)
                act.activation(ex1[:, :], ex1[:, :], ACT.Exp).then_inc(S["exp_made"], 1)
                if h:
                    head_squares(act, h - 1)
            head_squares(act, HEADS1 - 1)
            act.wait_ge(S["h_var"], 1)
            act.activation(stats[:, 16:24], stats[:, 8:16], ACT.Sqrt).then_inc(S["h_std"], 1)
            for g in range(4):
                act.wait_ge(S["ym_copied"], g + 1)
                act.activation(xt_hi[:, (4 + g) * 512:(5 + g) * 512], turn[:, g % 2 * 512:(g % 2 + 1) * 512],
                               ACT.Copy).then_inc(S["ym_hi"], 1)
        if "out1" in run:
            for u in range(16):
                split("out1", 16, 0, u)
                if u == 12:
                    squares(1, x_nat, 0)
                    squares(1, x_nat, 1)
        if "ffn0" in run:
            norm(1, 1, 2)
            ffn(0, 2)
        if "final1" in run:
            square_sum(2, x_nat, 2)
        if "ffn1" in run:
            norm(3, 2)
            ffn(1, 4)
            square_sum(4, f_nat, 2)
        if "mix2" in run:
            norm(5, 3)

            def copy_tile2(i, s):
                act.activation(pt2[:, ds(i * 4 * T + s * T, T)], bank(s, 0, T),
                               ACT.Copy).then_inc(S["tile_copied"], 1)

            for u in range(4):
                split("in2", 4, 0, u)
                if u >= 2:
                    copy_tile2(0, u - 2)
            with act.Fori(1, 7) as i:
                for u in range(4):
                    split("in2", 4, i, u)
                    copy_tile2(i - 1 if u < 2 else i, (u + 2) % 4)
            for u in range(2):
                act.wait_ge(split_used, plan["in2"][1] + 29 + u)
                copy_tile2(6, u + 2)
            act.wait_ge(S["wg_in"], 32)
            act.activation(wg_hi[:, :], wg_raw[:, :], ACT.Copy).then_inc(S["wg_split_hi"], 1)
            act.wait_ge(S["g_made"], 2)
            act.activation(g_nat[:, :], bank(0, 0, 96), ACT.Sigmoid).then_inc(S["g_copied"], 1)
            act.wait_ge(S["vt_made"], 1)
            for br in range(2):
                act.activation(v_nat[:, br * 512:(br + 1) * 512], bank(1 + br), ACT.Copy).then_inc(S["vn_copied"], 1)
        if "cmp" in run:
            act.wait_ge(S["rev_out"], 16)
            for x in range(2):
                act.wait_ge(direct_used, 2 * x + 2)
                act.activation(hid_n[:, x * T:(x + 1) * T], bank(6 + x, 0, T, 60),
                               ACT.Gelu_apprx_tanh).then_inc(S["hn_gelu"], 1)
            for m in range(MT):
                act.wait_ge(S["cs_max"], m + 1)
                act.activation(cmp_s[:, m * 240:(m + 1) * 240], cmp_s[:, m * 240:(m + 1) * 240],
                               ACT.Exp).then_inc(S["cs_exp"], 1)
            for x in range(8):
                act.wait_ge(S["ct_made"], x + 1)
                act.activation(cmp_t[:, x % 2 * 512:(x % 2 + 1) * 512], bank(x % 2, 0, 512, 15),
                               ACT.Copy).then_inc(S["ct_copied"], 1)
        if "attn" in run:
            for i in range(2 * NH + 1):
                if i < 2 * NH:
                    act.wait_ge(S["sc_max"], i + 1)
                    for m in range(MT):
                        at = slice(i % 2 * 384 + m * P, i % 2 * 384 + (m + 1) * P + m * P)
                        last = act.activation(soft[:, at], soft[:, at], ACT.Exp,
                                              bias=sm[:, 64 + 2 * i + m:65 + 2 * i + m],
                                              accum_out=sm[:, 128 + 2 * i + m:129 + 2 * i + m])
                    last.then_inc(S["sc_exp"], 1)
                if i:
                    j = i - 1
                    act.wait_ge(S["pt_turned"], j + 1)
                    act.activation(turned[:, j % 2 * 384:(j % 2 + 1) * 384], bank(2 + j % 2, 0, 384),
                                   ACT.Copy).then_inc(S["pt_copied"], 1)
            for g in range(4):
                act.wait_ge(S["on_copied"], g + 1)
                act.activation(po_hi[:, g * 512:(g + 1) * 512], hval[:, :], ACT.Copy).then_inc(S["on_hi"], 1)
        if "s5" in run:
            act.wait_ge(S["s5_in"], 16 * N_S5)
            pc = lambda i: par[:, i * ST:(i + 1) * ST]
            act.activation(pc(0), cols[:, C_LDT:C_LDT + ST], ACT.Exp).then_inc(S["p_dt"], 1)
            act.wait_ge(S["p_x"], 1)
            act.activation(pc(4), pc(2), ACT.Exp).then_inc(S["p_mag"], 1)
            act.wait_ge(S["p_phi"], 1)
            act.activation(pc(6), pc(5), ACT.Sin, scale=6.283185)
            link.then(act.activation(pc(7), pc(5), ACT.Sin, scale=3.1415925))
            act.activation(pc(7), pc(7), ACT.Square, scale=math.sqrt(2)).then_inc(S["p_sin"], 1)

            def waves(pr):
                at = slice(pr % 2 * 512, (pr % 2 + 1) * 512)
                act.wait_ge(S["ang_made"], pr + 1)
                if pr >= 2:
                    act.wait_ge(S["back_made"], pr - 1)
                act.activation(sine[:, at], trig[:, at], ACT.Sin, scale=6.283185).then_inc(act_step, 1)
                link.n += 1
                act.wait_ge(act_step, link.n)
                link.then(act.activation(trig[:, at], trig[:, at], ACT.Sin, scale=3.1415925))
                act.activation(trig[:, at], trig[:, at], ACT.Square, scale=math.sqrt(2)).then_inc(S["ang_sin"], 1)

            def take_b(c):
                act.wait_ge(S["bt_made"], c + 1)
                if c:
                    act.wait_ge(S["bu_made"], 2 * c)
                for v in range(2):
                    act.activation(bt[:, v * 512:(v + 1) * 512], bank(4 + v), ACT.Copy).then_inc(S["bt_copied"], 1)

            def finish_y(c):
                act.wait_ge(S["y_sum"], c + 1)
                v = hval[:, c % 2 * T:(c % 2 + 1) * T]
                link.then(act.activation(v, v, ACT.Gelu_apprx_tanh))
                act.activation(chunk(ps_hi, c), v, ACT.Copy).then_inc(S["y_hi"], 1)

            waves(0)
            take_b(0)
            for c in range(8):
                for pr in (2 * c, 2 * c + 1):
                    if pr < 15:
                        waves(pr + 1)
                    if pr % 2 == 0 and c:
                        finish_y(c - 1)
                if c < 7:
                    take_b(c + 1)
            finish_y(7)
        if "merge" in run:
            def gate(dst, b, unit_count, sem_name):
                act.wait_ge(split_used, unit_count)
                act.activation(dst, bank(b, 0, T), ACT.Sigmoid).then_inc(S[sem_name], 1)

            mb = plan["merge"][1]
            sg_a, sg_b, sg_2 = (sgates[:, k * T:(k + 1) * T] for k in range(3))

            def merge(i, fresh):
                split("merge", 4, i, 0)
                if not fresh:
                    gate(sg_2, 3, mb + 1 + i * 4, "mg_2")
                split("merge", 4, i, 1)
                split("merge", 4, i, 2)
                if not fresh:
                    act.wait_ge(S["mg_sum"], i)
                    act.activation(hid_hi[:, ds(i * T - T, T)], hval[:, 0:T], ACT.Copy).then_inc(S["mg_hi"], 1)
                gate(sg_a, 0, mb + 3 + i * 4, "mg_a")
                split("merge", 4, i, 3)
                gate(sg_b, 1, mb + 4 + i * 4, "mg_b")
            merge(0, True)
            with act.Fori(1, 16) as i:
                merge(i, False)
            gate(sg_2, 3, mb + 65, "mg_2")
            act.wait_ge(S["mg_sum"], 16)
            act.activation(hid_hi[:, 15 * T:16 * T], hval[:, 0:T], ACT.Copy).then_inc(S["mg_hi"], 1)
        if "out2" in run:
            for u in range(16):
                split("out2", 16, 0, u)
                if u == 12:
                    squares(6, f_nat, 0)
                    squares(6, f_nat, 1)
            square_sum(6, f_nat, 2)
        if "ffn2" in run:
            norm(7, 4)
            ffn(2, 8)
            square_sum(8, f_nat, 2)

    @block.vector
    def _(dve):
        link = Steps(dve, dve_step)
        dve.sem_inc(S["hid_made"], 2)
        dve.sem_inc(S["pair_d1"], 2)

        def split(name, per_body, i, u):
            before = plan[name][1]
            dve.wait_ge(hi_made, before + u + 1 + i * per_body)
            n = HALF if name == "merge" and u == 3 else UNIT
            part = slice(u % 2 * UNIT, u % 2 * UNIT + n)
            dve.tensor_tensor(w_lo[:, part], stage[:, u % SLOTS * UNIT:u % SLOTS * UNIT + n], w_hi[:, part].bitcast(F32),
                              ALU.subtract).then_inc(split_made, 1)

        def rest(dst, src, hi, signal):
            dve.tensor_tensor(dst, src, hi.bitcast(F32), ALU.subtract).then_inc(signal, 1)

        def inverse_rms(e):
            dve.wait_ge(S["norm_ssq"], pieces_before(e + 1))
            total = stats[:, 0:2]
            if PIECES[e] == 4:
                total = stats[:, 4:6]
                link.then(dve.tensor_tensor(total, stats[:, 0:2], stats[:, 2:4], ALU.add))
            dve.tensor_scalar(stats[:, 4:6], total, 1.0 / D, EPS, ALU.mult, ALU.add).then_inc(S["norm_var"], 1)
            dve.wait_ge(S["norm_std"], e + 1)
            dve.reciprocal(stats[:, 8:10], stats[:, 6:8]).then_inc(S["norm_rs"], 1)
            dve.wait_ge(S["norm_rs"], e + 1)

        def norm(e, n, scale, shift):
            norm_scale(e)
            norm_finish(n, scale, shift)

        def norm_scale(e):
            inverse_rms(e)
            dve.tensor_scalar(f_nat[:, 0:D], x_nat[:, 0:D], stats[:, 8:9], None, ALU.mult).then_inc(S["norm_xhat"], 1)

        def norm_finish(n, scale, shift):
            for g in range(9):
                if g < 8:
                    dve.wait_ge(S["norm_turned"], 8 * n + g + 1)
                    if g >= 2:
                        dve.wait_ge(S["norm_done"], 8 * n + g - 1)
                    for k in range(2):
                        dst = turn[:, g % 2 * 512 + k * T:g % 2 * 512 + (k + 1) * T]
                        c = 2 * g + k
                        if shift is None:
                            last = dve.tensor_scalar(dst, bank(g % 4, k * T, T), scale[:, c:c + 1], None, ALU.mult)
                        else:
                            last = dve.tensor_scalar(dst, bank(g % 4, k * T, T), scale[:, c:c + 1],
                                                     shift[:, c:c + 1], ALU.mult, ALU.add)
                    last.then_inc(S["norm_scaled"], 1)
                if g:
                    dve.wait_ge(S["norm_hi"], 8 * n + g)
                    at = slice((g - 1) * 512, g * 512)
                    rest(xt_lo[:, at], turn[:, (g - 1) % 2 * 512:((g - 1) % 2 + 1) * 512], xt_hi[:, at],
                         S["norm_done"])

        def ffn(n, finish):
            conv = ffn_w[n]["conv"]

            def take(part, half):
                half_done(dve, f"down{n}{part}", half)
                for m in range(MT):
                    dst = f_nat[:, m * D + half * HALF:m * D + (half + 1) * HALF]
                    if part == 0:
                        last = dve.tensor_copy(dst, rows_cols(half, m))
                    else:
                        last = dve.tensor_tensor(dst, dst, rows_cols(half, m), ALU.add)
                        if n:
                            last.then_inc(S["piece_made"], 1)
                            if m == 0:
                                continue
                            dve.wait_ge(S["piece_made"], pieces_before(2 * n + 2 if n == 1 else 8) + 2 * half)
                            dve.sem_inc(S["rows_taken"], 1)
                            return
                last.then_inc(S["rows_taken"], 1)

            for part, (f0, chunks) in enumerate(PARTS):
                name, q0 = f"up{n}{part}", n * FC + f0

                def d1(j, s):
                    dve.wait_ge(S["pair_e1"], j + (q0 + 1))
                    if not conv:
                        dve.wait_ge(S["hid_made"], j + (q0 + 1))
                        dve.tensor_tensor(hval[:, s * T:(s + 1) * T], conv_a[:, s * T:(s + 1) * T],
                                          bank(s, T, T), ALU.mult).then_inc(S["pair_d1"], 1)
                        return
                    for t, o in ((conv_a, 0), (conv_v, FC)):
                        a = bank(s, 0 if o == 0 else T, T)
                        dve.scalar_tensor_tensor(
                            out=t[:, s * T + 1:(s + 1) * T], in0=a[:, 0:T - 1],
                            scalar=cols[:, ds(j + (C_CONV[0] + o + f0), 1)],
                            in1=t[:, s * T + 1:(s + 1) * T], op0=ALU.mult, op1=ALU.add).then_inc(S["conv_step"], 1)
                    dve.wait_ge(S["conv_step"], 2 * j + (2 * q0 + 2))
                    for t, o in ((conv_a, 0), (conv_v, FC)):
                        a = bank(s, 0 if o == 0 else T, T)
                        last = dve.scalar_tensor_tensor(
                            out=t[:, s * T:(s + 1) * T - 1], in0=a[:, 1:T],
                            scalar=cols[:, ds(j + (C_CONV[2] + o + f0), 1)],
                            in1=t[:, s * T:(s + 1) * T - 1], op0=ALU.mult, op1=ALU.add)
                    last.then_inc(S["pair_d1"], 1)

                def d2(j, s):
                    dve.wait_ge(S["pair_e2"], j + (q0 + 1))
                    dve.wait_ge(S["hid_made"], j + (q0 + 1))
                    dve.tensor_tensor(hval[:, s * T:(s + 1) * T], conv_a[:, s * T:(s + 1) * T],
                                      conv_v[:, s * T:(s + 1) * T], ALU.mult).then_inc(S["pair_d2"], 1)

                def d3(j, s):
                    dve.wait_ge(S["pair_e3"], j + (q0 + 1))
                    rest(hid_lo[:, ds(j * T, T)], hval[:, s * T:(s + 1) * T], hid_hi[:, ds(j * T, T)],
                         S["hid_made"])

                up_phase(dve, lambda i, u: split(name, 4, i, u), d2 if conv else d3,
                         d3 if conv else nothing, d1, chunks,
                         pending=(lambda: take(0, 1)) if part else nothing)
                down = f"down{n}{part}"
                for u in range(chunks):
                    split(down, chunks, 0, u)
                    if u == chunks // 2 + 1:
                        take(part, 0)
                    if part and u == chunks // 2 + 5:
                        finish(0)
            take(1, 1)
            finish(1)

        crep = xt_hi[:, :].rearrange("p (k n) -> p k n", n=T)
        dve.wait_ge(S["crep_hi"], 1)
        dve.tensor_tensor(crep[:, :, 32:64], csilu[:, :].unsqueeze(2).to_broadcast([P, KC, 32]),
                          xt_hi[:, :].bitcast(F32).rearrange("p (k n) -> p k n", n=T)[:, :, 0:32],
                          ALU.subtract).then_inc(S["crep_made"], 1)

        def ada(i):
            for h in range(32):
                dve.wait_ge(hi_made, 32 * i + (h + 1))
                at = slice(h % 4 * HALF, (h % 4 + 1) * HALF)
                dve.tensor_tensor(w_lo[:, at], stage[:, h % 8 * HALF:(h % 8 + 1) * HALF],
                                  w_hi[:, at].bitcast(F32), ALU.subtract).then_inc(split_made, 1)
        ada(0)
        norm_scale(0)
        with dve.Fori(1, 6) as i:
            ada(i)
        dve.wait_ge(S["tab_turned"], 1)
        for t, q in enumerate(TABLE_ROWS):
            last = dve.tensor_copy(cols[:, t * P:t * P + q], bank(5 + t // 4, t % 4 * P, q))
        last.then_inc(S["cols_made"], 1)
        if "ada" in run:
            dve.wait_ge(S["cols_made"], 1)
            dve.wait_ge(S["mod_turned"], 1)
            dve.tensor_tensor(mod[:, :], bank(7, 0, 96), cols[:, 0:96], ALU.add).then_inc(S["mod_made"], 1)
            dve.wait_ge(S["mod_made"], 1)
            for b in range(2):
                last = dve.scalar_tensor_tensor(out=scale_cols[:, b * KC:(b + 1) * KC],
                                                in0=mod[:, 16 + 48 * b:32 + 48 * b], scalar=1.0,
                                                in1=cols[:, C_N1 + KC * b:C_N1 + KC * (b + 1)],
                                                op0=ALU.add, op1=ALU.mult)
            link.then(last)
        if "norm0" in run:
            norm_finish(0, scale_cols[:, 0:KC], mod[:, 0:16])
        if "in" in run:
            with dve.Fori(0, 4) as i:
                for u in range(4):
                    split("in_tiles", 4, i, u)
            dve.memset(v_one[:, :].rearrange("p (k n) -> p k n", n=257)[:, :, 256:257], 1.0)
            for u in range(16):
                split("in_rows", 16, 0, u)
            dve.wait_ge(S["wg_split_hi"], 1)
            dve.tensor_tensor(wg_lo[:, 0:KC * 16].rearrange("p (k n) -> p k n", n=16),
                              wg_raw[:, :].rearrange("p (k n) -> p k n", n=48)[:, :, 0:16],
                              wg_hi[:, 0:KC * 16].bitcast(F32).rearrange("p (k n) -> p k n", n=16),
                              ALU.subtract).then_inc(S["wg_split"], 1)
            dve.wait_ge(S["g_made"], 1)
            dve.tensor_copy(g_nat[:, 0:32], bank(0, 0, 32)).then_inc(S["g_copied"], 1)
        if "four" in run:
            for g in range(4):
                dve.wait_ge(S["four2"], g + 1)
                dve.tensor_copy(turn[:, g % 2 * 512:(g % 2 + 1) * 512], bank(4 + g)).then_inc(S["four2_copied"], 1)
                dve.wait_ge(S["four2_hi"], g + 1)
                at = slice(g * 512, (g + 1) * 512)
                rest(xt_lo[:, at], turn[:, g % 2 * 512:(g % 2 + 1) * 512], xt_hi[:, at], S["mix_lo"])
        if "mlstm" in run:
            dve.wait_ge(S["gt_made"], 1)
            dve.wait_ge(S["const_in"], 32)
            dve.wait_ge(S["mix_lo"], 4)
            for k in range(4):
                last = dve.tensor_scalar(grow[:, k * T:(k + 1) * T], ps[0:4, k * T:(k + 1) * T],
                                         bgate[0:4, k:k + 1], None, ALU.add)
            last.then_inc(S["grow_made"], 1)
            dve.wait_ge(S["grow_made"], 1)
            igates = grow[:, :].rearrange("h (d k t) -> h k d t", d=2, k=2)[:, 0]
            fgates = grow[:, :].rearrange("h (d k t) -> h k d t", d=2, k=2)[:, 1]
            two = lambda a: a.rearrange("h (d t) -> h d t", d=2)
            dve.wait_ge(S["f_exp"], 1)
            dve.tensor_scalar(crow[:, :], crow[:, :], 1.0, None, ALU.add).then_inc(S["f_add"], 1)
            dve.wait_ge(S["f_ln"], 1)
            link.then(dve.scalar_tensor_tensor(out=two(lfrow[:, :]), in0=fgates, scalar=0.0,
                                               in1=two(crow[:, :]), op0=ALU.min, op1=ALU.subtract))

            def way(t, k, d):
                r = t[:, k * T:(k + 1) * T]
                return r if d == 0 else r[:, ::-1]
            for d in range(2):
                last = dve.tensor_tensor_scan(way(rows1, 2 + d, d), ones1[:, :], way(lfrow, d, d), 0.0,
                                              ALU.mult, ALU.add)
            link.then(last)
            link.then(dve.tensor_tensor(two(rows1[:, 0:512]), igates, two(rows1[:, 512:1024]), ALU.subtract))
            for d in range(2):
                last = dve.tensor_tensor_scan(way(rows1, 4 + d, d), ones1[:, :], way(rows1, d, d), NEG,
                                              ALU.mult, ALU.max)
            link.then(last)
            dve.tensor_tensor(rows1[:, 512:1024], rows1[:, 512:1024], rows1[:, 1024:1536],
                              ALU.add).then_inc(S["rows_made"], 1)
            dve.wait_ge(S["ec_made"], 1)
            dve.tensor_copy(ecols[:, :], bank(2, 0, 32)).then_inc(S["ec_copied"], 1)
            dve.wait_ge(S["ec_copied"], 1)
            dve.wait_ge(S["mask_in"], 16)
            dve.wait_ge(S["em_made"], 1)
            for h in range(HEADS1):
                dve.wait_ge(S["bcast_made"], h + 1)
                if h:
                    dve.wait_ge(S["pt_made"], h)
                for d in range(2):
                    for s in range(2):
                        x = 2 * d + s
                        last = dve.scalar_tensor_tensor(
                            out=ex1[:, x * T:(x + 1) * T], in0=mask1[:, x * T:(x + 1) * T],
                            scalar=ecols[:, x * 4 + h:x * 4 + h + 1], in1=bank(3, d * T, T),
                            op0=ALU.add, op1=ALU.subtract)
                last.then_inc(S["arg_made"], 1)
                dve.wait_ge(S["score_made"], h + 1)
                dve.wait_ge(S["exp_made"], h + 1)
                if h:
                    dve.wait_ge(S["num_made"], h)
                for d in range(2):
                    for s in range(2):
                        x = 2 * d + s
                        last = dve.scalar_tensor_tensor(
                            out=pt1[:, x * T:(x + 1) * T], in0=bank(4 + h % 2, s * T, T),
                            scalar=DK ** -0.5, in1=ex1[:, x * T:(x + 1) * T], op0=ALU.mult, op1=ALU.mult)
                last.then_inc(S["pt_made"], 1)
                dve.wait_ge(S["num_made"], h + 1)
                for d in range(2):
                    for m in range(MT):
                        x = 2 * d + m
                        last = dve.tensor_scalar(dcols[:, h * 8 + x:h * 8 + x + 1], bank(NUM[x], 256, 1), -1.0,
                                                 None, ALU.mult)
                link.then(last)
                for x in range(4):
                    last = dve.scalar_tensor_tensor(out=dcols[:, h * 8 + 4 + x:h * 8 + 5 + x],
                                                    in0=bank(NUM[x], 256, 1),
                                                    scalar=ecols[:, 16 + x * 4 + h:17 + x * 4 + h],
                                                    in1=dcols[:, h * 8 + x:h * 8 + x + 1], op0=ALU.max, op1=ALU.max)
                link.then(last)
                dinv = dcols[:, 32 + h * 8:36 + h * 8]
                link.then(dve.reciprocal(dinv, dcols[:, h * 8 + 4:h * 8 + 8]))
                for m in range(MT):
                    dst = h_nat[:, m * 1024 + h * 256:m * 1024 + (h + 1) * 256]
                    last = dve.tensor_scalar(dst, bank(NUM[m], 0, 256), dinv[:, m:m + 1], None, ALU.mult)
                link.then(last)
                for m in range(MT):
                    dst = h_nat[:, m * 1024 + h * 256:m * 1024 + (h + 1) * 256]
                    last = dve.scalar_tensor_tensor(out=dst, in0=bank(NUM[2 + m], 0, 256),
                                                    scalar=dinv[:, 2 + m:3 + m],
                                                    in1=dst, op0=ALU.mult, op1=ALU.add)
                last.then_inc(S["num_taken"], 1)
            dve.wait_ge(S["h_ssq"], 8)
            dve.tensor_scalar(stats[:, 8:16], stats[:, 8:16], 1.0 / DV, EPS, ALU.mult, ALU.add).then_inc(S["h_var"], 1)
            dve.wait_ge(S["h_std"], 1)
            link.then(dve.reciprocal(stats[:, 24:32], stats[:, 16:24]))
            dve.wait_ge(S["row_in"], 16)
            for m in range(MT):
                for h in range(HEADS1):
                    dst = h_nat[:, m * 1024 + h * 256:m * 1024 + (h + 1) * 256]
                    last = dve.scalar_tensor_tensor(out=dst, in0=dst, scalar=stats[:, 24 + m * 4 + h:25 + m * 4 + h],
                                                    in1=row[:, h * 256:(h + 1) * 256], op0=ALU.mult, op1=ALU.mult)
            last.then_inc(S["row_used"], 1)
            dve.wait_ge(S["row_used"], 1)
            dve.wait_ge(S["rows_taken"], 2)
            dve.tensor_tensor(h_nat[:, :], h_nat[:, :], o_sig[:, :], ALU.mult).then_inc(S["h_done"], 1)
            for g in range(4):
                dve.wait_ge(S["ym_turned"], g + 1)
                if g >= 2:
                    dve.wait_ge(S["mix_lo"], 3 + g)
                dve.tensor_copy(turn[:, g % 2 * 512:(g % 2 + 1) * 512], bank(g)).then_inc(S["ym_copied"], 1)
                dve.wait_ge(S["ym_hi"], g + 1)
                at = slice((4 + g) * 512, (5 + g) * 512)
                rest(xt_lo[:, at], turn[:, g % 2 * 512:(g % 2 + 1) * 512], xt_hi[:, at], S["mix_lo"])
        if "out1" in run:
            def take_out1(half):
                half_done(dve, "out1", half)
                dve.wait_ge(S["row_in"], 32)
                at = [slice(m * D + half * HALF, m * D + (half + 1) * HALF) for m in range(MT)]
                for m in range(MT):
                    last = dve.tensor_tensor(f_nat[:, at[m]], rows_cols(half, m),
                                             row[:, half * HALF:(half + 1) * HALF], ALU.mult)
                last.then_inc(S["rows_taken"], 1)
                dve.wait_ge(S["rows_taken"], 2 * rows_index["out1"] + half + 1)
                for m in range(MT):
                    dve.tensor_tensor(x_nat[:, at[m]], x_nat[:, at[m]], f_nat[:, at[m]],
                                      ALU.add).then_inc(S["piece_made"], 1)
                dve.wait_ge(S["piece_made"], 2 * half + 2)
            for u in range(16):
                split("out1", 16, 0, u)
                if u == 9:
                    take_out1(0)
            take_out1(1)
            dve.sem_inc(S["x_made"], 1)
            dve.sem_inc(S["row_used"], 1)
        if "ffn0" in run:
            norm(1, 1, scale_cols[:, KC:2 * KC], mod[:, 48:64])

            def finish0(half):
                dve.wait_ge(S["rows_taken"], 7 + half)
                dve.wait_ge(S["row_in"], 48)
                at = [slice(m * D + half * HALF, m * D + (half + 1) * HALF) for m in range(MT)]
                for m in range(MT):
                    last = dve.tensor_tensor(f_nat[:, at[m]], f_nat[:, at[m]], row[:, half * HALF:(half + 1) * HALF],
                                             ALU.mult)
                link.then(last)
                if half:
                    dve.sem_inc(S["row_used"], 1)
                for m in range(MT):
                    dve.tensor_tensor(x_nat[:, at[m]], x_nat[:, at[m]], f_nat[:, at[m]],
                                      ALU.add).then_inc(S["piece_made"], 1)
                dve.wait_ge(S["piece_made"], pieces_before(2) + 2 * half)
                if half:
                    dve.sem_inc(S["x_made"], 1)
            ffn(0, finish0)
        if "final1" in run:
            inverse_rms(2)
            dve.wait_ge(S["row_in"], 64)
            for m in range(MT):
                at = slice(m * D, (m + 1) * D)
                dve.scalar_tensor_tensor(out=x_nat[:, at], in0=x_nat[:, at], scalar=stats[:, 8 + m:9 + m],
                                         in1=row[:, :], op0=ALU.mult, op1=ALU.mult).then_inc(S["piece_made"], 1)
            dve.wait_ge(S["piece_made"], pieces_before(4) - 2)
            dve.sem_inc(S["row_used"], 1)
            dve.sem_inc(S["x_made"], 1)

        def post_norm(e, n_rows, weight, half):
            dve.wait_ge(S["row_in"], 16 * n_rows)
            for m in range(MT):
                at = slice(m * D + half * HALF, m * D + (half + 1) * HALF)
                dve.wait_ge(S["norm_ssq"], pieces_before(e) + 2 * half + m + 1)
                last = dve.tensor_tensor(f_nat[:, at], f_nat[:, at], row[:, half * HALF:(half + 1) * HALF], ALU.mult)
            link.then(last)
            if not half:
                return
            dve.sem_inc(S["row_used"], 1)
            inverse_rms(e)
            link.then(dve.tensor_scalar(stats[:, 10:12], stats[:, 8:10], weight, None, ALU.mult))
            for m in range(MT):
                at = slice(m * D, (m + 1) * D)
                last = dve.scalar_tensor_tensor(out=x_nat[:, at], in0=f_nat[:, at], scalar=stats[:, 10 + m:11 + m],
                                                in1=x_nat[:, at], op0=ALU.mult, op1=ALU.add).then_inc(S["piece_made"], 1)
            dve.wait_ge(S["piece_made"], pieces_before(e + 1))
            dve.sem_inc(S["x_made"], 1)
        if "ffn1" in run:
            norm(3, 2, cols[:, C_F1:C_F1 + KC], None)
            ffn(1, lambda half: post_norm(4, 5, 0.5, half))
        if "mix2" in run:
            norm(5, 3, cols[:, C_MP:C_MP + KC], None)
            with dve.Fori(0, 7) as i:
                for u in range(4):
                    split("in2", 4, i, u)
            dve.wait_ge(S["wg_split_hi"], 2)
            dve.tensor_tensor(wg_lo[:, :], wg_raw[:, :], wg_hi[:, :].bitcast(F32), ALU.subtract).then_inc(S["wg_split"], 1)
            dve.wait_ge(S["tile_copied"], 48)
            dve.tensor_scalar(pt2[:, 8 * T:16 * T], pt2[:, 8 * T:16 * T], DH ** -0.5, None,
                              ALU.mult).then_inc(S["q_scaled"], 1)
            for br in range(2):
                src = pt2[:, (20 + 4 * br) * T:(22 + 4 * br) * T]
                dve.tensor_copy(swp[0:64, br * 512:(br + 1) * 512], src[64:128, :])
                last = dve.tensor_copy(swp[64:128, br * 512:(br + 1) * 512], src[0:64, :])
            last.then_inc(S["swapped"], 1)
            dve.wait_ge(S["rev_made"], 1)
            dve.tensor_copy(rev_sb[:, :], bank(3, 0, 384, 16)).then_inc(S["rev_copied"], 1)
            dve.wait_ge(S["biasc_made"], 1)
            dve.wait_ge(S["x_made"], 4)
            dve.tensor_copy(biasc[:, :], bank(4, 0, 480)).then_inc(S["biasc_copied"], 1)
            dve.wait_ge(S["pos_made"], 1)
            dve.tensor_copy(pos_t[:, :], bank(5, 0, 32)).then_inc(S["pos_copied"], 1)
        if "cmp" in run:
            dve.wait_ge(S["pos_copied"], 1)
            for x, raw in enumerate((raw_k, raw_v)):
                for g in range(NKV):
                    src = pt2[g % 2 * 64:g % 2 * 64 + 64, (16 + 2 * x + g // 2) * T:(17 + 2 * x + g // 2) * T]
                    tok = src.rearrange("p (i l two) -> p two l i", l=8, two=2)
                    pos = pos_t[g % 2 * 64:g % 2 * 64 + 64, :].rearrange("p (l two) -> p two l", two=2)
                    for two in range(2):
                        dst = raw[two * 64:two * 64 + 64, :].rearrange("p (l c) -> p l c", c=60)
                        for lh in range(2):
                            last = dve.tensor_tensor(
                                dst[:, 8 * lh:8 * lh + 8, 15 * g:15 * g + 15], tok[:, two, :, lh:lh + 15],
                                pos[:, two, 8 * lh:8 * lh + 8].unsqueeze(2).to_broadcast([64, 8, 15]), ALU.add)
                last.then_inc(S["raw_made"], 1)
            for x in range(2):
                dve.wait_ge(S["ht_made"], x + 1)
                dve.tensor_copy(hid_t[:, x * 120:(x + 1) * 120], bank(x, 0, 120)).then_inc(S["ht_copied"], 1)
            dve.wait_ge(S["kv_made"], 1)
            dve.tensor_copy(kc_t[:, :], bank(2, 0, 60))
            dve.tensor_copy(vc_n[:, :], bank(3, 0, 256, 15)).then_inc(S["kv_copied"], 1)
            for m in range(MT):
                v = cmp_s[:, m * 240:(m + 1) * 240].rearrange("p (h i) -> p h i", i=15)
                mx = sm[:, m * 16:(m + 1) * 16]
                wide = lambda a: a.unsqueeze(2).to_broadcast([P, NH, NCMP])
                dve.wait_ge(S["cs_made"], m + 1)
                dve.wait_ge(S["biasc_copied"], 1)
                for odd in range(2):
                    last = dve.tensor_tensor(
                        v.rearrange("p (a two) i -> p two a i", two=2)[:, odd],
                        bank((4, 2)[odd] + m, 0, 120).rearrange("p (h i) -> p h i", i=15),
                        biasc[:, m * 240:(m + 1) * 240].rearrange("p (i h two) -> p two h i", h=8, two=2)[:, odd], ALU.add)
                link.then(last)
                link.then(dve.tensor_reduce(mx, v, AX.X, ALU.max))
                dve.tensor_tensor(v, v, wide(mx), ALU.subtract).then_inc(S["cs_max"], 1)
                dve.wait_ge(S["cs_exp"], m + 1)
                rs = sm[:, 32:48]
                link.then(dve.tensor_reduce(rs, v, AX.X, ALU.add))
                link.then(dve.reciprocal(rs, rs))
                gate = g_nat[:, m * 48:(m + 1) * 48].rearrange("p (h b) -> p b h", b=3)[:, 0]
                link.then(dve.tensor_tensor(rs, rs, gate, ALU.mult))
                if m == 0:
                    link.then(dve.tensor_scalar(rs, rs, live[:, 0:1], None, ALU.mult))
                dve.tensor_tensor(v, v, wide(rs), ALU.mult).then_inc(S["cs_done"], 1)
                dve.wait_ge(S["cs_done"], m + 1)
            for x in range(4):
                dve.wait_ge(S["co_made"], x + 1)
                dve.tensor_copy(o_nat[:, x * 512:(x + 1) * 512], bank(6 + x % 2)).then_inc(S["co_copied"], 1)
        if "attn" in run:
            dve.wait_ge(S["strips_in"], 16)
            dve.wait_ge(S["co_copied"], 4)
            for i in range(2 * NH + 3):
                if i < 2 * NH:
                    h = i % NH
                    dve.wait_ge(S["sc_made"], i + 1)
                    if i >= 2:
                        dve.wait_ge(S["pt_turned"], i - 1)
                    for m in range(MT):
                        at = i % 2 * 384 + m * P
                        n = (m + 1) * P
                        last = dve.tensor_tensor_reduce(soft[:, at:at + n], bank(i % 2, m * P, n),
                                                        strips[:, h * T + T - n:(h + 1) * T], 1.0, -3e38, ALU.add,
                                                        ALU.max, sm[:, 2 * i + m:2 * i + m + 1])
                    link.then(last)
                    dve.tensor_scalar(sm[:, 64 + 2 * i:66 + 2 * i], sm[:, 2 * i:2 * i + 2], -1.0, None,
                                      ALU.mult).then_inc(S["sc_max"], 1)
                if i >= 6 and (i - 6) % 4 == 0:
                    take4(dve, link, (i - 6) // 4)
            for g in range(4):
                dve.wait_ge(S["on_turned"], g + 1)
                if g:
                    dve.wait_ge(S["on_lo"], g)
                dve.tensor_copy(hval[:, :], bank(g)).then_inc(S["on_copied"], 1)
                dve.wait_ge(S["on_hi"], g + 1)
                at = slice(g * 512, (g + 1) * 512)
                rest(po_lo[:, at], hval[:, :], po_hi[:, at], S["on_lo"])
        if "s5" in run:
            pc = lambda i: par[:, i * ST:(i + 1) * ST]
            a_im = cols[:, C_AIM:C_AIM + ST]
            tt = lambda o, a, b, op: dve.tensor_tensor(o, a, b, op)
            dve.wait_ge(S["s5_in"], 16 * N_S5)
            dve.memset(cw[:, :], 0.0)
            link.then(dve.tensor_scalar(pc(1), cols[:, C_ARE:C_ARE + ST], -1e-4, None, ALU.min))
            dve.wait_ge(S["p_dt"], 1)
            dve.tensor_tensor(pc(2), pc(1), pc(0), ALU.mult).then_inc(S["p_x"], 1)
            tt(pc(8), pc(1), pc(1), ALU.mult)
            tt(pc(9), a_im, a_im, ALU.mult)
            link.then(tt(pc(3), a_im, pc(0), ALU.mult))
            c1 = 6.28125
            c2 = math.floor((TWO_PI - c1) * 2 ** 20) / 2 ** 20
            c3 = TWO_PI - c1 - c2
            tt(pc(8), pc(8), pc(9), ALU.add)
            link.then(dve.tensor_scalar(pc(10), pc(3), 1 / TWO_PI, ROUND, ALU.mult, ALU.add))
            link.then(dve.tensor_scalar(pc(10), pc(10), ROUND, None, ALU.subtract))
            for c in (c1, c2, c3):
                link.then(dve.scalar_tensor_tensor(out=pc(3), in0=pc(10), scalar=-c, in1=pc(3), op0=ALU.mult, op1=ALU.add))
            link.then(dve.tensor_scalar(pc(5), pc(3), 1 / TWO_PI, 0.5, ALU.mult, ALU.min))
            dve.tensor_scalar(pc(5), pc(5), -0.5, None, ALU.max).then_inc(S["p_phi"], 1)
            dve.reciprocal(pc(9), pc(8))
            dve.wait_ge(S["p_mag"], 1)
            dve.wait_ge(S["p_sin"], 1)
            link.then(dve.tensor_scalar(pc(7), pc(7), -1.0, 1.0, ALU.mult, ALU.add))
            tt(pc(6), pc(6), pc(4), ALU.mult)
            link.then(tt(pc(7), pc(7), pc(4), ALU.mult))
            link.then(dve.tensor_scalar(pc(7), pc(7), -1.0, None, ALU.add))
            tt(pc(10), pc(7), pc(1), ALU.mult)
            tt(pc(11), pc(6), a_im, ALU.mult)
            tt(pc(12), pc(6), pc(1), ALU.mult)
            link.then(tt(pc(13), pc(7), a_im, ALU.mult))
            tt(pc(10), pc(10), pc(11), ALU.add)
            link.then(tt(pc(12), pc(12), pc(13), ALU.subtract))
            tt(pc(14), pc(10), pc(9), ALU.mult)
            link.then(tt(pc(15), pc(12), pc(9), ALU.mult))

            def angle(pr):
                base_at = pr % 2 * 512
                at = slice(base_at, base_at + 512)
                if pr >= 2:
                    dve.wait_ge(S["cos_made"], pr - 1)
                for e in range(2):
                    last = dve.tensor_scalar(trig[:, base_at + e * T:base_at + (e + 1) * T], trow[:, :],
                                             pc(5)[:, 2 * pr + e:2 * pr + e + 1], ROUND, ALU.mult, ALU.add)
                link.then(last)
                link.then(dve.tensor_scalar(trig[:, at], trig[:, at], ROUND, None, ALU.subtract))
                for e in range(2):
                    part = slice(base_at + e * T, base_at + (e + 1) * T)
                    last = dve.scalar_tensor_tensor(out=trig[:, part], in0=trow[:, :],
                                                    scalar=pc(5)[:, 2 * pr + e:2 * pr + e + 1],
                                                    in1=trig[:, part], op0=ALU.mult, op1=ALU.subtract)
                last.then_inc(S["ang_made"], 1)

            def make_cosine(pr):
                at = slice(pr % 2 * 512, (pr % 2 + 1) * 512)
                dve.wait_ge(S["ang_sin"], pr + 1)
                if pr >= 2:
                    dve.wait_ge(S["back_made"], pr - 1)
                dve.tensor_scalar(cosine[:, at], trig[:, at], -1.0, 1.0, ALU.mult, ALU.add).then_inc(S["cos_made"], 1)

            def make_c(c):
                dve.wait_ge(S["bt_made"], c + 1)
                if c >= 2:
                    dve.wait_ge(S["y_made"], 2 * (c - 1))
                cr, ci = bank(6, 0, P), bank(6, P, P)
                f = [pc(14 + v)[:, 4 * c:4 * c + 4].unsqueeze(2).to_broadcast([P, 4, 32]) for v in range(2)]
                b3 = lambda a: a.rearrange("p (j n) -> p j n", n=32)
                t = [ct[:, k * P:(k + 1) * P] for k in range(4)]
                for o, a, b in ((0, cr, 0), (1, ci, 1), (2, cr, 1), (3, ci, 0)):
                    last = tt(b3(t[o]), b3(a), f[b], ALU.mult)
                link.then(last)
                tt(t[0], t[0], t[1], ALU.subtract)
                link.then(tt(t[2], t[2], t[3], ALU.add))
                base_at = (c % 2) * 1536
                mk = cmask[:, :].unsqueeze(1).to_broadcast([P, 4, 32])
                for k, (a, sign) in enumerate(((t[0], 1.0), (t[0], -1.0), (t[2], -1.0))):
                    whole = cw[:, base_at + k * 512:base_at + (k + 1) * 512]
                    for jj in range(4):
                        dst = whole[:, jj * P + jj * 32:jj * P + jj * 32 + 32]
                        last = dve.scalar_tensor_tensor(out=dst, in0=a[:, jj * 32:(jj + 1) * 32], scalar=sign,
                                                        in1=cmask[:, :], op0=ALU.mult, op1=ALU.mult)
                last.then_inc(S["cw_made"], 1)
                dve.wait_ge(S["cw_made"], c + 1)

            def sum_y(c):
                dve.wait_ge(S["y_made"], 2 * c + 2)
                if c >= 2:
                    dve.wait_ge(S["y_lo"], c - 1)
                dve.scalar_tensor_tensor(out=hval[:, c % 2 * T:(c % 2 + 1) * T], in0=chunk(pt2, c),
                                         scalar=cols[:, C_SD + c:C_SD + c + 1], in1=bank(7, 0, T),
                                         op0=ALU.mult, op1=ALU.add).then_inc(S["y_sum"], 1)

            def rest_y(c):
                dve.wait_ge(S["y_hi"], c + 1)
                rest(chunk(ps_lo, c), hval[:, c % 2 * T:(c % 2 + 1) * T], chunk(ps_hi, c), S["y_lo"])

            angle(0)
            make_cosine(0)
            for c in range(8):
                make_c(c)
                for pr in (2 * c, 2 * c + 1):
                    at = slice(pr % 2 * 512, (pr % 2 + 1) * 512)
                    if pr < 15:
                        angle(pr + 1)
                    dve.wait_ge(S["bu_made"], pr + 1)
                    dve.wait_ge(S["cos_made"], pr + 1)
                    if pr >= 1:
                        dve.wait_ge(S["scan_made"], pr)
                    if pr >= 2:
                        dve.wait_ge(S["back_made"], pr - 1)
                    br, bi = bank(2 * (pr % 2)), bank(2 * (pr % 2) + 1)
                    tt(rot_r[:, :], br, cosine[:, at], ALU.mult)
                    tt(z_r[:, at], bi, sine[:, at], ALU.mult)
                    tt(rot_i[:, :], bi, cosine[:, at], ALU.mult)
                    link.then(tt(z_i[:, at], br, sine[:, at], ALU.mult))
                    tt(rot_r[:, :], rot_r[:, :], z_r[:, at], ALU.add)
                    link.then(tt(rot_i[:, :], rot_i[:, :], z_i[:, at], ALU.subtract))
                    for src, dst in ((rot_r, z_r), (rot_i, z_i)):
                        for e in range(2):
                            j = 2 * pr + e
                            part = slice(pr % 2 * 512 + e * T, pr % 2 * 512 + (e + 1) * T)
                            last = dve.tensor_tensor_scan(dst[:, part], pc(4)[:, j:j + 1].to_broadcast([P, T]),
                                                          src[:, e * T:(e + 1) * T], 0.0, ALU.mult, ALU.add)
                    last.then_inc(S["scan_made"], 1)
                    if pr < 15:
                        make_cosine(pr + 1)
                    if pr % 2 == 0 and c:
                        sum_y(c - 1)
                    if pr % 2 == 1 and c:
                        rest_y(c - 1)
            sum_y(7)
            rest_y(7)
        if "merge" in run:
            sg_a, sg_b, sg_2 = (sgates[:, k * T:(k + 1) * T] for k in range(3))
            ta, tb = (sgates[:, k * T:(k + 1) * T] for k in (3, 4))
            mb = plan["merge"][1]

            def branch_a(i):
                dve.wait_ge(S["mg_2"], i)
                dve.wait_ge(S["mg_a"], i)
                dve.tensor_tensor(ta, bank(2, 0, T), sg_2, ALU.mult).then_inc(S["mg_d"], 1)
                dve.wait_ge(S["mg_d"], i)
                dve.tensor_tensor(ta, ta, sg_a, ALU.mult).then_inc(dve_merge, 1)

            def both(i):
                dve.wait_ge(split_used, mb + 2 + i * 4)
                dve.wait_ge(S["mg_b"], i)
                dve.tensor_tensor(tb, bank(4, 0, T), sg_b, ALU.mult).then_inc(dve_merge, 1)
                dve.wait_ge(dve_merge, 2 * i)
                dve.tensor_tensor(hval[:, 0:T], ta, tb, ALU.add).then_inc(S["mg_sum"], 1)

            def rest_merge(i):
                dve.wait_ge(S["mg_hi"], i)
                rest(hid_lo[:, ds(i * T - T, T)], hval[:, 0:T], hid_hi[:, ds(i * T - T, T)], S["mixed_made"])
                dve.wait_ge(S["mixed_made"], i)

            def merge(i, fresh):
                split("merge", 4, i, 0)
                if not fresh:
                    branch_a(i)
                split("merge", 4, i, 1)
                if not fresh:
                    both(i)
                split("merge", 4, i, 2)
                if not fresh:
                    rest_merge(i)
                split("merge", 4, i, 3)
            merge(0, True)
            with dve.Fori(1, 16) as i:
                merge(i, False)
            branch_a(16)
            both(16)
            rest_merge(16)
        if "out2" in run:
            def take_out2(half):
                half_done(dve, "out2", half)
                for m in range(MT):
                    dve.tensor_copy(f_nat[:, m * D + half * HALF:m * D + (half + 1) * HALF],
                                    rows_cols(half, m)).then_inc(S["piece_made"], 1)
                dve.wait_ge(S["piece_made"], pieces_before(6) + 2 * half)
                dve.sem_inc(S["rows_taken"], 1)
            for u in range(16):
                split("out2", 16, 0, u)
                if u == 9:
                    take_out2(0)
                if u == 14:
                    post_norm(6, 6, 1.0, 0)
            take_out2(1)
            post_norm(6, 6, 1.0, 1)
        if "ffn2" in run:
            norm(7, 4, cols[:, C_F2:C_F2 + KC], None)
            ffn(2, lambda half: post_norm(8, 7, 0.5, half))

    @block.tensor
    def _(pe):
        pe.sem_inc(split_used, 2)

        def tile_unit(name, per_body, i, u, dst, xh=xt_hi, xl=xt_lo, k0=0, n=KC, w0=0, waits=True, done=True,
                      norm_index=None):
            if waits:
                pe.wait_ge(split_made, plan[name][1] + u + 1 + i * per_body)
            at = u % 2 * UNIT + w0
            for k in range(n):
                if norm_index is not None and k % 2 == 0:
                    pe.wait_ge(S["norm_done"], 8 * norm_index + k // 2 + 1)
                wh, wl = (w[:, at + k * P:at + (k + 1) * P] for w in (w_hi, w_lo))
                pe.matmul(dst, wh, chunk(xh, k0 + k), start=k == 0, stop=False)
                pe.matmul(dst, wh, chunk(xl, k0 + k), start=False, stop=False)
                last = pe.matmul(dst, wl, chunk(xh, k0 + k), start=False, stop=k == n - 1)
            if done:
                last.then_inc(split_used, 1)
            return last

        def rows_half(name, per_half, half, u0, split0, xh=xt_hi, xl=xt_lo):
            for c in range(per_half):
                u = u0 + c
                pe.wait_ge(split_made, split0 + c + 1)
                for kk in range(2):
                    k = 2 * c + kk
                    for m in range(MT):
                        a, b = chunk(xh, k, m), chunk(xl, k, m)
                        st, en = k == 0, k == 2 * per_half - 1
                        at = u % 2 * UNIT + kk * HALF
                        for n in range(2):
                            wh, wl = (w[:, at + n * 512:at + (n + 1) * 512] for w in (w_hi, w_lo))
                            pe.matmul(rows_cols(half, m, n, 512), a, wh, start=st, stop=False)
                            pe.matmul(rows_cols(half, m, n, 512), a, wl, start=False, stop=False)
                        for n in range(2):
                            wh = w_hi[:, at + n * 512:at + (n + 1) * 512]
                            last = pe.matmul(rows_cols(half, m, n, 512), b, wh, start=False, stop=en)
                last.then_inc(split_used, 1)

        def rows_phase(name, per_half, xh=xt_hi, xl=xt_lo):
            r = rows_index[name]
            if r:
                pe.wait_ge(S["rows_taken"], 2 * r)
            before = plan[name][1]
            if per_half % 2 == 0:
                with pe.Fori(0, 2) as half:
                    rows_half(name, per_half, half, 0, half * per_half + before, xh, xl)
            else:
                for half in range(2):
                    rows_half(name, per_half, half, half * per_half, half * per_half + before, xh, xl)

        def norm(n, groups=range(8)):
            pe.wait_ge(S["norm_xhat"], 2 * (n + 1))
            for g in groups:
                if g >= 4:
                    pe.wait_ge(S["norm_scaled"], 8 * n + g - 3)
                for k in range(2):
                    for m in range(MT):
                        c = 2 * g + k
                        last = pe.transpose(bank(g % 4, k * T + m * P, P),
                                            f_nat[:, m * D + c * P:m * D + (c + 1) * P], ident[:, :])
                last.then_inc(S["norm_turned"], 1)

        def ffn(n):
            for part, (f0, chunks) in enumerate(PARTS):
                q0 = n * FC + f0
                name = f"up{n}{part}"
                if part:
                    pe.wait_ge(S["rows_taken"], 2 * rows_index[f"down{n}0"] + 1)
                with pe.Fori(0, chunks // 2) as i:
                    for s in range(2):
                        pe.wait_ge(S["pair_d1"], q0 + 1 + s + 2 * i)
                        for v in range(2):
                            tile_unit(name, 4, i, 2 * s + v, bank(s, v * T, T),
                                      norm_index=None if part or s or v else NORM_OF[n])
                pe.wait_ge(S["hid_made"], q0 + chunks + 2)
                rows_phase(f"down{n}{part}", chunks // 2, hid_hi, hid_lo)

        pe.wait_ge(S["c_in"], 32)
        pe.transpose(bank(4, 0, KC), conv_a[0:16, 0:P], ident[0:16, 0:16]).then_inc(S["c_turned"], 1)
        pe.wait_ge(S["crep_made"], 1)
        with pe.Fori(0, 6) as i:
            for b in range(2):
                pe.wait_ge(S["ada_taken"], 2 * i + (b + 1))
                for k in range(KC):
                    pe.wait_ge(split_made, 32 * i + (16 * b + k + 1))
                    a = xt_hi[:, k * T:k * T + 64]
                    at = k % 4 * HALF
                    for n in range(2):
                        dst = bank(2 * b + n, 0, 512, 64)
                        pe.matmul(dst, a, w_hi[:, at + n * 512:at + (n + 1) * 512], start=k == 0, stop=False)
                        last = pe.matmul(dst, a, w_lo[:, at + n * 512:at + (n + 1) * 512], start=False,
                                         stop=k == KC - 1)
                    last.then_inc(split_used, 1)
        pe.wait_ge(S["tab_ready"], 1)
        pe.wait_ge(S["norm_xhat"], 2)
        for t, q in enumerate(TABLE_ROWS):
            last = pe.transpose(bank(5 + t // 4, t % 4 * P, q), rowtab[0:q, t * P:(t + 1) * P], ident[0:q, 0:q])
        last.then_inc(S["tab_turned"], 1)
        pe.wait_ge(S["ada_taken"], 14)
        norm(0, range(4))
        pe.wait_ge(S["modrow_in"], 32)
        for v, t in enumerate((conv_a, conv_v)):
            last = pe.matmul(bank(7, 0, 96), t[0:96, 0:P], ident[0:96, 0:96], start=v == 0, stop=v == 1)
        last.then_inc(S["mod_turned"], 1)
        norm(0, range(4, 8))
        if "in" in run:
            with pe.Fori(0, 4) as i:
                for u in range(4):
                    pe.wait_ge(S["tile_copied"], 4 * i + (u + 1))
                    tile_unit("in_tiles", 4, i, u, bank(u, 0, T), norm_index=None if u else 0)
            pe.wait_ge(S["tile_copied"], 20)
            rows_phase("in_rows", 8)
            pe.wait_ge(S["wg_split"], 1)
            pe.wait_ge(S["rows_taken"], 1)
            gates(pe, 16, 0)
        if "four" in run:
            pe.wait_ge(S["dft_in"], 32)
            pe.wait_ge(S["g_copied"], 1)

            def four1(g):
                if g >= 2:
                    pe.wait_ge(S["four1_copied"], 2 * (g - 1))
                for m in range(MT):
                    for k in range(2):
                        last = pe.matmul(bank(2 * (g % 2) + m), chunk(projt, 2 * g + k, m),
                                         dft1[:, k * 512:(k + 1) * 512], start=k == 0, stop=k == 1)
                last.then_inc(S["four1"], 1)

            four1(0)
            pe.wait_ge(S["rows_taken"], 2)
            for g in range(4):
                if g < 3:
                    four1(g + 1)
                pe.wait_ge(S["four1_copied"], 2 * (g + 1))
                for c in range(2):
                    for s in range(2):
                        for v in range(2):
                            a = s * 512 + v * T + c * P
                            last = pe.matmul(bank(4 + g, c * T, T), four[:, a:a + P],
                                             dft2[:, s * 512 + v * T:s * 512 + (v + 1) * T],
                                             start=s + v == 0, stop=s + v == 2)
                last.then_inc(S["four2"], 1)
        if "mlstm" in run:
            for k in range(4):
                for m in range(MT):
                    last = pe.transpose(ps[0:4, k * T + m * P:k * T + (m + 1) * P],
                                        g_nat[:, m * 16 + 4 * k:m * 16 + 4 * k + 4], ident[:, :])
            last.then_inc(S["gt_made"], 1)
            pe.wait_ge(S["rows_made"], 1)
            for r in range(4):
                for s in range(2):
                    last = pe.transpose(bank(2, (2 * r + s) * 4, 4), rows1[:, r * T + s * P:r * T + (s + 1) * P],
                                        ident[0:4, 0:4])
            last.then_inc(S["ec_made"], 1)
            pe.wait_ge(S["const_in"], 32)
            for h in range(HEADS1):
                if h:
                    pe.wait_ge(S["arg_made"], h)
                pe.matmul(bank(3), sel1[:, h * P:(h + 1) * P], rows1[:, 1024:1536], start=True,
                          stop=True).then_inc(S["bcast_made"], 1)
                for s in range(2):
                    last = pe.matmul(bank(4 + h % 2, s * T, T), chunk(projt, 12 + h, s), chunk(projt, 8 + h),
                                     start=True, stop=True)
                last.then_inc(S["score_made"], 1)
                pe.wait_ge(S["pt_made"], h + 1)
                if h:
                    pe.wait_ge(S["num_taken"], h)
                for d in range(2):
                    for m in range(MT):
                        keys = [s for s in range(2) if (s <= m if d == 0 else s >= m)]
                        for s in keys:
                            x = 2 * d + s
                            last = pe.matmul(bank(NUM[2 * d + m], 0, 257), pt1[:, x * T + m * P:x * T + (m + 1) * P],
                                             v_one[:, s * 1028 + h * 257:s * 1028 + (h + 1) * 257],
                                             start=s == keys[0], stop=s == keys[-1])
                last.then_inc(S["num_made"], 1)
            pe.wait_ge(S["h_done"], 1)
            for g in range(4):
                for k in range(2):
                    for m in range(MT):
                        c = 2 * g + k
                        last = pe.transpose(bank(g, k * T + m * P, P),
                                            h_nat[:, m * 1024 + c * P:m * 1024 + (c + 1) * P], ident[:, :])
                last.then_inc(S["ym_turned"], 1)
        if "out1" in run:
            pe.wait_ge(S["mix_lo"], 8)
            rows_phase("out1", 8)
        if "ffn0" in run:
            norm(1)
            ffn(0)
        if "ffn1" in run:
            norm(2)
            ffn(1)
        if "mix2" in run:
            norm(3)
            with pe.Fori(0, 7) as i:
                for u in range(4):
                    pe.wait_ge(S["tile_copied"], 4 * i + (u + 17))
                    tile_unit("in2", 4, i, u, bank(u, 0, T), norm_index=None if u else 3)
            pe.wait_ge(S["tile_copied"], 48)
            pe.wait_ge(S["wg_split"], 2)
            gates(pe, 48, 1)
            for br in range(2):
                for st in range(2):
                    for c in range(2):
                        last = pe.transpose(bank(1 + br, st * T + c * P, P), chunk(pt2, 22 + 4 * br + c, st), ident[:, :])
            last.then_inc(S["vt_made"], 1)
            pe.wait_ge(S["oh_in"], 64)
            pe.matmul(bank(3, 0, 384, 16), relb[:, :], oh_rev[:, :], start=True, stop=True).then_inc(S["rev_made"], 1)
            for m in range(MT):
                for i in range(NCMP):
                    a = 255 + P * m - 16 * i - 31
                    last = pe.matmul(bank(4, m * 240 + i * 16, 16), oh_fwd[:, a:a + P], relb[:, :],
                                     start=True, stop=True)
            last.then_inc(S["biasc_made"], 1)
            pe.wait_ge(S["small_in"], 16 * N_SMALL)
            pe.transpose(bank(5, 0, 32), pos2[:, :], ident[0:32, 0:32]).then_inc(S["pos_made"], 1)
        if "cmp" in run:
            for x, raw in enumerate((raw_k, raw_v)):
                pe.wait_ge(S["raw_made"], x + 1)
                for u in range(2):
                    pe.wait_ge(landed[2 * x + u], 16 * (plan["cmp"][0] // SLOTS + 1))
                    for k in range(8):
                        kk = 8 * u + k
                        last = pe.matmul(bank(6 + x, 0, T, 60), raw[:, kk * 60:(kk + 1) * 60],
                                         stage[:, (2 * x + u) * UNIT + k * T:(2 * x + u) * UNIT + (k + 1) * T],
                                         start=kk == 0, stop=kk == 15)
                    last.then_inc(direct_used, 1)
            pe.wait_ge(S["pos_copied"], 1)
            for x in range(2):
                pe.wait_ge(S["hn_gelu"], x + 1)
                for c in range(2):
                    last = pe.transpose(bank(x, c * 60, 60), hid_n[:, x * T + c * P:x * T + (c + 1) * P], ident[0:60, 0:60])
                last.then_inc(S["ht_made"], 1)
            pe.wait_ge(S["ht_copied"], 2)
            for c in range(2):
                pe.matmul(bank(2, 0, 60), w2[:, c * P:(c + 1) * P], hid_t[:, c * 60:(c + 1) * 60], start=c == 0, stop=c == 1)
            for g in range(NKV):
                for c in range(2):
                    last = pe.matmul(bank(3, g * DH, DH, 15), hid_t[:, 120 + c * 60 + g * 15:120 + c * 60 + (g + 1) * 15],
                                     w2[:, 2 * P + c * DH:2 * P + (c + 1) * DH], start=c == 0, stop=c == 1)
            last.then_inc(S["kv_made"], 1)
            pe.wait_ge(S["kv_copied"], 1)
            for m in range(MT):
                for h in range(NH):
                    half = slice(h % 2 * 64, h % 2 * 64 + 64)
                    q = pt2[half, (8 + h // 2) * T + m * P:(8 + h // 2) * T + (m + 1) * P]
                    last = pe.matmul(bank((4, 2)[h % 2] + m, h // 2 * 15, 15), q, kc_t[half, h // 4 * 15:(h // 4 + 1) * 15],
                                     start=True, stop=True)
                last.then_inc(S["cs_made"], 1)
            x = 0
            for m in range(MT):
                pe.wait_ge(S["cs_done"], m + 1)
                for q4 in range(4):
                    if x >= 2:
                        pe.wait_ge(S["ct_copied"], x - 1)
                    for j in range(4):
                        h = 4 * q4 + j
                        last = pe.transpose(bank(x % 2, j * P, P, 15), cmp_s[:, m * 240 + h * 15:m * 240 + (h + 1) * 15],
                                            ident[:, :])
                    last.then_inc(S["ct_made"], 1)
                    pe.wait_ge(S["ct_copied"], x + 1)
                    if x % 2 == 0 and x >= 4:
                        pe.wait_ge(S["co_copied"], x // 2 - 1)
                    for j in range(4):
                        h = 4 * q4 + j
                        last = pe.matmul(bank(6 + x // 2 % 2, (h % 8) * DH, DH), cmp_t[:, x % 2 * 512 + j * P:x % 2 * 512 + (j + 1) * P],
                                         vc_n[:, h // 4 * DH:(h // 4 + 1) * DH], start=True, stop=True)
                    if q4 % 2:
                        last.then_inc(S["co_made"], 1)
                    x += 1
        if "attn" in run:
            def key_tile(br, h):
                g = h // 4
                if g % 2 == h % 2:
                    return pt2, 20 + 4 * br + g // 2
                return swp, 2 * br + g // 2

            for i in range(2 * NH + 2):
                if i < 2 * NH:
                    br, h = i // NH, i % NH
                    if i >= 2:
                        pe.wait_ge(S["sc_max"], i - 1)
                    else:
                        pe.wait_ge(S["co_copied"], 4)
                    half = slice(h % 2 * 64, h % 2 * 64 + 64)
                    kt, kc = key_tile(br, h)
                    for m in range(MT):
                        n = (m + 1) * P
                        last = pe.matmul(bank(i % 2, m * P, n), pt2[half, (8 + h // 2) * T + m * P:(8 + h // 2) * T + (m + 1) * P],
                                         kt[half, kc * T:kc * T + n], start=True, stop=True)
                    last.then_inc(S["sc_made"], 1)
                if 1 <= i <= 2 * NH:
                    j = i - 1
                    pe.wait_ge(S["sc_exp"], j + 1)
                    if j >= 2:
                        pe.wait_ge(S["pt_copied"], j - 1)
                    for b in range(3):
                        last = pe.transpose(bank(2 + j % 2, b * P, P), soft[:, j % 2 * 384 + b * P:j % 2 * 384 + (b + 1) * P],
                                            ident[:, :])
                    last.then_inc(S["pt_turned"], 1)
                if i >= 2:
                    j = i - 2
                    br, h = j // NH, j % NH
                    pe.wait_ge(S["pt_copied"], j + 1)
                    if j % 4 == 0 and j >= 8:
                        pe.wait_ge(S["av_taken"], j // 4 - 1)
                    b, at = 4 + j // 4 % 2, j % 4 * P
                    for m in range(MT):
                        for st in range(m + 1):
                            last = pe.matmul(bank(b, at + m * DH, DH), turned[:, j % 2 * 384 + (m + st) * P:j % 2 * 384 + (m + st + 1) * P],
                                             v_nat[:, br * 512 + st * T + h // 4 * DH:br * 512 + st * T + (h // 4 + 1) * DH],
                                             start=st == 0, stop=st == m)
                    if j % 4 == 3:
                        last.then_inc(S["av_made"], 1)
            pe.wait_ge(S["o_added"], 8)
            for g in range(4):
                for k in range(2):
                    for m in range(MT):
                        c = 2 * g + k
                        last = pe.transpose(bank(g, k * T + m * P, P), o_nat[:, m * 1024 + c * P:m * 1024 + (c + 1) * P],
                                            ident[:, :])
                last.then_inc(S["on_turned"], 1)
        if "s5" in run:
            def bring(c):
                pe.wait_ge(S["bn_made"], c + 1)
                if c:
                    pe.wait_ge(S["bt_copied"], 2 * c)
                    pe.wait_ge(S["cw_made"], c)
                else:
                    pe.wait_ge(S["on_copied"], 4)
                    pe.wait_ge(S["av_taken"], 8)
                for v in range(2):
                    for jj in range(4):
                        last = pe.transpose(bank(4 + v, jj * P, P), bn[:, v * 512 + jj * P:v * 512 + (jj + 1) * P], ident[:, :])
                for v in range(2):
                    last = pe.transpose(bank(6, v * P, P), cc[:, (v * 8 + c) * P:(v * 8 + c + 1) * P], ident[:, :])
                last.then_inc(S["bt_made"], 1)

            pe.wait_ge(S["s5_in"], 16 * N_S5)
            def drive(pr):
                c = pr // 2
                if pr % 2 == 0:
                    pe.wait_ge(S["bt_copied"], 2 * c + 2)
                if pr >= 2:
                    pe.wait_ge(S["scan_made"], pr - 1)
                for v in range(2):
                    for e in range(2):
                        jj = 2 * (pr % 2) + e
                        last = pe.matmul(bank(2 * (pr % 2) + v, e * T, T), bt[:, v * 512 + jj * P:v * 512 + (jj + 1) * P],
                                         chunk(pt2, c), start=True, stop=True)
                last.then_inc(S["bu_made"], 1)

            def read(pr):
                c = pr // 2
                if pr % 2 == 0:
                    pe.wait_ge(S["cw_made"], c + 1)
                    if c:
                        pe.wait_ge(S["y_sum"], c)
                pe.wait_ge(S["back_made"], pr + 1)
                for e in range(2):
                    jj = 2 * (pr % 2) + e
                    for x, wsel in enumerate((0, 1, 2, 2)):
                        a = (c % 2) * 1536 + wsel * 512 + jj * P
                        last = pe.matmul(bank(7, 0, T), cw[:, a:a + P],
                                         backs[pr % 2][:, x * 512 + e * T:x * 512 + (e + 1) * T],
                                         start=pr % 2 + e + x == 0, stop=pr % 2 + e == 2 and x == 3)
                last.then_inc(S["y_made"], 1)

            bring(0)
            drive(0)
            drive(1)
            bring(1)
            for pr in range(16):
                if pr < 14:
                    drive(pr + 2)
                read(pr)
                if pr % 2 and pr < 13:
                    bring((pr + 3) // 2)
        if "merge" in run:
            pe.wait_ge(S["on_lo"], 4)
            pe.wait_ge(S["y_lo"], 8)

            def merge(i, fresh):
                for u in range(4):
                    pe.wait_ge(split_made, plan["merge"][1] + u + 1 + i * 4)
                    if u == 0 and not fresh:
                        pe.wait_ge(S["mg_a"], i)
                    if u == 1 and not fresh:
                        pe.wait_ge(S["mg_b"], i)
                    if u == 2 and not fresh:
                        pe.wait_ge(S["mg_d"], i)
                    if u == 3 and not fresh:
                        pe.wait_ge(S["mg_sum"], i)
                    if u < 2:
                        last = tile_unit("merge", 4, i, u, bank(u, 0, T), waits=False)
                    elif u == 2:
                        tile_unit("merge", 4, i, u, bank(2, 0, T), ps_hi, ps_lo, n=8, waits=False, done=False)
                        tile_unit("merge", 4, i, u, bank(3, 0, T), ps_hi, ps_lo, n=8, w0=8 * P, waits=False)
                    else:
                        tile_unit("merge", 4, i, u, bank(4, 0, T), po_hi, po_lo, n=8, waits=False)
            merge(0, True)
            with pe.Fori(1, 16) as i:
                merge(i, False)
        if "out2" in run:
            pe.wait_ge(S["mixed_made"], 16)
            rows_phase("out2", 8, hid_hi, hid_lo)
        if "ffn2" in run:
            norm(4)
            ffn(2)

    block_scope.__exit__(None, None, None)
    ctx.close()
    return locals()


def constants():
    t = np.arange(T)
    angle = 2 * np.pi * np.outer(t, t) / T
    cos, sin = np.cos(angle) / 16, np.sin(angle) / 16
    mask = np.zeros((P, 4, T), np.float32)
    for d in range(2):
        for s in range(2):
            src = s * P + np.arange(P)[:, None]
            dead = src > t[None] if d == 0 else src < t[None]
            mask[:, 2 * d + s][dead] = NEG
    sel = np.zeros((4, 4, P), np.float32)
    for h in range(4):
        sel[h, h] = 1
    def onehot(dist):
        d = np.maximum(dist, 0)
        far = 16 + (np.log(np.maximum(d, 1).astype(np.float32) / np.float32(16)) / np.float32(math.log(64))
                    * np.float32(16)).astype(np.int32)
        bucket = np.where(d < 16, d, np.minimum(far, 31))
        oh = np.zeros((33, dist.size), np.float32)
        oh[np.where(dist >= 0, bucket, 32), np.arange(dist.size)] = 1
        return oh
    rows = np.arange(P)
    return {
        "k_oh_rev": onehot(255 - np.arange(384)),
        "k_oh_fwd": onehot(np.arange(512) - 255),
        "k_live": (rows >= 31).astype(np.float32)[:, None],
        "k_trow": np.tile(np.arange(T, dtype=np.float32), (P, 1)),
        "k_cmask": (rows[:, None] // 64 == np.arange(32)[None] // 16).astype(np.float32),
        "k_ident": np.eye(P, dtype=np.float32),
        "k_dft1": np.concatenate([cos, sin], 1).astype(np.float32),
        "k_dft2": np.concatenate([cos, -sin], 1).astype(np.float32),
        "k_mask": mask,
        "k_sel": sel.reshape(4, 4 * P),
    }


_NAMES = [
    "x", "c", "w_ada", "b_ada", "norm1_w", "w_in", "b_gates", "mlstm_norm_w", "w_out", "norm2_w", "w_up",
    "w_conv", "b_conv", "w_down", "norm_f_w", "ffn1_pre_g_2", "ffn1_w_gate_2", "ffn1_w_up_2",
    "ffn1_w_down_2", "ffn1_post_g_2", "mix_pre_g_2", "w_in_2", "ssm_a_re_2", "ssm_a_im_2", "ssm_log_dt_2",
    "ssm_b_re_2", "ssm_b_im_2", "ssm_c_re_2", "ssm_c_im_2", "ssm_d_2", "ssm_glu_w1_2", "ssm_glu_w2_2",
    "cmp_pos_2", "cmp_k_w1_2", "cmp_k_w2_2", "cmp_v_w1_2", "cmp_v_w2_2", "nsa_w_o_2", "w_out_2",
    "mix_post_g_2", "ffn2_pre_g_2", "ffn2_w_gate_2", "ffn2_w_up_2", "ffn2_w_down_2", "ffn2_post_g_2",
    "rel_bias_2",
]
_LAYERED = {
    "ffn1_w_gate_2", "ffn1_w_up_2", "ffn1_w_down_2", "w_in_2", "ssm_glu_w1_2", "ssm_glu_w2_2",
    "cmp_pos_2", "cmp_k_w1_2", "cmp_k_w2_2", "cmp_v_w1_2", "cmp_v_w2_2", "nsa_w_o_2", "w_out_2",
    "ffn2_w_gate_2", "ffn2_w_up_2", "ffn2_w_down_2", "ssm_b_re_2", "ssm_b_im_2", "ssm_c_re_2", "ssm_c_im_2",
}


def declare(nc, arrays):
    I = {}
    for name, a in arrays.items():
        I[name] = nc.dram_tensor(f"in_{name}", a.shape, mybir.dt.from_np(a.dtype), kind="ExternalInput").ap()
        if name in _LAYERED:
            I[name] = I[name][0]
    return I, nc.dram_tensor("out_x", (1, T, D), F32, kind="ExternalOutput").ap()


def kernel(**inputs):
    import concourse.bacc as bacc
    from concourse.bass_utils import run_bass_kernel_spmd

    arrays = {n: np.ascontiguousarray(inputs[n]) for n in _NAMES}
    arrays.update(constants())
    nc = bacc.Bacc("TRN2", target_bir_lowering=False, num_devices=1)
    build(nc, *declare(nc, arrays))
    r = run_bass_kernel_spmd(nc, [{f"in_{n}": a for n, a in arrays.items()}], core_ids=[0])
    return r.results[0]["out_x"]
```

```python
import math
from contextlib import ExitStack

import numpy as np
import concourse.bass as bass
from concourse import mybir

F32 = mybir.dt.float32
F32R = mybir.dt.float32r
ACT = mybir.ActivationFunctionType
ALU = mybir.AluOpType
AX = mybir.AxisListType
ds = bass.ds

P = 128
T = 256
MT = T // P
D = 2048
KC = D // P
FF = 5632
FC = FF // P
PARTS = ((0, 24), (24, 20))
EPS = 1e-6
UNIT = 2048
SLOTS = 4
HALF = 1024
HEADS1, DK, DV = 4, 128, 256
G_IN2 = 3584
GA_IN2 = G_IN2 + 48
GB_IN2 = GA_IN2 + D
NH, NKV, DH = 16, 4, 64
NCMP = 15
NEG = -1e30
ST = 32
TWO_PI = 2 * math.pi
ROUND = 1.5 * 2.0 ** 23


class Steps:

    def __init__(self, eng, sem):
        self.eng, self.sem, self.n = eng, sem, 0

    def then(self, ins):
        self.n += 1
        ins.then_inc(self.sem, 1)
        self.eng.wait_ge(self.sem, self.n)


def stream_plan():
    order = [("ada", 96, True), ("in_tiles", 16, True), ("in_rows", 16, True), ("out1", 16, True)]

    def ffn(n):
        for part, (_, chunks) in enumerate(PARTS):
            order.append((f"up{n}{part}", 2 * chunks, True))
            order.append((f"down{n}{part}", chunks, True))

    ffn(0)
    ffn(1)
    order += [("in2", 28, True), ("cmp", 4, False), ("merge", 64, True),
              ("out2", 16, True)]
    ffn(2)
    plan, unit, split, direct = {}, 0, 0, 0
    for name, n, is_split in order:
        plan[name] = (unit, split, direct, n)
        unit += n
        counts = 2 * n if name == "ada" else n
        split, direct = (split + counts, direct) if is_split else (split, direct + n)
    return plan


def build(nc, I, out):
    plan = stream_plan()
    ctx = ExitStack()

    def sem(name):
        return ctx.enter_context(nc.semaphore(name))

    base = 16512
    here = [base]

    def sb(name, cols, dt=F32, at=None, parts=P):
        at = here[0] if at is None else at
        t = nc.alloc_sbuf_tensor_at(name, [parts, cols], dt, offset=at)
        here[0] = max(here[0], at + (4 * cols + 31) // 32 * 32)
        return t

    stage = sb("stage", SLOTS * UNIT)
    w_hi = sb("w_hi", 2 * UNIT, F32R)
    w_lo = sb("w_lo", 2 * UNIT, F32R)
    xt_hi = sb("xt_hi", KC * T, F32R)
    xt_lo = sb("xt_lo", KC * T, F32R)
    x_nat = sb("x_nat", MT * D)
    OV = here[0]
    hid_hi = sb("hid_hi", 24 * T, F32R)
    hid_lo = sb("hid_lo", 24 * T, F32R)
    FN = here[0]
    f_nat = sb("f_nat", MT * D)
    RB = here[0]
    row = sb("row", D)
    ident = sb("ident", P)
    cols = sb("cols", 6 * P)
    mod = sb("mod", 96)
    scale_cols = sb("scale_cols", 2 * KC)
    csilu = sb("csilu", KC)
    bgate = sb("bgate", 4)
    stats = sb("stats", 32)
    TT = here[0]
    turn = sb("turn", 2 * 512)
    conv_a = sb("conv_a", 2 * T)
    conv_v = sb("conv_v", 2 * T)
    hval = sb("hval", 2 * T)
    MISC = here[0]

    projt = sb("projt", 16 * T, at=OV)
    v_one = sb("v_one", MT * HEADS1 * 257, at=OV + 16384)
    o_sig = sb("o_sig", MT * 1024, at=OV + 24640)
    dft1 = sb("dft1", 2 * 512, at=OV + 32832)
    dft2 = sb("dft2", 2 * 512, at=OV + 36928)
    four = sb("four", MT * 512, at=OV + 41024)
    rows1 = sb("rows1", 6 * T, at=FN + 12288, parts=4)
    pt1 = sb("pt1", 4 * T, at=OV + 32832)
    ex1 = [sb(f"ex{k}", 4 * T, at=OV + 36928 + 4096 * k) for k in range(2)]
    h_nat = sb("h_nat", MT * 1024, at=FN)
    mask1 = sb("mask1", 4 * T, at=FN + 8192)
    grow = sb("grow", 4 * T, at=FN, parts=4)
    lfrow = sb("lfrow", 2 * T, at=TT + 4096, parts=4)
    crow = sb("crow", 2 * T, at=TT + 6144, parts=4)
    WG = here[0]
    wg_raw = sb("wg_raw", KC * 48)
    wg_hi = sb("wg_hi", KC * 48, F32R, at=FN)
    wg_lo = sb("wg_lo", KC * 48, F32R, at=FN + 3072)
    g_nat = sb("g_nat", MT * 48)
    ecols = sb("ecols", 32)
    dcols = sb("dcols", 64)
    SEL = here[0]
    sel1 = sb("sel1", 4 * P, parts=4)
    ones1 = sb("ones1", T, parts=4)
    mod_row = sb("mod_row", 6 * D, at=OV, parts=64)
    rowtab = sb("rowtab", 6 * P, at=TT)
    pt2 = sb("pt2", 28 * T, at=OV)
    swp = sb("swp", 4 * T, at=OV + 28672)
    v_nat = sb("v_nat", 4 * T, at=OV + 32768)
    o_nat = sb("o_nat", MT * 1024, at=OV + 36864)
    raw_k = sb("raw_k", 16 * 60, at=OV + 36864)
    raw_v = sb("raw_v", 16 * 60, at=OV + 40960)
    soft = sb("soft", 2 * 384, at=OV + 45056)
    strips = sb("strips", NH * T, at=FN)
    ps_hi = sb("ps_hi", 8 * T, F32R, at=FN)
    ps_lo = sb("ps_lo", 8 * T, F32R, at=FN + 8192)
    sgates = sb("sgates", 5 * T, at=OV + 40960)
    po_hi = sb("po_hi", 8 * T, F32R, at=RB)
    po_lo = sb("po_lo", 8 * T, F32R, at=TT)
    turned = sb("turned", 2 * 384, at=TT)
    hid_n = sb("hid_n", 2 * T, at=TT + 4096, parts=60)
    hid_t = sb("hid_t", 2 * 120, at=TT + 6144)
    kc_t = sb("kc_t", 60)
    VC = here[0]
    vc_n = sb("vc_n", T, parts=15)
    w2 = sb("w2", 2 * P + P, at=SEL)
    cmp_s = sb("cmp_s", 2 * 240, at=RB)
    cmp_t = sb("cmp_t", 2 * 512, at=RB + 2048, parts=15)
    biasc = sb("biasc", 2 * 240, at=RB + 6144)
    oh_rev = sb("oh_rev", 384, at=TT, parts=33)
    oh_fwd = sb("oh_fwd", 512, at=TT + 1536, parts=33)
    rev_sb = sb("rev_sb", 384, at=TT + 3584, parts=16)
    relb = sb("relb", 16, parts=33)
    pos2 = sb("pos2", P, at=SEL + 1536, parts=32)
    pos_t = sb("pos_t", 32)
    live = sb("live", 1)
    sm = sb("sm", 256, at=SEL + 2048)
    S5 = OV + 8192
    bc = sb("bc", 2 * ST * 16, at=S5 + 8192)
    cc = sb("cc", 2 * 8 * P, at=base + 2 * UNIT * 4)
    bn = sb("bn", 2 * 512, at=S5 + 12288)
    bt = sb("bt", 2 * 512, at=S5 + 16384)
    cw = sb("cw", 2 * 3 * 512, at=S5 + 20480)
    ct = sb("ct", 4 * P, at=S5 + 32768)
    par = sb("par", 20 * ST, at=WG)
    trow = sb("trow", T, at=VC)
    cmask = sb("cmask", 32, at=WG + 80 * ST)
    WR = base + SLOTS * UNIT * 4
    trig = sb("trig", 2 * 512, at=WR)
    sine = sb("sine", 2 * 512, at=WR + 4096)
    cosine = sb("cosine", 2 * 512, at=WR + 8192)
    rot_r = sb("rot_r", 512, at=WR + 12288)
    rot_i = sb("rot_i", 512, at=WR + 14336)
    z_r = sb("z_r", 2 * 512, at=WR + 16384)
    z_i = sb("z_i", 2 * 512, at=WR + 20480)
    backs = [sb("back_even", 4 * 512, at=WR + 24576), sb("back_odd", 4 * 512, at=base + 3 * UNIT * 4)]
    assert here[0] <= nc.sbuf_usable_end, (here[0], nc.sbuf_usable_end)

    ps = ctx.enter_context(nc.psum_tensor("ps", [P, 8 * 512], F32))
    gates_dram = nc.dram_tensor("gates_scratch", [2, D], F32).ap()
    modrow_dram = nc.dram_tensor("modrow_scratch", [2, 6 * D], F32).ap()
    rev_dram = nc.dram_tensor("rev_scratch", [16, P, 384], F32).ap()

    landed = [sem(f"landed{s}") for s in range(SLOTS)]
    hi_made = sem("hi_made")
    split_made = sem("split_made")
    split_used = sem("split_used")
    direct_used = sem("direct_used")
    act_step = sem("act_step")
    dve_step = sem("dve_step")
    pool_step = sem("pool_step")

    names = """const_in tab_in tab_ready tab_turned cols_made c_in c_turned mod_made x_in
        ada_taken modrow_out modrow_in mod_turned crep_hi crep_made norm_ssq norm_var norm_std norm_xhat norm_rs piece_made norm_turned norm_scaled norm_hi norm_done
        tile_copied rows_taken wg_in wg_split_hi wg_split g_rows g_rows_copied g_made g_copied
        dft_in four1 four1_copied four2 four2_copied four2_hi mix_lo
        gt_made grow_made f_exp f_add f_ln rows_made ec_made ec_copied em_made
        bcast_made score_made arg_made exp_made pt_made num_made num_taken h_ssq h_var h_std h_done
        ym_turned ym_copied ym_hi row_in row_used gate_out mask_in
        pair_e1 pair_d1 pair_e2 pair_d2 pair_e3 hid_made conv_step x_made out_done
        q_scaled swapped vt_made vn_copied oh_in rev_made rev_copied rev_out strips_in biasc_made
        biasc_copied small_in pos_made pos_copied raw_made hn_gelu ht_made ht_copied kv_made
        kv_copied cs_made cs_max cs_exp cs_done ct_made ct_copied co_made co_copied sc_made sc_max sc_exp
        pt_turned pt_copied av_made av_taken o_added on_turned on_copied on_hi on_lo
        s5_in p_dt p_x p_mag p_phi p_sin bn_made bt_made bt_copied cw_made
        ang_made cos_made bu_made scan_made back_made y_made y_sum y_hi y_lo
        mg_half_hi mg_half_lo mg_a mg_b mg_2 mg_d mg_sum mg_hi mixed_made
        """.split()
    S = {n: sem(n) for n in names}
    dve_merge = sem("dve_merge")
    N_SMALL, N_S5 = 7, 8

    ffn_w = [
        dict(up=(I["w_up"], I["w_up"]), off=(0, FF), down=I["w_down"], conv=True),
        dict(up=(I["ffn1_w_gate_2"], I["ffn1_w_up_2"]), off=(0, 0), down=I["ffn1_w_down_2"], conv=False),
        dict(up=(I["ffn2_w_gate_2"], I["ffn2_w_up_2"]), off=(0, 0), down=I["ffn2_w_down_2"], conv=False),
    ]

    def bank(b, a=0, n=512, parts=P):
        return ps[0:parts, b * 512 + a:b * 512 + a + n]

    def chunk(t, k, m=None):
        return t[:, k * T:(k + 1) * T] if m is None else t[:, k * T + m * P:k * T + (m + 1) * P]

    def slot(s):
        return stage[:, s * UNIT:(s + 1) * UNIT]

    TABLE_ROWS = (128, 96, 120, 104, 120, 64)
    C_ADA, C_N1, C_N2 = 0, 96, 112
    C_CONV = (P, 2 * P, 3 * P)
    C_SD = P + 88
    C_F1, C_MP = 2 * P + 88, 2 * P + 104
    C_F2 = 3 * P + 88
    C_CB, C_ARE = 4 * P, 4 * P + 88
    C_AIM, C_LDT = 5 * P, 5 * P + 32

    ctx.enter_context(nc.allow_non_contiguous_dma(reason="small vectors are laid along the partitions"))
    block_scope = nc.Block()
    block = block_scope.__enter__()

    @block.sync
    def _(sp):
        def load(name, body_units, n_iter, fetch):
            first, split, direct, _ = plan[name]
            is_direct = name == "cmp"
            used, before = (direct_used, direct) if is_direct else (split_made, split)

            def body(i, fresh):
                for u in range(body_units):
                    moves = fetch(i, u)
                    if u >= SLOTS or not fresh:
                        step = 2 if name == "ada" else 1
                        sp.wait_ge(used, before + (i * body_units + u - SLOTS + 1) * step)
                    if name == "merge" and fresh and u == 2:
                        sp.wait_ge(S["bt_made"], 8)
                    if name == "merge" and fresh and u == 3:
                        sp.wait_ge(S["y_made"], 16)
                    for dst, src in moves:
                        sp.dma_start(dst, src).then_inc(landed[u % SLOTS], 16)

            kind_before = {"cmp": (split_made, plan["cmp"][1]), "merge": (direct_used, 4)}
            if name in kind_before:
                sp.wait_ge(*kind_before[name])
            if name == "ada" or name in kind_before:
                body(0, True)
                start = 1
            else:
                start = 0
            if n_iter - start == 1:
                body(start, False)
            elif n_iter > start:
                with sp.Fori(start, n_iter) as i:
                    body(i, False)

        def tiles(w, off=0):
            view = w.rearrange("(k p) n -> p k n", p=P)
            return lambda i, u: [(slot(u % SLOTS).rearrange("p (k n) -> p k n", n=P),
                                  view[:, :, ds(i * 4 * P + (off + u * P), P)])]

        def rows(w, r0, per_half, off=0):
            view = w[r0:r0 + 2 * P * per_half, :].rearrange("(c k p) n -> c p k n", p=P, k=2)
            return lambda i, u: [(slot(u % SLOTS).rearrange("p (k n) -> p k n", k=2),
                                  view[u % per_half][:, :, ds(i * HALF + (off + u // per_half * HALF), HALF)])]

        def pairs(ws, offs, f0):
            views = [w.rearrange("(k p) n -> p k n", p=P) for w in ws]
            return lambda i, u: [(slot(u % SLOTS).rearrange("p (k n) -> p k n", n=P),
                                  views[u % 2][:, :, ds(i * 2 * P + (offs[u % 2] + (f0 + u // 2) * P), P)])]

        def load_ffn(n):
            f = ffn_w[n]
            for part, (f0, chunks) in enumerate(PARTS):
                load(f"up{n}{part}", 4, chunks // 2, pairs(f["up"], f["off"], f0))
                per_half = chunks // 2
                if per_half % SLOTS == 0:
                    load(f"down{n}{part}", per_half, 2, rows(f["down"], f0 * P, per_half))
                else:
                    load(f"down{n}{part}", 2 * per_half, 1, rows(f["down"], f0 * P, per_half))

        view = I["w_ada"].rearrange("(c k p) n -> c p k n", p=P, k=2)
        load("ada", 16, 6, lambda i, u: [(slot(u % SLOTS).rearrange("p (k n) -> p k n", k=2),
                                          view[u % 8][:, :, ds(i * 2 * HALF + u // 8 * HALF, HALF)])])
        load("in_tiles", 4, 4, tiles(I["w_in"]))
        load("in_rows", 8, 2, rows(I["w_in"], 0, 8, off=2048))
        load("out1", 8, 2, rows(I["w_out"], 0, 8))
        load_ffn(0)
        load_ffn(1)
        load("in2", 4, 7, tiles(I["w_in_2"]))
        def fetch_cmp(i, u):
            w = I["cmp_k_w1_2"] if u < 2 else I["cmp_v_w1_2"]
            view = w.rearrange("(h k p) n -> h p k n", p=P, k=8)
            return [(slot(u).rearrange("p (k n) -> p k n", n=256), view[u % 2])]
        load("cmp", 4, 1, fetch_cmp)
        in2 = I["w_in_2"].rearrange("(k p) n -> p k n", p=P)
        halves = [I[n].rearrange("(k p) n -> p k n", p=P) for n in ("ssm_glu_w1_2", "ssm_glu_w2_2", "nsa_w_o_2")]

        def fetch_merge(i, u):
            to = slot(u).rearrange("p (k n) -> p k n", n=P)
            if u < 2:
                return [(to, in2[:, :, ds(i * P + (GA_IN2, GB_IN2)[u], P)])]
            at = i * P if isinstance(i, int) else (i + 1) * P - P
            if u == 2:
                return [(to[:, 8 * v:8 * v + 8], halves[v][:, :, ds(at, P)]) for v in range(2)]
            return [(to[:, 0:8], halves[2][:, :, ds(at, P)])]
        load("merge", 4, 16, fetch_merge)
        load("out2", 8, 2, rows(I["w_out_2"], 0, 8))
        load_ffn(2)
        sp.wait_ge(S["x_made"], 6)
        sp.dma_start(out.rearrange("b (m p) d -> p (b m) d", p=P),
                     x_nat[:, :].rearrange("p (m d) -> p m d", m=MT)).then_inc(S["out_done"], 16)
        sp.wait_ge(S["out_done"], 16)

    @block.gpsimd
    def _(pool):
        link = Steps(pool, pool_step)
        link.then(pool.memset(ones1[:, :], 1.0))
        link.then(pool.memset(relb[32:33, :], NEG))
        tab = rowtab[:, :].rearrange("q (t p) -> q t p", p=P)

        def vec(name):
            return I[name].rearrange("(q p) -> q p", p=P)

        conv = I["w_conv"].rearrange("t (q p) -> t q p", p=P)
        loads = [
            (tab[0:96, 0, :], vec("b_ada")), (tab[96:112, 0, :], vec("norm1_w")),
            (tab[112:128, 0, :], vec("norm2_w")),
            (tab[0:88, 1, :], conv[0]), (tab[88:96, 1, :], I["ssm_d_2"].rearrange("b (q p) -> (b q) p", p=P)),
            (tab[0:88, 2, :], conv[1]), (tab[88:104, 2, :], I["ffn1_pre_g_2"].rearrange("b (q p) -> (b q) p", p=P)),
            (tab[104:120, 2, :], I["mix_pre_g_2"].rearrange("b (q p) -> (b q) p", p=P)),
            (tab[0:88, 3, :], conv[2]), (tab[88:104, 3, :], I["ffn2_pre_g_2"].rearrange("b (q p) -> (b q) p", p=P)),
            (tab[0:88, 4, :], vec("b_conv")),
            (tab[88:120, 4, :], I["ssm_a_re_2"].rearrange("b (q g) p -> (b q) (g p)", g=2)),
            (tab[0:32, 5, :], I["ssm_a_im_2"].rearrange("b (q g) p -> (b q) (g p)", g=2)),
        ]
        for dst, src in loads:
            pool.dma_start(dst, src).then_inc(S["tab_in"], 16)
        pool.dma_start(hval[32:64, 0:2], I["ssm_log_dt_2"].rearrange("b (q g) -> (b q) g", g=2)).then_inc(S["tab_in"], 16)
        pool.wait_ge(S["tab_in"], 16 * (len(loads) + 1))
        for g in range(2):
            last = pool.tensor_copy(tab[32:64, 5, 64 * g:64 * g + 64],
                                    hval[32:64, g:g + 1].to_broadcast([32, 64]))
        last.then_inc(S["tab_ready"], 1)
        pool.dma_start(x_nat[:, :].rearrange("p (m d) -> p m d", m=MT),
                       I["x"].rearrange("b (m p) d -> p (b m) d", p=P)).then_inc(S["x_in"], 16)
        pool.dma_start(bgate[0:4, :], I["b_gates"].rearrange("(k h) -> h k", h=4)).then_inc(S["const_in"], 16)
        pool.dma_start(sel1[:, :], I["k_sel"]).then_inc(S["const_in"], 16)
        wgv = wg_raw[:, :].rearrange("p (k n) -> p k n", n=48)
        pool.dma_start(wgv[:, :, 0:16], I["w_in"].rearrange("(k p) n -> p k n", p=P)[:, :, 4096:4112]).then_inc(S["wg_in"], 16)
        pool.wait_ge(S["ada_taken"], 14)
        for v in range(2):
            pool.dma_start(modrow_dram[v:v + 1], mod_row[32 * v:32 * v + 1, :]).then_inc(S["modrow_out"], 16)
        pool.wait_ge(S["modrow_out"], 32)
        for v, t in enumerate((conv_a, conv_v)):
            pool.dma_start(t[0:96, 0:P], modrow_dram[v].rearrange("(q p) -> q p", p=P)).then_inc(S["modrow_in"], 16)
        for dst, src in ((dft1, "k_dft1"), (dft2, "k_dft2")):
            pool.dma_start(dst[:, :].rearrange("p (k n) -> p k n", n=512),
                           I[src].rearrange("(k p) n -> p k n", p=P)).then_inc(S["dft_in"], 16)
        pool.wait_ge(S["mod_made"], 1)
        pool.dma_start(gates_dram[0].rearrange("(k p) -> p k", p=P), mod[:, 32:48]).then_inc(S["gate_out"], 16)
        pool.dma_start(gates_dram[1].rearrange("(k p) -> p k", p=P), mod[:, 80:96]).then_inc(S["gate_out"], 16)
        pool.wait_ge(S["gate_out"], 32)

        rows_in = [0]

        def spread_row(src, at=0):
            if rows_in[0]:
                pool.wait_ge(S["row_used"], rows_in[0])
            rows_in[0] += 1
            pool.dma_start(row[:, at:D], src.partition_broadcast(P)).then_inc(S["row_in"], 16)

        pool.wait_ge(S["g_made"], 1)
        pool.dma_start(mask1[:, :].rearrange("p (k n) -> p k n", n=T), I["k_mask"]).then_inc(S["mask_in"], 16)
        spread_row(I["mlstm_norm_w"], D - 1024)
        spread_row(gates_dram[0])
        spread_row(gates_dram[1])
        spread_row(I["norm_f_w"])
        spread_row(I["ffn1_post_g_2"][0])
        pool.wait_ge(S["g_copied"], 1)
        pool.dma_start(wgv, I["w_in_2"].rearrange("(k p) n -> p k n", p=P)[:, :, G_IN2:G_IN2 + 48]).then_inc(S["wg_in"], 16)
        pool.wait_ge(S["num_taken"], 4)
        pool.wait_ge(S["rows_made"], 1)
        for c in range(2):
            for k in range(2):
                pool.dma_start(w2[:, c * P + k * DH:c * P + (k + 1) * DH], I["cmp_k_w2_2"][c * P:(c + 1) * P, :]).then_inc(S["small_in"], 16)
        pool.dma_start(w2[:, 2 * P:3 * P].rearrange("p (c n) -> p c n", n=DH),
                       I["cmp_v_w2_2"].rearrange("(c p) n -> p c n", p=P)).then_inc(S["small_in"], 16)
        for k in range(2):
            pool.dma_start(pos2[:, k * DH:(k + 1) * DH], I["cmp_pos_2"]).then_inc(S["small_in"], 16)
        pool.wait_ge(S["norm_done"], 32)
        pool.dma_start(oh_rev[:, :], I["k_oh_rev"]).then_inc(S["oh_in"], 16)
        pool.dma_start(oh_fwd[:, :], I["k_oh_fwd"]).then_inc(S["oh_in"], 16)
        pool.dma_start(relb[0:32, :], I["rel_bias_2"]).then_inc(S["oh_in"], 16)
        pool.dma_start(live[:, :], I["k_live"]).then_inc(S["oh_in"], 16)
        pool.wait_ge(S["rev_copied"], 1)
        pool.dma_start(rev_dram, rev_sb[:, :].unsqueeze(1).to_broadcast([16, P, 384])).then_inc(S["rev_out"], 16)
        pool.wait_ge(S["rev_out"], 16)
        pool.wait_ge(S["g_made"], 2)
        pool.dma_start(strips[:, :].rearrange("p (h x) -> p h x", h=NH),
                       bass.AP(rev_dram.tensor, 127, [[383, P], [P * 384, NH], [1, T]])).then_inc(S["strips_in"], 16)
        pool.wait_ge(S["raw_made"], 2)
        for v, n in enumerate(("ssm_b_re_2", "ssm_b_im_2")):
            pool.dma_start(bc[:, v * 512:(v + 1) * 512].rearrange("p (j c) -> p j c", c=16),
                           I[n].rearrange("(j g) p c -> (g p) j c", g=2)).then_inc(S["s5_in"], 16)
        pool.wait_ge(direct_used, 3)
        for v, n in enumerate(("ssm_c_re_2", "ssm_c_im_2")):
            for k in range(2):
                pool.dma_start(cc[:, v * 1024:(v + 1) * 1024].rearrange("p (c k n) -> p c k n", k=2, n=64)[:, :, k],
                               I[n].rearrange("(c g) h p -> (g h) c p", c=8)).then_inc(S["s5_in"], 16)
        pool.wait_ge(S["wg_split"], 2)
        pool.wait_ge(S["co_made"], 4)
        pool.dma_start(trow[:, :], I["k_trow"]).then_inc(S["s5_in"], 16)
        pool.dma_start(cmask[:, :], I["k_cmask"]).then_inc(S["s5_in"], 16)
        pool.wait_ge(S["on_turned"], 4)
        pool.wait_ge(S["av_made"], 8)
        link.then(pool.memset(bn[:, :], 0.0))
        pool.wait_ge(S["s5_in"], 16 * N_S5)

        def spread_b(c):
            if c:
                pool.wait_ge(S["bt_made"], c)
            for v in range(2):
                for jj in range(4):
                    for g in range(2):
                        at = v * 512 + jj * P + 32 * jj + 16 * g
                        last = pool.tensor_copy(bn[64 * g:64 * g + 64, at:at + 16],
                                                bc[64 * g:64 * g + 64, v * 512 + (4 * c + jj) * 16:v * 512 + (4 * c + jj + 1) * 16])
            last.then_inc(S["bn_made"], 1)
            pool.wait_ge(S["bn_made"], c + 1)

        spread_b(0)
        for pr in range(16):
            at = slice(pr % 2 * 512, (pr % 2 + 1) * 512)
            pool.wait_ge(S["scan_made"], pr + 1)
            if pr >= 2:
                pool.wait_ge(S["y_made"], pr - 1)
            for k, (w, z) in enumerate(((cosine, z_r), (sine, z_i), (cosine, z_i), (sine, z_r))):
                last = pool.tensor_tensor(backs[pr % 2][:, k * 512:(k + 1) * 512], w[:, at], z[:, at], ALU.mult)
            last.then_inc(S["back_made"], 1)
            if pr % 2 == 0 and pr < 14:
                pool.wait_ge(S["back_made"], pr + 1)
                spread_b(pr // 2 + 1)
        pool.wait_ge(split_used, plan["merge"][1] + 66)
        spread_row(I["mix_post_g_2"][0])
        spread_row(I["ffn2_post_g_2"][0])


    rows_index = {n: r for r, n in enumerate(["in_rows", "out1", "down00", "down01", "down10", "down11",
                                              "out2", "down20", "down21"])}

    def rows_cols(half, m, n=0, width=HALF, swapped=False):
        at = m * HALF + n * 512
        return ps[:, ds(2048 - half * 2048 + at if swapped else half * 2048 + at, width)]

    def turn_bank(n, g):
        return 4 + g % 4 if n else g

    PAIR_BANK = (0, 4)

    def up_body_order(i, split, s2, s3, s1):
        static = isinstance(i, int) and i == 0
        split(0)
        if not static:
            s2(2 * i - 2, 0)
        split(1)
        if not static:
            s3(2 * i - 2, 0)
            s1(2 * i - 1, 1)
        split(2)
        if not static:
            s2(2 * i - 1, 1)
        split(3)
        if not static:
            s3(2 * i - 1, 1)
        s1(2 * i, 0)

    def nothing(*_):
        pass

    def up_phase(eng, split, s2, s3, s1, chunks, split_down, pending=nothing, norm_rest=nothing):
        def first_split(u):
            split(0, u)
            if u == 0:
                norm_rest()
            if u == 1:
                pending()
        up_body_order(0, first_split, s2, s3, s1)
        with eng.Fori(1, chunks // 2) as i:
            up_body_order(i, lambda u: split(i, u), s2, s3, s1)
        last = chunks - 2
        s2(last, 0)
        s3(last, 0)
        split_down(0)
        s1(last + 1, 1)
        split_down(1)
        s2(last + 1, 1)
        s3(last + 1, 1)

    PIECES = (2, 4, 4, 2, 4, 2, 4, 2, 4)

    def pieces_before(e):
        return sum(PIECES[:e])
    NORM_OF = (1, 2, 4)
    NUM = (0, 1, 6, 7)

    def take4(dve, link, q):
        br, h0 = q // 4, q % 4 * 4
        dve.wait_ge(S["av_made"], q + 1)
        rs = sm[:, 128 + 8 * q:136 + 8 * q]
        link.then(dve.reciprocal(rs, rs))
        gate = g_nat[:, :].rearrange("p (m h b) -> p h m b", h=NH, b=3)[:, h0:h0 + 4, :, 1 + br]
        link.then(dve.tensor_tensor(rs.rearrange("p (h m) -> p h m", m=2), rs.rearrange("p (h m) -> p h m", m=2),
                                    gate, ALU.mult))
        part = hval[:, :].rearrange("p (x d) -> p x d", d=DH)
        dve.tensor_tensor(part, bank(4 + q % 2).rearrange("p (x d) -> p x d", d=DH),
                          rs.unsqueeze(2).to_broadcast([P, 8, DH]), ALU.mult).then_inc(S["av_taken"], 1)
        dve.wait_ge(S["av_taken"], q + 1)
        dst = o_nat[:, :].rearrange("p (m h d) -> p h m d", m=2, d=DH)[:, h0:h0 + 4]
        dve.tensor_tensor(dst, dst, hval[:, :].rearrange("p (h m d) -> p h m d", m=2, d=DH), ALU.add).then_inc(S["o_added"], 1)
        dve.wait_ge(S["o_added"], q + 1)

    def half_done(eng, name, half):
        eng.wait_ge(split_used, plan[name][1] + plan[name][3] // 2 * (half + 1) + 2)

    def head_squares(act, h):
        act.wait_ge(S["num_taken"], h + 1)
        for m in range(MT):
            if h + m:
                act.wait_ge(S["h_ssq"], 2 * h + m)
            act.activation(turn[:, 0:256], h_nat[:, m * 1024 + h * 256:m * 1024 + (h + 1) * 256], ACT.Square,
                           accum_out=stats[:, 8 + m * 4 + h:9 + m * 4 + h]).then_inc(S["h_ssq"], 1)

    def gates(pe, n, turn_index):
        for k in range(KC):
            wh, wl = (w[:, k * n:(k + 1) * n] for w in (wg_hi, wg_lo))
            pe.matmul(bank(0, 0, T, n), wh, chunk(xt_hi, k), start=k == 0, stop=False)
            pe.matmul(bank(0, 0, T, n), wh, chunk(xt_lo, k), start=False, stop=False)
            last = pe.matmul(bank(0, 0, T, n), wl, chunk(xt_hi, k), start=False, stop=k == KC - 1)
        last.then_inc(S["g_rows"], 1)
        pe.wait_ge(S["g_rows_copied"], turn_index + 1)
        for m in range(MT):
            last = pe.transpose(bank(0, T + m * n, n), hval[0:n, m * P:(m + 1) * P], ident[0:n, 0:n])
        last.then_inc(S["g_made"], 1)

    def copy_gate_rows(dve, n, turn_index):
        dve.wait_ge(S["g_rows"], turn_index + 1)
        dve.tensor_copy(hval[0:n, 0:T], bank(0, 0, T, n)).then_inc(S["g_rows_copied"], 1)

    @block.scalar
    def _(act):
        link = Steps(act, act_step)
        act.sem_inc(S["ada_taken"], 2)
        act.sem_inc(S["tile_copied"], 4)

        def split(name, per_body, i, u):
            first, before, _, _ = plan[name]
            loads = 2 if name == "merge" and u == 2 else 1
            earlier = first // SLOTS
            if first > plan["merge"][0] and u % SLOTS == 2:
                earlier += 16
            act.wait_ge(landed[u % SLOTS], (earlier + loads * (u // SLOTS + 1 + i * (per_body // SLOTS))) * 16)
            act.wait_ge(split_used, before + u + 1 + i * per_body)
            n = HALF if name == "merge" and u == 3 else UNIT
            if name == "merge" and u == 0:
                act.activation(w_hi[:, 0:HALF], stage[:, 0:HALF], ACT.Copy).then_inc(S["mg_half_hi"], 1)
                act.activation(w_hi[:, HALF:UNIT], stage[:, HALF:UNIT], ACT.Copy).then_inc(hi_made, 1)
                return
            act.activation(w_hi[:, u % 2 * UNIT:u % 2 * UNIT + n], stage[:, u % SLOTS * UNIT:u % SLOTS * UNIT + n],
                           ACT.Copy).then_inc(hi_made, 1)

        def squares(e, src, k):
            n = pieces_before(e) + k
            if e:
                act.wait_ge(S["piece_made"], n - 1)
            if n:
                act.wait_ge(S["norm_ssq"], n)
            if PIECES[e] == 4:
                half, m = divmod(k, 2)
                part, to = src[:, m * D + half * HALF:m * D + (half + 1) * HALF], ps[:, 0:HALF]
            else:
                part, to = src[:, k * D:(k + 1) * D], ps[:, 2048:4096]
            act.activation(to, part, ACT.Square, accum_out=stats[:, k:k + 1]).then_inc(S["norm_ssq"], 1)

        def root(e):
            act.wait_ge(S["norm_var"], e + 1)
            act.activation(stats[:, 6:8], stats[:, 4:6], ACT.Sqrt).then_inc(S["norm_std"], 1)

        def square_sum(e, src, first=0):
            for k in range(first, PIECES[e]):
                squares(e, src, k)
            root(e)

        def second_tile(n, e):
            act.wait_ge(S["norm_rs"], e + 1)
            act.activation(f_nat[:, D:2 * D], x_nat[:, D:2 * D], ACT.Copy, scale=stats[:, 9:10]).then_inc(S["norm_xhat"], 1)

        def norm_begin(e, n, first=0):
            square_sum(e, x_nat, first)
            second_tile(n, e)

        def norm_split(n):
            for g in range(8):
                act.wait_ge(S["norm_scaled"], 8 * n + g + 1)
                act.activation(xt_hi[:, g * 512:(g + 1) * 512], turn[:, g % 2 * 512:(g % 2 + 1) * 512],
                               ACT.Copy).then_inc(S["norm_hi"], 1)

        def ffn(n, e_post):
            conv = ffn_w[n]["conv"]
            for part, (f0, chunks) in enumerate(PARTS):
                name, q0 = f"up{n}{part}", n * FC + f0
                before, pb = plan[name][1], PAIR_BANK[part]

                def split_down(u):
                    split(f"down{n}{part}", chunks, 0, u)

                def e1(j, s):
                    act.wait_ge(split_used, 2 * j + (before + 4))
                    if conv:
                        act.activation(conv_a[:, s * T:(s + 1) * T], bank(pb + s, 0, T), ACT.Identity,
                                       scale=cols[:, ds(j + (C_CONV[1] + f0), 1)],
                                       bias=cols[:, ds(j + (C_CB + f0), 1)])
                        act.activation(conv_v[:, s * T:(s + 1) * T], bank(pb + s, T, T), ACT.Identity,
                                       scale=cols[:, ds(j + (C_CONV[1] + FC + f0), 1)],
                                       bias=cols[:, ds(j + (C_CB + FC + f0), 1)]).then_inc(S["pair_e1"], 1)
                    else:
                        act.activation(conv_a[:, s * T:(s + 1) * T], bank(pb + s, 0, T),
                                       ACT.Silu).then_inc(S["pair_e1"], 1)

                def e2(j, s):
                    act.wait_ge(S["pair_d1"], j + (q0 + 3))
                    act.activation(conv_a[:, s * T:(s + 1) * T], conv_a[:, s * T:(s + 1) * T],
                                   ACT.Silu).then_inc(S["pair_e2"], 1)

                def e3(j, s):
                    if conv:
                        act.wait_ge(S["pair_d2"], j + (q0 + 1))
                    else:
                        act.wait_ge(S["pair_d1"], j + (q0 + 3))
                    act.activation(hid_hi[:, ds(j * T, T)], hval[:, s * T:(s + 1) * T],
                                   ACT.Copy).then_inc(S["pair_e3"], 1)

                up_phase(act, lambda i, u: split(name, 4, i, u), e2 if conv else e3,
                         e3 if conv else nothing, e1, chunks, split_down,
                         norm_rest=(lambda: norm_split(NORM_OF[n])) if part == 0 else nothing)
                for u in range(2, chunks):
                    split_down(u)
                    if part and u == chunks // 2 + (3 if n else 7):
                        squares(e_post, x_nat if n == 0 else f_nat, 0)
                        squares(e_post, x_nat if n == 0 else f_nat, 1)

        act.dma_start(conv_a[0:16, 0:P], I["c"].rearrange("b (q p) -> (b q) p", p=P)).then_inc(S["c_in"], 16)
        act.dma_start(ident[:, :], I["k_ident"]).then_inc(S["c_in"], 16)
        act.wait_ge(S["c_turned"], 1)
        link.then(act.activation(csilu[:, :], bank(4, 0, KC), ACT.Silu))
        crep = xt_hi[:, :].rearrange("p (k n) -> p k n", n=T)
        act.activation(crep[:, :, 0:32], csilu[:, :].unsqueeze(2).to_broadcast([P, KC, 32]),
                       ACT.Copy).then_inc(S["crep_hi"], 1)

        def take_ada(b, h):
            act.wait_ge(split_used, 16 * b + 18)
            act.activation(mod_row[0:64, ds(b * HALF, HALF)], ps[0:64, h * HALF:(h + 1) * HALF],
                           ACT.Copy).then_inc(S["ada_taken"], 1)

        def ada(i):
            for u in range(16):
                act.wait_ge(landed[u % SLOTS], (u // SLOTS + 1 + i * (16 // SLOTS)) * 16)
                for s in range(2):
                    used = 32 * i + (2 * u + s - 1)
                    if not isinstance(i, int) or used > 0:
                        act.wait_ge(split_used, used)
                    at = slice(u % 2 * UNIT + s * HALF, u % 2 * UNIT + (s + 1) * HALF)
                    act.activation(w_hi[:, at], stage[:, u % SLOTS * UNIT + s * HALF:u % SLOTS * UNIT + (s + 1) * HALF],
                                   ACT.Copy).then_inc(hi_made, 1)
                if u == 1 and not isinstance(i, int):
                    take_ada(2 * i - 1, 1)
                if u == 9:
                    take_ada(2 * i, 0)
        ada(0)
        act.wait_ge(S["x_in"], 16)
        square_sum(0, x_nat)
        second_tile(0, 0)
        with act.Fori(1, 6) as i:
            ada(i)
        take_ada(11, 1)
        split("in_tiles", 4, 0, 0)
        norm_split(0)
        def copy_tile(i, s):
            act.activation(projt[:, ds(i * 4 * T + s * T, T)], bank(s, 0, T),
                           ACT.Copy).then_inc(S["tile_copied"], 1)

        split("in_tiles", 4, 0, 1)
        split("in_tiles", 4, 0, 2)
        copy_tile(0, 0)
        split("in_tiles", 4, 0, 3)
        copy_tile(0, 1)
        with act.Fori(1, 4) as i:
            for u in range(4):
                split("in_tiles", 4, i, u)
                if u < 2:
                    copy_tile(i - 1, u + 2)
                else:
                    copy_tile(i, u - 2)
        for u in range(2):
            split("in_rows", 16, 0, u)
            copy_tile(3, u + 2)
        for u in range(2, 16):
            split("in_rows", 16, 0, u)
            if u == 9:
                half_done(act, "in_rows", 0)
                for m in range(MT):
                    dst = v_one[:, m * 1028:(m + 1) * 1028].rearrange("p (h n) -> p h n", n=257)
                    last = act.activation(dst[:, :, 0:256], rows_cols(0, m).rearrange("p (h n) -> p h n", n=256),
                                   ACT.Copy)
                last.then_inc(S["rows_taken"], 1)
        act.wait_ge(S["wg_in"], 16)
        act.wait_ge(S["norm_turned"], 8)
        act.activation(wg_hi[:, 0:KC * 16].rearrange("p (k n) -> p k n", n=16),
                       wg_raw[:, :].rearrange("p (k n) -> p k n", n=48)[:, :, 0:16],
                       ACT.Copy).then_inc(S["wg_split_hi"], 1)
        half_done(act, "in_rows", 1)
        for m in range(MT):
            last = act.activation(o_sig[:, m * 1024:(m + 1) * 1024], rows_cols(1, m),
                           ACT.Sigmoid)
        last.then_inc(S["rows_taken"], 1)
        act.wait_ge(S["grow_made"], 1)
        link.then(act.activation(crow[:, :].rearrange("h (d t) -> h d t", d=2),
                                 grow[:, :].rearrange("h (d k t) -> h k d t", d=2, k=2)[:, 1], ACT.Abs))
        act.activation(crow[:, :], crow[:, :], ACT.Exp, scale=-1.0).then_inc(S["f_exp"], 1)
        act.wait_ge(S["f_add"], 1)
        act.activation(crow[:, :], crow[:, :], ACT.Ln).then_inc(S["f_ln"], 1)
        for g in range(4):
            act.wait_ge(S["four1"], g + 1)
            if g:
                act.wait_ge(S["four2"], g)
            for m in range(MT):
                act.activation(four[:, m * 512:(m + 1) * 512], bank(2 * (g % 2) + m),
                               ACT.Copy).then_inc(S["four1_copied"], 1)
            act.wait_ge(S["four2_copied"], g + 1)
            act.activation(xt_hi[:, g * 512:(g + 1) * 512], turn[:, g % 2 * 512:(g % 2 + 1) * 512],
                           ACT.Copy).then_inc(S["four2_hi"], 1)
        act.wait_ge(S["ec_copied"], 1)
        act.activation(ecols[:, 16:32], ecols[:, 16:32], ACT.Exp, scale=-1.0).then_inc(S["em_made"], 1)
        for h in range(HEADS1):
            act.wait_ge(S["arg_made"], h + 1)
            act.activation(ex1[h % 2][:, :], ex1[h % 2][:, :], ACT.Exp).then_inc(S["exp_made"], 1)
            if h:
                head_squares(act, h - 1)
            if h >= 2:
                split("out1", 16, 0, h - 2)
        head_squares(act, HEADS1 - 1)
        act.wait_ge(S["h_var"], 1)
        act.activation(stats[:, 16:24], stats[:, 8:16], ACT.Sqrt).then_inc(S["h_std"], 1)
        split("out1", 16, 0, 2)
        for g in range(4):
            if g == 2:
                split("out1", 16, 0, 3)
            act.wait_ge(S["ym_copied"], g + 1)
            act.activation(xt_hi[:, (4 + g) * 512:(5 + g) * 512], turn[:, g % 2 * 512:(g % 2 + 1) * 512],
                           ACT.Copy).then_inc(S["ym_hi"], 1)
        for u in range(4, 16):
            split("out1", 16, 0, u)
            if u == 12:
                squares(1, x_nat, 0)
                squares(1, x_nat, 1)
        norm_begin(1, 1, 2)
        ffn(0, 2)
        square_sum(2, x_nat, 2)
        norm_begin(3, 2)
        ffn(1, 4)
        square_sum(4, f_nat, 2)
        norm_begin(5, 3)

        def copy_tile2(i, s):
            act.activation(pt2[:, ds(i * 4 * T + s * T, T)], bank(s, 0, T),
                           ACT.Copy).then_inc(S["tile_copied"], 1)

        for u in range(4):
            split("in2", 4, 0, u)
            if u == 0:
                norm_split(3)
            if u >= 2:
                copy_tile2(0, u - 2)
        with act.Fori(1, 7) as i:
            for u in range(4):
                split("in2", 4, i, u)
                copy_tile2(i - 1 if u < 2 else i, (u + 2) % 4)
        for u in range(2):
            act.wait_ge(split_used, plan["in2"][1] + 29 + u)
            copy_tile2(6, u + 2)
        act.wait_ge(S["wg_in"], 32)
        act.activation(wg_hi[:, :], wg_raw[:, :], ACT.Copy).then_inc(S["wg_split_hi"], 1)
        act.wait_ge(S["g_made"], 2)
        act.activation(g_nat[:, :], bank(0, T, 96), ACT.Sigmoid).then_inc(S["g_copied"], 1)
        act.wait_ge(S["vt_made"], 1)
        for br in range(2):
            act.activation(v_nat[:, br * 512:(br + 1) * 512], bank(1 + br), ACT.Copy).then_inc(S["vn_copied"], 1)
        act.wait_ge(S["rev_out"], 16)
        for x in range(2):
            act.wait_ge(direct_used, 2 * x + 2)
            act.activation(hid_n[:, x * T:(x + 1) * T], bank(6 + x, 0, T, 60),
                           ACT.Gelu_apprx_tanh).then_inc(S["hn_gelu"], 1)
        for m in range(MT):
            act.wait_ge(S["cs_max"], m + 1)
            act.activation(cmp_s[:, m * 240:(m + 1) * 240], cmp_s[:, m * 240:(m + 1) * 240],
                           ACT.Exp).then_inc(S["cs_exp"], 1)
        for x in range(8):
            act.wait_ge(S["ct_made"], x + 1)
            act.activation(cmp_t[:, x % 2 * 512:(x % 2 + 1) * 512], bank(x % 2, 0, 512, 15),
                           ACT.Copy).then_inc(S["ct_copied"], 1)
        act.wait_ge(S["wg_split"], 2)
        pc = lambda i: par[:, i * ST:(i + 1) * ST]
        act.activation(pc(0), cols[:, C_LDT:C_LDT + ST], ACT.Exp).then_inc(S["p_dt"], 1)
        act.wait_ge(S["p_x"], 1)
        act.activation(pc(4), pc(2), ACT.Exp).then_inc(S["p_mag"], 1)
        act.wait_ge(S["p_phi"], 1)
        act.activation(pc(6), pc(5), ACT.Sin, scale=6.283185)
        link.then(act.activation(pc(7), pc(5), ACT.Sin, scale=3.1415925))
        act.activation(pc(7), pc(7), ACT.Square, scale=math.sqrt(2)).then_inc(S["p_sin"], 1)

        def waves(pr):
            at = slice(pr % 2 * 512, (pr % 2 + 1) * 512)
            act.wait_ge(S["ang_made"], pr + 1)
            if pr >= 2:
                act.wait_ge(S["back_made"], pr - 1)
            link.then(act.activation(sine[:, at], trig[:, at], ACT.Sin, scale=6.283185))
            link.then(act.activation(trig[:, at], trig[:, at], ACT.Abs))
            act.activation(cosine[:, at], trig[:, at], ACT.Sin, scale=-6.283185,
                           bias=par[:, 16 * ST:16 * ST + 1]).then_inc(S["cos_made"], 1)

        for i in range(2 * NH + 1):
            if i < 2 * NH:
                act.wait_ge(S["sc_max"], i + 1)
                for m in range(MT):
                    at = slice(i % 2 * 384 + m * P, i % 2 * 384 + (m + 1) * P + m * P)
                    last = act.activation(soft[:, at], soft[:, at], ACT.Exp,
                                          bias=sm[:, 64 + 2 * i + m:65 + 2 * i + m],
                                          accum_out=sm[:, 128 + 2 * i + m:129 + 2 * i + m])
                last.then_inc(S["sc_exp"], 1)
            if i == 10:
                waves(0)
            if i:
                j = i - 1
                act.wait_ge(S["pt_turned"], j + 1)
                act.activation(turned[:, j % 2 * 384:(j % 2 + 1) * 384], bank(2 + j % 2, 0, 384),
                               ACT.Copy).then_inc(S["pt_copied"], 1)
        for g in range(4):
            act.wait_ge(S["on_copied"], g + 1)
            act.activation(po_hi[:, g * 512:(g + 1) * 512], hval[:, :], ACT.Copy).then_inc(S["on_hi"], 1)
        def take_b(c):
            act.wait_ge(S["bt_made"], c + 1)
            if c:
                act.wait_ge(S["bu_made"], 2 * c)
            for v in range(2):
                act.activation(bt[:, v * 512:(v + 1) * 512], bank(4 + v), ACT.Copy).then_inc(S["bt_copied"], 1)

        def finish_y(c):
            act.wait_ge(S["y_sum"], c + 1)
            v = hval[:, c % 2 * T:(c % 2 + 1) * T]
            link.then(act.activation(v, v, ACT.Gelu_apprx_tanh))
            act.activation(chunk(ps_hi, c), v, ACT.Copy).then_inc(S["y_hi"], 1)

        take_b(0)
        for c in range(8):
            for pr in (2 * c, 2 * c + 1):
                if pr < 15:
                    waves(pr + 1)
                if pr % 2 == 0 and c:
                    finish_y(c - 1)
            if c < 7:
                take_b(c + 1)
        finish_y(7)
        def gate(dst, b, unit_count, sem_name):
            act.wait_ge(split_used, unit_count)
            act.activation(dst, bank(b, 0, T), ACT.Sigmoid).then_inc(S[sem_name], 1)

        mb = plan["merge"][1]
        sg_a, sg_b, sg_2 = (sgates[:, k * T:(k + 1) * T] for k in range(3))

        def merge(i, fresh):
            split("merge", 4, i, 0)
            if not fresh:
                gate(sg_2, 3, mb + 1 + i * 4, "mg_2")
            split("merge", 4, i, 1)
            split("merge", 4, i, 2)
            if not fresh:
                act.wait_ge(S["mg_sum"], i)
                act.activation(hid_hi[:, ds(i * T - T, T)], hval[:, 0:T], ACT.Copy).then_inc(S["mg_hi"], 1)
            gate(sg_a, 0, mb + 3 + i * 4, "mg_a")
            split("merge", 4, i, 3)
            gate(sg_b, 1, mb + 4 + i * 4, "mg_b")
        merge(0, True)
        with act.Fori(1, 16) as i:
            merge(i, False)
        gate(sg_2, 3, mb + 65, "mg_2")
        act.wait_ge(S["mg_sum"], 16)
        act.activation(hid_hi[:, 15 * T:16 * T], hval[:, 0:T], ACT.Copy).then_inc(S["mg_hi"], 1)
        for u in range(16):
            split("out2", 16, 0, u)
            if u == 12:
                squares(6, f_nat, 0)
                squares(6, f_nat, 1)
        square_sum(6, f_nat, 2)
        norm_begin(7, 4)
        ffn(2, 8)
        square_sum(8, f_nat, 2)

    @block.vector
    def _(dve):
        link = Steps(dve, dve_step)
        dve.sem_inc(S["hid_made"], 2)
        dve.sem_inc(S["pair_d1"], 2)

        def split(name, per_body, i, u):
            before = plan[name][1]
            if name == "merge" and u == 0:
                dve.wait_ge(S["mg_half_hi"], i + 1)
                dve.tensor_tensor(w_lo[:, 0:HALF], stage[:, 0:HALF], w_hi[:, 0:HALF].bitcast(F32),
                                  ALU.subtract).then_inc(S["mg_half_lo"], 1)
                dve.wait_ge(hi_made, before + u + 1 + i * per_body)
                dve.tensor_tensor(w_lo[:, HALF:UNIT], stage[:, HALF:UNIT], w_hi[:, HALF:UNIT].bitcast(F32),
                                  ALU.subtract).then_inc(split_made, 1)
                return
            dve.wait_ge(hi_made, before + u + 1 + i * per_body)
            n = HALF if name == "merge" and u == 3 else UNIT
            part = slice(u % 2 * UNIT, u % 2 * UNIT + n)
            dve.tensor_tensor(w_lo[:, part], stage[:, u % SLOTS * UNIT:u % SLOTS * UNIT + n], w_hi[:, part].bitcast(F32),
                              ALU.subtract).then_inc(split_made, 1)

        def rest(dst, src, hi, signal):
            dve.tensor_tensor(dst, src, hi.bitcast(F32), ALU.subtract).then_inc(signal, 1)

        def inverse_rms(e):
            dve.wait_ge(S["norm_ssq"], pieces_before(e + 1))
            total = stats[:, 0:2]
            if PIECES[e] == 4:
                total = stats[:, 4:6]
                link.then(dve.tensor_tensor(total, stats[:, 0:2], stats[:, 2:4], ALU.add))
            dve.tensor_scalar(stats[:, 4:6], total, 1.0 / D, EPS, ALU.mult, ALU.add).then_inc(S["norm_var"], 1)
            dve.wait_ge(S["norm_std"], e + 1)
            dve.reciprocal(stats[:, 8:10], stats[:, 6:8]).then_inc(S["norm_rs"], 1)
            dve.wait_ge(S["norm_rs"], e + 1)

        def norm_scale(e):
            inverse_rms(e)
            dve.tensor_scalar(f_nat[:, 0:D], x_nat[:, 0:D], stats[:, 8:9], None, ALU.mult).then_inc(S["norm_xhat"], 1)

        def norm_finish(n, scale, shift):
            for g in range(9):
                if g < 8:
                    dve.wait_ge(S["norm_turned"], 8 * n + g + 1)
                    if g >= 2:
                        dve.wait_ge(S["norm_done"], 8 * n + g - 1)
                    for k in range(2):
                        dst = turn[:, g % 2 * 512 + k * T:g % 2 * 512 + (k + 1) * T]
                        src = bank(turn_bank(n, g), k * T, T)
                        c = 2 * g + k
                        if shift is None:
                            last = dve.tensor_scalar(dst, src, scale[:, c:c + 1], None, ALU.mult)
                        else:
                            last = dve.tensor_scalar(dst, src, scale[:, c:c + 1],
                                                     shift[:, c:c + 1], ALU.mult, ALU.add)
                    last.then_inc(S["norm_scaled"], 1)
                if g:
                    dve.wait_ge(S["norm_hi"], 8 * n + g)
                    at = slice((g - 1) * 512, g * 512)
                    rest(xt_lo[:, at], turn[:, (g - 1) % 2 * 512:((g - 1) % 2 + 1) * 512], xt_hi[:, at],
                         S["norm_done"])

        def ffn(n, finish, norm_rest):
            conv = ffn_w[n]["conv"]

            def take(part, half):
                half_done(dve, f"down{n}{part}", half)
                for m in range(MT):
                    dst = f_nat[:, m * D + half * HALF:m * D + (half + 1) * HALF]
                    if part == 0:
                        last = dve.tensor_copy(dst, rows_cols(half, m, swapped=True))
                    else:
                        last = dve.tensor_tensor(dst, dst, rows_cols(half, m), ALU.add)
                        if n:
                            last.then_inc(S["piece_made"], 1)
                            if m == 0:
                                continue
                            dve.wait_ge(S["piece_made"], pieces_before(2 * n + 2 if n == 1 else 8) + 2 * half)
                            dve.sem_inc(S["rows_taken"], 1)
                            return
                last.then_inc(S["rows_taken"], 1)

            for part, (f0, chunks) in enumerate(PARTS):
                name, q0 = f"up{n}{part}", n * FC + f0
                pb = PAIR_BANK[part]

                def split_down(u):
                    split(f"down{n}{part}", chunks, 0, u)

                def d1(j, s):
                    dve.wait_ge(S["pair_e1"], j + (q0 + 1))
                    if not conv:
                        dve.wait_ge(S["hid_made"], j + (q0 + 1))
                        dve.tensor_tensor(hval[:, s * T:(s + 1) * T], conv_a[:, s * T:(s + 1) * T],
                                          bank(pb + s, T, T), ALU.mult).then_inc(S["pair_d1"], 1)
                        return
                    for t, o in ((conv_a, 0), (conv_v, FC)):
                        a = bank(pb + s, 0 if o == 0 else T, T)
                        dve.scalar_tensor_tensor(
                            out=t[:, s * T + 1:(s + 1) * T], in0=a[:, 0:T - 1],
                            scalar=cols[:, ds(j + (C_CONV[0] + o + f0), 1)],
                            in1=t[:, s * T + 1:(s + 1) * T], op0=ALU.mult, op1=ALU.add).then_inc(S["conv_step"], 1)
                    dve.wait_ge(S["conv_step"], 2 * j + (2 * q0 + 2))
                    for t, o in ((conv_a, 0), (conv_v, FC)):
                        a = bank(pb + s, 0 if o == 0 else T, T)
                        last = dve.scalar_tensor_tensor(
                            out=t[:, s * T:(s + 1) * T - 1], in0=a[:, 1:T],
                            scalar=cols[:, ds(j + (C_CONV[2] + o + f0), 1)],
                            in1=t[:, s * T:(s + 1) * T - 1], op0=ALU.mult, op1=ALU.add)
                    last.then_inc(S["pair_d1"], 1)

                def d2(j, s):
                    dve.wait_ge(S["pair_e2"], j + (q0 + 1))
                    dve.wait_ge(S["hid_made"], j + (q0 + 1))
                    dve.tensor_tensor(hval[:, s * T:(s + 1) * T], conv_a[:, s * T:(s + 1) * T],
                                      conv_v[:, s * T:(s + 1) * T], ALU.mult).then_inc(S["pair_d2"], 1)

                def d3(j, s):
                    dve.wait_ge(S["pair_e3"], j + (q0 + 1))
                    rest(hid_lo[:, ds(j * T, T)], hval[:, s * T:(s + 1) * T], hid_hi[:, ds(j * T, T)],
                         S["hid_made"])

                up_phase(dve, lambda i, u: split(name, 4, i, u), d2 if conv else d3,
                         d3 if conv else nothing, d1, chunks, split_down,
                         pending=(lambda: take(0, 1)) if part else nothing,
                         norm_rest=nothing if part else norm_rest)
                for u in range(2, chunks):
                    split_down(u)
                    if u == chunks // 2 + 1:
                        take(part, 0)
                    if part and u == chunks // 2 + 5:
                        finish(0)
            take(1, 1)
            finish(1)

        crep = xt_hi[:, :].rearrange("p (k n) -> p k n", n=T)
        dve.wait_ge(S["crep_hi"], 1)
        dve.tensor_tensor(crep[:, :, 32:64], csilu[:, :].unsqueeze(2).to_broadcast([P, KC, 32]),
                          xt_hi[:, :].bitcast(F32).rearrange("p (k n) -> p k n", n=T)[:, :, 0:32],
                          ALU.subtract).then_inc(S["crep_made"], 1)

        def ada(i):
            for h in range(32):
                dve.wait_ge(hi_made, 32 * i + (h + 1))
                at = slice(h % 4 * HALF, (h % 4 + 1) * HALF)
                dve.tensor_tensor(w_lo[:, at], stage[:, h % 8 * HALF:(h % 8 + 1) * HALF],
                                  w_hi[:, at].bitcast(F32), ALU.subtract).then_inc(split_made, 1)
        ada(0)
        norm_scale(0)
        with dve.Fori(1, 6) as i:
            ada(i)
        split("in_tiles", 4, 0, 0)
        dve.wait_ge(S["tab_turned"], 1)
        for t, q in enumerate(TABLE_ROWS):
            last = dve.tensor_copy(cols[:, t * P:t * P + q], bank(5 + t // 4, t % 4 * P, q))
        last.then_inc(S["cols_made"], 1)
        dve.wait_ge(S["cols_made"], 1)
        dve.wait_ge(S["mod_turned"], 1)
        dve.tensor_tensor(mod[:, :], bank(7, 0, 96), cols[:, 0:96], ALU.add).then_inc(S["mod_made"], 1)
        dve.wait_ge(S["mod_made"], 1)
        for b in range(2):
            last = dve.scalar_tensor_tensor(out=scale_cols[:, b * KC:(b + 1) * KC],
                                            in0=mod[:, 16 + 48 * b:32 + 48 * b], scalar=1.0,
                                            in1=cols[:, C_N1 + KC * b:C_N1 + KC * (b + 1)],
                                            op0=ALU.add, op1=ALU.mult)
        link.then(last)
        norm_finish(0, scale_cols[:, 0:KC], mod[:, 0:16])
        for u in range(1, 4):
            split("in_tiles", 4, 0, u)
        with dve.Fori(1, 4) as i:
            for u in range(4):
                split("in_tiles", 4, i, u)
        dve.memset(v_one[:, :].rearrange("p (k n) -> p k n", n=257)[:, :, 256:257], 1.0)
        for u in range(16):
            split("in_rows", 16, 0, u)
        dve.wait_ge(S["wg_split_hi"], 1)
        dve.tensor_tensor(wg_lo[:, 0:KC * 16].rearrange("p (k n) -> p k n", n=16),
                          wg_raw[:, :].rearrange("p (k n) -> p k n", n=48)[:, :, 0:16],
                          wg_hi[:, 0:KC * 16].bitcast(F32).rearrange("p (k n) -> p k n", n=16),
                          ALU.subtract).then_inc(S["wg_split"], 1)
        copy_gate_rows(dve, 16, 0)
        dve.wait_ge(S["g_made"], 1)
        dve.tensor_copy(g_nat[:, 0:32], bank(0, T, 32)).then_inc(S["g_copied"], 1)
        dve.wait_ge(S["gt_made"], 1)
        dve.wait_ge(S["const_in"], 32)
        for k in range(4):
            last = dve.tensor_scalar(grow[:, k * T:(k + 1) * T], ps[0:4, 1024 + k * T:1024 + (k + 1) * T],
                                     bgate[0:4, k:k + 1], None, ALU.add)
        last.then_inc(S["grow_made"], 1)
        dve.wait_ge(S["grow_made"], 1)
        igates = grow[:, :].rearrange("h (d k t) -> h k d t", d=2, k=2)[:, 0]
        fgates = grow[:, :].rearrange("h (d k t) -> h k d t", d=2, k=2)[:, 1]
        two = lambda a: a.rearrange("h (d t) -> h d t", d=2)
        dve.wait_ge(S["f_exp"], 1)
        dve.tensor_scalar(crow[:, :], crow[:, :], 1.0, None, ALU.add).then_inc(S["f_add"], 1)
        dve.wait_ge(S["f_ln"], 1)
        link.then(dve.scalar_tensor_tensor(out=two(lfrow[:, :]), in0=fgates, scalar=0.0,
                                           in1=two(crow[:, :]), op0=ALU.min, op1=ALU.subtract))

        def way(t, k, d):
            r = t[:, k * T:(k + 1) * T]
            return r if d == 0 else r[:, ::-1]
        for d in range(2):
            last = dve.tensor_tensor_scan(way(rows1, 2 + d, d), ones1[:, :], way(lfrow, d, d), 0.0,
                                          ALU.mult, ALU.add)
        link.then(last)
        link.then(dve.tensor_tensor(two(rows1[:, 0:512]), igates, two(rows1[:, 512:1024]), ALU.subtract))
        for d in range(2):
            last = dve.tensor_tensor_scan(way(rows1, 4 + d, d), ones1[:, :], way(rows1, d, d), NEG,
                                          ALU.mult, ALU.max)
        link.then(last)
        dve.tensor_tensor(rows1[:, 512:1024], rows1[:, 512:1024], rows1[:, 1024:1536],
                          ALU.add).then_inc(S["rows_made"], 1)
        for g in range(4):
            dve.wait_ge(S["four2"], g + 1)
            dve.tensor_copy(turn[:, g % 2 * 512:(g % 2 + 1) * 512], bank(4 + g)).then_inc(S["four2_copied"], 1)
            dve.wait_ge(S["four2_hi"], g + 1)
            at = slice(g * 512, (g + 1) * 512)
            rest(xt_lo[:, at], turn[:, g % 2 * 512:(g % 2 + 1) * 512], xt_hi[:, at], S["mix_lo"])
        dve.wait_ge(S["ec_made"], 1)
        dve.tensor_copy(ecols[:, :], bank(2, 0, 32)).then_inc(S["ec_copied"], 1)
        dve.wait_ge(S["ec_copied"], 1)
        dve.wait_ge(S["mask_in"], 16)
        dve.wait_ge(S["em_made"], 1)
        def exponents(h):
            dve.wait_ge(S["bcast_made"], h + 1)
            if h >= 2:
                dve.wait_ge(S["pt_made"], h - 1)
            for d in range(2):
                for s in range(2):
                    x = 2 * d + s
                    last = dve.scalar_tensor_tensor(
                        out=ex1[h % 2][:, x * T:(x + 1) * T], in0=mask1[:, x * T:(x + 1) * T],
                        scalar=ecols[:, x * 4 + h:x * 4 + h + 1], in1=bank(3, d * T, T),
                        op0=ALU.add, op1=ALU.subtract)
            last.then_inc(S["arg_made"], 1)

        exponents(0)
        for h in range(HEADS1):
            dve.wait_ge(S["score_made"], h + 1)
            dve.wait_ge(S["exp_made"], h + 1)
            if h:
                dve.wait_ge(S["num_made"], h)
            for d in range(2):
                for s in range(2):
                    x = 2 * d + s
                    last = dve.scalar_tensor_tensor(
                        out=pt1[:, x * T:(x + 1) * T], in0=bank(4 + h % 2, s * T, T),
                        scalar=DK ** -0.5, in1=ex1[h % 2][:, x * T:(x + 1) * T], op0=ALU.mult, op1=ALU.mult)
            last.then_inc(S["pt_made"], 1)
            if h < HEADS1 - 1:
                exponents(h + 1)
            if h >= 2:
                split("out1", 16, 0, h - 2)
            dve.wait_ge(S["num_made"], h + 1)
            for d in range(2):
                for m in range(MT):
                    x = 2 * d + m
                    last = dve.tensor_scalar(dcols[:, h * 8 + x:h * 8 + x + 1], bank(NUM[x], 256, 1), -1.0,
                                             None, ALU.mult)
            link.then(last)
            for x in range(4):
                last = dve.scalar_tensor_tensor(out=dcols[:, h * 8 + 4 + x:h * 8 + 5 + x],
                                                in0=bank(NUM[x], 256, 1),
                                                scalar=ecols[:, 16 + x * 4 + h:17 + x * 4 + h],
                                                in1=dcols[:, h * 8 + x:h * 8 + x + 1], op0=ALU.max, op1=ALU.max)
            link.then(last)
            dinv = dcols[:, 32 + h * 8:36 + h * 8]
            link.then(dve.reciprocal(dinv, dcols[:, h * 8 + 4:h * 8 + 8]))
            for m in range(MT):
                dst = h_nat[:, m * 1024 + h * 256:m * 1024 + (h + 1) * 256]
                last = dve.tensor_scalar(dst, bank(NUM[m], 0, 256), dinv[:, m:m + 1], None, ALU.mult)
            link.then(last)
            for m in range(MT):
                dst = h_nat[:, m * 1024 + h * 256:m * 1024 + (h + 1) * 256]
                last = dve.scalar_tensor_tensor(out=dst, in0=bank(NUM[2 + m], 0, 256),
                                                scalar=dinv[:, 2 + m:3 + m],
                                                in1=dst, op0=ALU.mult, op1=ALU.add)
            last.then_inc(S["num_taken"], 1)
        dve.wait_ge(S["h_ssq"], 8)
        dve.tensor_scalar(stats[:, 8:16], stats[:, 8:16], 1.0 / DV, EPS, ALU.mult, ALU.add).then_inc(S["h_var"], 1)
        dve.wait_ge(S["h_std"], 1)
        link.then(dve.reciprocal(stats[:, 24:32], stats[:, 16:24]))
        dve.wait_ge(S["row_in"], 16)
        for m in range(MT):
            for h in range(HEADS1):
                dst = h_nat[:, m * 1024 + h * 256:m * 1024 + (h + 1) * 256]
                last = dve.scalar_tensor_tensor(out=dst, in0=dst, scalar=stats[:, 24 + m * 4 + h:25 + m * 4 + h],
                                                in1=row[:, 1024 + h * 256:1024 + (h + 1) * 256], op0=ALU.mult, op1=ALU.mult)
        last.then_inc(S["row_used"], 1)
        dve.wait_ge(S["row_used"], 1)
        dve.wait_ge(S["rows_taken"], 2)
        dve.tensor_tensor(h_nat[:, :], h_nat[:, :], o_sig[:, :], ALU.mult).then_inc(S["h_done"], 1)
        split("out1", 16, 0, 2)
        for g in range(4):
            if g == 2:
                split("out1", 16, 0, 3)
            dve.wait_ge(S["ym_turned"], g + 1)
            if g >= 2:
                dve.wait_ge(S["mix_lo"], 3 + g)
            dve.tensor_copy(turn[:, g % 2 * 512:(g % 2 + 1) * 512], bank(4 + g)).then_inc(S["ym_copied"], 1)
            dve.wait_ge(S["ym_hi"], g + 1)
            at = slice((4 + g) * 512, (5 + g) * 512)
            rest(xt_lo[:, at], turn[:, g % 2 * 512:(g % 2 + 1) * 512], xt_hi[:, at], S["mix_lo"])
        def take_out1(half):
            half_done(dve, "out1", half)
            dve.wait_ge(S["row_in"], 32)
            at = [slice(m * D + half * HALF, m * D + (half + 1) * HALF) for m in range(MT)]
            for m in range(MT):
                last = dve.tensor_tensor(f_nat[:, at[m]], rows_cols(half, m),
                                         row[:, half * HALF:(half + 1) * HALF], ALU.mult)
            last.then_inc(S["rows_taken"], 1)
            dve.wait_ge(S["rows_taken"], 2 * rows_index["out1"] + half + 1)
            for m in range(MT):
                dve.tensor_tensor(x_nat[:, at[m]], x_nat[:, at[m]], f_nat[:, at[m]],
                                  ALU.add).then_inc(S["piece_made"], 1)
            dve.wait_ge(S["piece_made"], 2 * half + 2)
        for u in range(4, 16):
            split("out1", 16, 0, u)
            if u == 9:
                take_out1(0)
        take_out1(1)
        dve.sem_inc(S["x_made"], 1)
        dve.sem_inc(S["row_used"], 1)
        norm_scale(1)

        def finish0(half):
            dve.wait_ge(S["rows_taken"], 7 + half)
            dve.wait_ge(S["row_in"], 48)
            at = [slice(m * D + half * HALF, m * D + (half + 1) * HALF) for m in range(MT)]
            for m in range(MT):
                last = dve.tensor_tensor(f_nat[:, at[m]], f_nat[:, at[m]], row[:, half * HALF:(half + 1) * HALF],
                                         ALU.mult)
            link.then(last)
            if half:
                dve.sem_inc(S["row_used"], 1)
            for m in range(MT):
                dve.tensor_tensor(x_nat[:, at[m]], x_nat[:, at[m]], f_nat[:, at[m]],
                                  ALU.add).then_inc(S["piece_made"], 1)
            dve.wait_ge(S["piece_made"], pieces_before(2) + 2 * half)
            if half:
                dve.sem_inc(S["x_made"], 1)
        ffn(0, finish0, lambda: norm_finish(1, scale_cols[:, KC:2 * KC], mod[:, 48:64]))
        inverse_rms(2)
        dve.wait_ge(S["row_in"], 64)
        for m in range(MT):
            at = slice(m * D, (m + 1) * D)
            dve.scalar_tensor_tensor(out=x_nat[:, at], in0=x_nat[:, at], scalar=stats[:, 8 + m:9 + m],
                                     in1=row[:, :], op0=ALU.mult, op1=ALU.mult).then_inc(S["piece_made"], 1)
        dve.wait_ge(S["piece_made"], pieces_before(4) - 2)
        dve.sem_inc(S["row_used"], 1)
        dve.sem_inc(S["x_made"], 1)

        def post_norm(e, n_rows, weight, half):
            dve.wait_ge(S["row_in"], 16 * n_rows)
            for m in range(MT):
                at = slice(m * D + half * HALF, m * D + (half + 1) * HALF)
                dve.wait_ge(S["norm_ssq"], pieces_before(e) + 2 * half + m + 1)
                last = dve.tensor_tensor(f_nat[:, at], f_nat[:, at], row[:, half * HALF:(half + 1) * HALF], ALU.mult)
            link.then(last)
            if not half:
                return
            dve.sem_inc(S["row_used"], 1)
            inverse_rms(e)
            link.then(dve.tensor_scalar(stats[:, 10:12], stats[:, 8:10], weight, None, ALU.mult))
            for m in range(MT):
                at = slice(m * D, (m + 1) * D)
                last = dve.scalar_tensor_tensor(out=x_nat[:, at], in0=f_nat[:, at], scalar=stats[:, 10 + m:11 + m],
                                                in1=x_nat[:, at], op0=ALU.mult, op1=ALU.add).then_inc(S["piece_made"], 1)
            dve.wait_ge(S["piece_made"], pieces_before(e + 1))
            dve.sem_inc(S["x_made"], 1)
        norm_scale(3)
        ffn(1, lambda half: post_norm(4, 5, 0.5, half), lambda: norm_finish(2, cols[:, C_F1:C_F1 + KC], None))
        norm_scale(5)
        for u in range(4):
            split("in2", 4, 0, u)
            if u == 0:
                norm_finish(3, cols[:, C_MP:C_MP + KC], None)
        with dve.Fori(1, 4) as i:
            for u in range(4):
                split("in2", 4, i, u)
        dve.wait_ge(S["rev_made"], 1)
        dve.tensor_copy(rev_sb[:, :], bank(6, 0, 384, 16)).then_inc(S["rev_copied"], 1)
        dve.wait_ge(S["biasc_made"], 1)
        dve.wait_ge(S["x_made"], 4)
        dve.tensor_copy(biasc[:, :], bank(4, 0, 480)).then_inc(S["biasc_copied"], 1)
        dve.wait_ge(S["pos_made"], 1)
        dve.tensor_copy(pos_t[:, :], bank(5, 0, 32)).then_inc(S["pos_copied"], 1)
        with dve.Fori(4, 7) as i:
            for u in range(4):
                split("in2", 4, i, u)
        dve.wait_ge(S["wg_split_hi"], 2)
        dve.tensor_tensor(wg_lo[:, :], wg_raw[:, :], wg_hi[:, :].bitcast(F32), ALU.subtract).then_inc(S["wg_split"], 1)
        copy_gate_rows(dve, 48, 1)
        dve.wait_ge(S["tile_copied"], 48)
        dve.tensor_scalar(pt2[:, 8 * T:16 * T], pt2[:, 8 * T:16 * T], DH ** -0.5, None,
                          ALU.mult).then_inc(S["q_scaled"], 1)
        for br in range(2):
            src = pt2[:, (20 + 4 * br) * T:(22 + 4 * br) * T]
            dve.tensor_copy(swp[0:64, br * 512:(br + 1) * 512], src[64:128, :])
            last = dve.tensor_copy(swp[64:128, br * 512:(br + 1) * 512], src[0:64, :])
        last.then_inc(S["swapped"], 1)
        dve.wait_ge(S["pos_copied"], 1)
        for x, raw in enumerate((raw_k, raw_v)):
            for g in range(NKV):
                src = pt2[g % 2 * 64:g % 2 * 64 + 64, (16 + 2 * x + g // 2) * T:(17 + 2 * x + g // 2) * T]
                tok = src.rearrange("p (i l two) -> p two l i", l=8, two=2)
                pos = pos_t[g % 2 * 64:g % 2 * 64 + 64, :].rearrange("p (l two) -> p two l", two=2)
                for two in range(2):
                    dst = raw[two * 64:two * 64 + 64, :].rearrange("p (l c) -> p l c", c=60)
                    for lh in range(2):
                        last = dve.tensor_tensor(
                            dst[:, 8 * lh:8 * lh + 8, 15 * g:15 * g + 15], tok[:, two, :, lh:lh + 15],
                            pos[:, two, 8 * lh:8 * lh + 8].unsqueeze(2).to_broadcast([64, 8, 15]), ALU.add)
            last.then_inc(S["raw_made"], 1)
        for x in range(2):
            dve.wait_ge(S["ht_made"], x + 1)
            dve.tensor_copy(hid_t[:, x * 120:(x + 1) * 120], bank(x, 0, 120)).then_inc(S["ht_copied"], 1)
        dve.wait_ge(S["kv_made"], 1)
        dve.tensor_copy(kc_t[:, :], bank(2, 0, 60))
        dve.tensor_copy(vc_n[:, :], bank(3, 0, 256, 15)).then_inc(S["kv_copied"], 1)
        for m in range(MT):
            v = cmp_s[:, m * 240:(m + 1) * 240].rearrange("p (h i) -> p h i", i=15)
            mx = sm[:, m * 16:(m + 1) * 16]
            wide = lambda a: a.unsqueeze(2).to_broadcast([P, NH, NCMP])
            dve.wait_ge(S["cs_made"], m + 1)
            dve.wait_ge(S["biasc_copied"], 1)
            for odd in range(2):
                last = dve.tensor_tensor(
                    v.rearrange("p (a two) i -> p two a i", two=2)[:, odd],
                    bank((4, 2)[odd] + m, 0, 120).rearrange("p (h i) -> p h i", i=15),
                    biasc[:, m * 240:(m + 1) * 240].rearrange("p (i h two) -> p two h i", h=8, two=2)[:, odd], ALU.add)
            link.then(last)
            link.then(dve.tensor_reduce(mx, v, AX.X, ALU.max))
            dve.tensor_tensor(v, v, wide(mx), ALU.subtract).then_inc(S["cs_max"], 1)
            dve.wait_ge(S["cs_exp"], m + 1)
            rs = sm[:, 32:48]
            link.then(dve.tensor_reduce(rs, v, AX.X, ALU.add))
            link.then(dve.reciprocal(rs, rs))
            gate = g_nat[:, m * 48:(m + 1) * 48].rearrange("p (h b) -> p b h", b=3)[:, 0]
            link.then(dve.tensor_tensor(rs, rs, gate, ALU.mult))
            if m == 0:
                link.then(dve.tensor_scalar(rs, rs, live[:, 0:1], None, ALU.mult))
            dve.tensor_tensor(v, v, wide(rs), ALU.mult).then_inc(S["cs_done"], 1)
            dve.wait_ge(S["cs_done"], m + 1)
        for x in range(4):
            dve.wait_ge(S["co_made"], x + 1)
            dve.tensor_copy(o_nat[:, x * 512:(x + 1) * 512], bank(6 + x % 2)).then_inc(S["co_copied"], 1)
        pc = lambda i: par[:, i * ST:(i + 1) * ST]
        a_im = cols[:, C_AIM:C_AIM + ST]
        tt = lambda o, a, b, op: dve.tensor_tensor(o, a, b, op)
        dve.wait_ge(S["wg_split"], 2)
        link.then(dve.memset(par[:, 16 * ST:16 * ST + 1], math.pi / 2))
        link.then(dve.tensor_scalar(pc(1), cols[:, C_ARE:C_ARE + ST], -1e-4, None, ALU.min))
        dve.wait_ge(S["p_dt"], 1)
        dve.tensor_tensor(pc(2), pc(1), pc(0), ALU.mult).then_inc(S["p_x"], 1)
        tt(pc(8), pc(1), pc(1), ALU.mult)
        tt(pc(9), a_im, a_im, ALU.mult)
        link.then(tt(pc(3), a_im, pc(0), ALU.mult))
        c1 = 6.28125
        c2 = math.floor((TWO_PI - c1) * 2 ** 20) / 2 ** 20
        c3 = TWO_PI - c1 - c2
        tt(pc(8), pc(8), pc(9), ALU.add)
        link.then(dve.tensor_scalar(pc(10), pc(3), 1 / TWO_PI, ROUND, ALU.mult, ALU.add))
        link.then(dve.tensor_scalar(pc(10), pc(10), ROUND, None, ALU.subtract))
        for c in (c1, c2, c3):
            link.then(dve.scalar_tensor_tensor(out=pc(3), in0=pc(10), scalar=-c, in1=pc(3), op0=ALU.mult, op1=ALU.add))
        link.then(dve.tensor_scalar(pc(5), pc(3), 1 / TWO_PI, 0.5, ALU.mult, ALU.min))
        dve.tensor_scalar(pc(5), pc(5), -0.5, None, ALU.max).then_inc(S["p_phi"], 1)
        dve.reciprocal(pc(9), pc(8))
        dve.wait_ge(S["p_mag"], 1)
        dve.wait_ge(S["p_sin"], 1)
        link.then(dve.tensor_scalar(pc(7), pc(7), -1.0, 1.0, ALU.mult, ALU.add))
        tt(pc(6), pc(6), pc(4), ALU.mult)
        link.then(tt(pc(7), pc(7), pc(4), ALU.mult))
        link.then(dve.tensor_scalar(pc(7), pc(7), -1.0, None, ALU.add))
        tt(pc(10), pc(7), pc(1), ALU.mult)
        tt(pc(11), pc(6), a_im, ALU.mult)
        tt(pc(12), pc(6), pc(1), ALU.mult)
        link.then(tt(pc(13), pc(7), a_im, ALU.mult))
        tt(pc(10), pc(10), pc(11), ALU.add)
        link.then(tt(pc(12), pc(12), pc(13), ALU.subtract))
        tt(pc(14), pc(10), pc(9), ALU.mult)
        link.then(tt(pc(15), pc(12), pc(9), ALU.mult))

        def angle(pr):
            base_at = pr % 2 * 512
            at = slice(base_at, base_at + 512)
            if pr >= 2:
                dve.wait_ge(S["cos_made"], pr - 1)
            for e in range(2):
                last = dve.tensor_scalar(trig[:, base_at + e * T:base_at + (e + 1) * T], trow[:, :],
                                         pc(5)[:, 2 * pr + e:2 * pr + e + 1], ROUND, ALU.mult, ALU.add)
            link.then(last)
            link.then(dve.tensor_scalar(trig[:, at], trig[:, at], ROUND, None, ALU.subtract))
            for e in range(2):
                part = slice(base_at + e * T, base_at + (e + 1) * T)
                last = dve.scalar_tensor_tensor(out=trig[:, part], in0=trow[:, :],
                                                scalar=pc(5)[:, 2 * pr + e:2 * pr + e + 1],
                                                in1=trig[:, part], op0=ALU.mult, op1=ALU.subtract)
            last.then_inc(S["ang_made"], 1)

        dve.wait_ge(S["strips_in"], 16)
        dve.wait_ge(S["co_copied"], 4)
        for i in range(2 * NH + 3):
            if i < 2 * NH:
                h = i % NH
                dve.wait_ge(S["sc_made"], i + 1)
                if i >= 2:
                    dve.wait_ge(S["pt_turned"], i - 1)
                for m in range(MT):
                    at = i % 2 * 384 + m * P
                    n = (m + 1) * P
                    last = dve.tensor_tensor_reduce(soft[:, at:at + n], bank(i % 2, m * P, n),
                                                    strips[:, h * T + T - n:(h + 1) * T], 1.0, -3e38, ALU.add,
                                                    ALU.max, sm[:, 2 * i + m:2 * i + m + 1])
                link.then(last)
                dve.tensor_scalar(sm[:, 64 + 2 * i:66 + 2 * i], sm[:, 2 * i:2 * i + 2], -1.0, None,
                                  ALU.mult).then_inc(S["sc_max"], 1)
            if i == 8:
                dve.wait_ge(S["s5_in"], 16 * N_S5)
                angle(0)
            if i >= 6 and (i - 6) % 4 == 0:
                take4(dve, link, (i - 6) // 4)
        for g in range(4):
            dve.wait_ge(S["on_turned"], g + 1)
            if g:
                dve.wait_ge(S["on_lo"], g)
            dve.tensor_copy(hval[:, :], bank(g)).then_inc(S["on_copied"], 1)
            dve.wait_ge(S["on_hi"], g + 1)
            at = slice(g * 512, (g + 1) * 512)
            rest(po_lo[:, at], hval[:, :], po_hi[:, at], S["on_lo"])
        dve.memset(cw[:, :], 0.0)
        def make_c(c):
            dve.wait_ge(S["bt_made"], c + 1)
            if c >= 2:
                dve.wait_ge(S["y_made"], 2 * (c - 1))
            cr, ci = bank(6, 0, P), bank(6, P, P)
            f = [pc(14 + v)[:, 4 * c:4 * c + 4].unsqueeze(2).to_broadcast([P, 4, 32]) for v in range(2)]
            b3 = lambda a: a.rearrange("p (j n) -> p j n", n=32)
            t = [ct[:, k * P:(k + 1) * P] for k in range(4)]
            for o, a, b in ((0, cr, 0), (1, ci, 1), (2, cr, 1), (3, ci, 0)):
                last = tt(b3(t[o]), b3(a), f[b], ALU.mult)
            link.then(last)
            tt(t[0], t[0], t[1], ALU.subtract)
            link.then(tt(t[2], t[2], t[3], ALU.add))
            base_at = (c % 2) * 1536
            for k, (a, sign) in enumerate(((t[0], 1.0), (t[0], -1.0), (t[2], -1.0))):
                whole = cw[:, base_at + k * 512:base_at + (k + 1) * 512]
                for jj in range(4):
                    dst = whole[:, jj * P + jj * 32:jj * P + jj * 32 + 32]
                    last = dve.scalar_tensor_tensor(out=dst, in0=a[:, jj * 32:(jj + 1) * 32], scalar=sign,
                                                    in1=cmask[:, :], op0=ALU.mult, op1=ALU.mult)
            last.then_inc(S["cw_made"], 1)
            dve.wait_ge(S["cw_made"], c + 1)

        def sum_y(c):
            dve.wait_ge(S["y_made"], 2 * c + 2)
            if c >= 2:
                dve.wait_ge(S["y_lo"], c - 1)
            dve.scalar_tensor_tensor(out=hval[:, c % 2 * T:(c % 2 + 1) * T], in0=chunk(pt2, c),
                                     scalar=cols[:, C_SD + c:C_SD + c + 1], in1=bank(7, 0, T),
                                     op0=ALU.mult, op1=ALU.add).then_inc(S["y_sum"], 1)

        def rest_y(c):
            dve.wait_ge(S["y_hi"], c + 1)
            rest(chunk(ps_lo, c), hval[:, c % 2 * T:(c % 2 + 1) * T], chunk(ps_hi, c), S["y_lo"])

        for c in range(8):
            make_c(c)
            for pr in (2 * c, 2 * c + 1):
                at = slice(pr % 2 * 512, (pr % 2 + 1) * 512)
                if pr < 15:
                    angle(pr + 1)
                dve.wait_ge(S["bu_made"], pr + 1)
                dve.wait_ge(S["cos_made"], pr + 1)
                if pr >= 1:
                    dve.wait_ge(S["scan_made"], pr)
                if pr >= 2:
                    dve.wait_ge(S["back_made"], pr - 1)
                br, bi = bank(2 * (pr % 2)), bank(2 * (pr % 2) + 1)
                tt(rot_r[:, :], br, cosine[:, at], ALU.mult)
                tt(z_r[:, at], bi, sine[:, at], ALU.mult)
                tt(rot_i[:, :], bi, cosine[:, at], ALU.mult)
                link.then(tt(z_i[:, at], br, sine[:, at], ALU.mult))
                tt(rot_r[:, :], rot_r[:, :], z_r[:, at], ALU.add)
                link.then(tt(rot_i[:, :], rot_i[:, :], z_i[:, at], ALU.subtract))
                for src, dst in ((rot_r, z_r), (rot_i, z_i)):
                    for e in range(2):
                        j = 2 * pr + e
                        part = slice(pr % 2 * 512 + e * T, pr % 2 * 512 + (e + 1) * T)
                        last = dve.tensor_tensor_scan(dst[:, part], pc(4)[:, j:j + 1].to_broadcast([P, T]),
                                                      src[:, e * T:(e + 1) * T], 0.0, ALU.mult, ALU.add)
                last.then_inc(S["scan_made"], 1)
                if pr % 2 == 0 and c:
                    sum_y(c - 1)
                if pr % 2 == 1 and c:
                    rest_y(c - 1)
        sum_y(7)
        rest_y(7)
        sg_a, sg_b, sg_2 = (sgates[:, k * T:(k + 1) * T] for k in range(3))
        ta, tb = (sgates[:, k * T:(k + 1) * T] for k in (3, 4))
        mb = plan["merge"][1]

        def branch_a(i):
            dve.wait_ge(S["mg_2"], i)
            dve.wait_ge(S["mg_a"], i)
            dve.tensor_tensor(ta, bank(2, 0, T), sg_2, ALU.mult).then_inc(S["mg_d"], 1)
            dve.wait_ge(S["mg_d"], i)
            dve.tensor_tensor(ta, ta, sg_a, ALU.mult).then_inc(dve_merge, 1)

        def both(i):
            dve.wait_ge(split_used, mb + 2 + i * 4)
            dve.wait_ge(S["mg_b"], i)
            dve.tensor_tensor(tb, bank(4, 0, T), sg_b, ALU.mult).then_inc(dve_merge, 1)
            dve.wait_ge(dve_merge, 2 * i)
            dve.tensor_tensor(hval[:, 0:T], ta, tb, ALU.add).then_inc(S["mg_sum"], 1)

        def rest_merge(i):
            dve.wait_ge(S["mg_hi"], i)
            rest(hid_lo[:, ds(i * T - T, T)], hval[:, 0:T], hid_hi[:, ds(i * T - T, T)], S["mixed_made"])
            dve.wait_ge(S["mixed_made"], i)

        def merge(i, fresh):
            split("merge", 4, i, 0)
            if not fresh:
                branch_a(i)
            split("merge", 4, i, 1)
            if not fresh:
                both(i)
            split("merge", 4, i, 2)
            if not fresh:
                rest_merge(i)
            split("merge", 4, i, 3)
        merge(0, True)
        with dve.Fori(1, 16) as i:
            merge(i, False)
        branch_a(16)
        both(16)
        rest_merge(16)
        def take_out2(half):
            half_done(dve, "out2", half)
            for m in range(MT):
                dve.tensor_copy(f_nat[:, m * D + half * HALF:m * D + (half + 1) * HALF],
                                rows_cols(half, m)).then_inc(S["piece_made"], 1)
            dve.wait_ge(S["piece_made"], pieces_before(6) + 2 * half)
            dve.sem_inc(S["rows_taken"], 1)
        for u in range(16):
            split("out2", 16, 0, u)
            if u == 9:
                take_out2(0)
            if u == 14:
                post_norm(6, 6, 1.0, 0)
        take_out2(1)
        post_norm(6, 6, 1.0, 1)
        norm_scale(7)
        ffn(2, lambda half: post_norm(8, 7, 0.5, half), lambda: norm_finish(4, cols[:, C_F2:C_F2 + KC], None))

    @block.tensor
    def _(pe):
        pe.sem_inc(split_used, 2)

        def tile_unit(name, per_body, i, u, dst, xh=xt_hi, xl=xt_lo, k0=0, n=KC, w0=0, waits=True, done=True,
                      norm_index=None, start=True, stop=True):
            if waits:
                pe.wait_ge(split_made, plan[name][1] + u + 1 + i * per_body)
            at = u % 2 * UNIT + w0
            for k in range(n):
                if norm_index is not None and k % 2 == 0:
                    pe.wait_ge(S["norm_done"], 8 * norm_index + k // 2 + 1)
                wh, wl = (w[:, at + k * P:at + (k + 1) * P] for w in (w_hi, w_lo))
                pe.matmul(dst, wh, chunk(xh, k0 + k), start=start and k == 0, stop=False)
                pe.matmul(dst, wh, chunk(xl, k0 + k), start=False, stop=False)
                last = pe.matmul(dst, wl, chunk(xh, k0 + k), start=False, stop=stop and k == n - 1)
            if done:
                last.then_inc(split_used, 1)
            return last

        def rows_half(name, per_half, half, u0, split0, xh=xt_hi, xl=xt_lo, swapped=False, hid_base=None,
                      units=None, mixed=False):
            for c in units or range(per_half):
                u = u0 + c
                if mixed:
                    pe.wait_ge(S["mix_lo"], c + 1)
                pe.wait_ge(split_made, split0 + c + 1)
                if hid_base is not None:
                    pe.wait_ge(S["hid_made"], hid_base + 2 * c + 2)
                for kk in range(2):
                    k = 2 * c + kk
                    for m in range(MT):
                        a, b = chunk(xh, k, m), chunk(xl, k, m)
                        st, en = k == 0, k == 2 * per_half - 1
                        at = u % 2 * UNIT + kk * HALF
                        for n in range(2):
                            wh, wl = (w[:, at + n * 512:at + (n + 1) * 512] for w in (w_hi, w_lo))
                            pe.matmul(rows_cols(half, m, n, 512, swapped), a, wh, start=st, stop=False)
                            pe.matmul(rows_cols(half, m, n, 512, swapped), a, wl, start=False, stop=False)
                        for n in range(2):
                            wh = w_hi[:, at + n * 512:at + (n + 1) * 512]
                            last = pe.matmul(rows_cols(half, m, n, 512, swapped), b, wh, start=False, stop=en)
                last.then_inc(split_used, 1)

        def rows_phase(name, per_half, xh=xt_hi, xl=xt_lo, swapped=False, hid_base=None):
            r = rows_index[name]
            if r:
                pe.wait_ge(S["rows_taken"], 2 * r)
            before = plan[name][1]
            if per_half % 2 == 0:
                with pe.Fori(0, 2) as half:
                    rows_half(name, per_half, half, 0, half * per_half + before, xh, xl, swapped, hid_base)
            else:
                for half in range(2):
                    rows_half(name, per_half, half, half * per_half, half * per_half + before, xh, xl, swapped, hid_base)

        def norm(n, groups=range(8)):
            pe.wait_ge(S["norm_xhat"], 2 * (n + 1))
            for g in groups:
                if g >= 4 and n:
                    pe.wait_ge(S["norm_scaled"], 8 * n + g - 3)
                for k in range(2):
                    for m in range(MT):
                        c = 2 * g + k
                        last = pe.transpose(bank(turn_bank(n, g), k * T + m * P, P),
                                            f_nat[:, m * D + c * P:m * D + (c + 1) * P], ident[:, :])
                last.then_inc(S["norm_turned"], 1)

        def ffn(n):
            for part, (f0, chunks) in enumerate(PARTS):
                q0 = n * FC + f0
                name = f"up{n}{part}"
                if part:
                    pe.wait_ge(S["rows_taken"], 2 * rows_index[f"down{n}0"] + 1)
                with pe.Fori(0, chunks // 2) as i:
                    for s in range(2):
                        pe.wait_ge(S["pair_d1"], q0 + 1 + s + 2 * i)
                        for v in range(2):
                            tile_unit(name, 4, i, 2 * s + v, bank(PAIR_BANK[part] + s, v * T, T),
                                      norm_index=None if part or s or v else NORM_OF[n])
                rows_phase(f"down{n}{part}", chunks // 2, hid_hi, hid_lo, part == 0, q0 + 2)

        pe.wait_ge(S["c_in"], 32)
        pe.transpose(bank(4, 0, KC), conv_a[0:16, 0:P], ident[0:16, 0:16]).then_inc(S["c_turned"], 1)
        pe.wait_ge(S["crep_made"], 1)
        with pe.Fori(0, 6) as i:
            for b in range(2):
                pe.wait_ge(S["ada_taken"], 2 * i + (b + 1))
                for k in range(KC):
                    pe.wait_ge(split_made, 32 * i + (16 * b + k + 1))
                    a = xt_hi[:, k * T:k * T + 64]
                    at = k % 4 * HALF
                    for n in range(2):
                        dst = bank(2 * b + n, 0, 512, 64)
                        pe.matmul(dst, a, w_hi[:, at + n * 512:at + (n + 1) * 512], start=k == 0, stop=False)
                        last = pe.matmul(dst, a, w_lo[:, at + n * 512:at + (n + 1) * 512], start=False,
                                         stop=k == KC - 1)
                    last.then_inc(split_used, 1)
        pe.wait_ge(S["tab_ready"], 1)
        pe.wait_ge(S["norm_xhat"], 2)
        for t, q in enumerate(TABLE_ROWS):
            last = pe.transpose(bank(5 + t // 4, t % 4 * P, q), rowtab[0:q, t * P:(t + 1) * P], ident[0:q, 0:q])
        last.then_inc(S["tab_turned"], 1)
        pe.wait_ge(S["ada_taken"], 14)
        norm(0, range(4))
        pe.wait_ge(S["modrow_in"], 32)
        for v, t in enumerate((conv_a, conv_v)):
            last = pe.matmul(bank(7, 0, 96), t[0:96, 0:P], ident[0:96, 0:96], start=v == 0, stop=v == 1)
        last.then_inc(S["mod_turned"], 1)
        pe.wait_ge(S["mod_made"], 1)
        norm(0, range(4, 8))
        with pe.Fori(0, 4) as i:
            for u in range(4):
                pe.wait_ge(S["tile_copied"], 4 * i + (u + 1))
                tile_unit("in_tiles", 4, i, u, bank(u, 0, T), norm_index=None if u else 0)
        pe.wait_ge(S["tile_copied"], 20)
        rows_phase("in_rows", 8)
        pe.wait_ge(S["wg_split"], 1)
        pe.wait_ge(S["rows_taken"], 1)
        gates(pe, 16, 0)
        pe.wait_ge(S["dft_in"], 32)
        pe.wait_ge(S["g_copied"], 1)

        def four1(g):
            if g >= 2:
                pe.wait_ge(S["four1_copied"], 2 * (g - 1))
            for m in range(MT):
                for k in range(2):
                    last = pe.matmul(bank(2 * (g % 2) + m), chunk(projt, 2 * g + k, m),
                                     dft1[:, k * 512:(k + 1) * 512], start=k == 0, stop=k == 1)
            last.then_inc(S["four1"], 1)

        four1(0)
        for k in range(4):
            for m in range(MT):
                last = pe.transpose(ps[0:4, 1024 + k * T + m * P:1024 + k * T + (m + 1) * P],
                                    g_nat[:, m * 16 + 4 * k:m * 16 + 4 * k + 4], ident[:, :])
        last.then_inc(S["gt_made"], 1)
        pe.wait_ge(S["rows_taken"], 2)
        pe.wait_ge(S["grow_made"], 1)
        for g in range(4):
            if g < 3:
                four1(g + 1)
            pe.wait_ge(S["four1_copied"], 2 * (g + 1))
            for c in range(2):
                for s in range(2):
                    for v in range(2):
                        a = s * 512 + v * T + c * P
                        last = pe.matmul(bank(4 + g, c * T, T), four[:, a:a + P],
                                         dft2[:, s * 512 + v * T:s * 512 + (v + 1) * T],
                                         start=s + v == 0, stop=s + v == 2)
            last.then_inc(S["four2"], 1)
        pe.wait_ge(S["rows_made"], 1)
        for r in range(4):
            for s in range(2):
                last = pe.transpose(bank(2, (2 * r + s) * 4, 4), rows1[:, r * T + s * P:r * T + (s + 1) * P],
                                    ident[0:4, 0:4])
        last.then_inc(S["ec_made"], 1)
        pe.wait_ge(S["const_in"], 32)

        def scores(h):
            if h:
                pe.wait_ge(S["arg_made"], h)
            pe.matmul(bank(3), sel1[:, h * P:(h + 1) * P], rows1[:, 1024:1536], start=True,
                      stop=True).then_inc(S["bcast_made"], 1)
            for s in range(2):
                last = pe.matmul(bank(4 + h % 2, s * T, T), chunk(projt, 12 + h, s), chunk(projt, 8 + h),
                                 start=True, stop=True)
            last.then_inc(S["score_made"], 1)

        scores(0)
        for h in range(HEADS1):
            if h < HEADS1 - 1:
                scores(h + 1)
            pe.wait_ge(S["pt_made"], h + 1)
            if h:
                pe.wait_ge(S["num_taken"], h)
            for d in range(2):
                for m in range(MT):
                    keys = [s for s in range(2) if (s <= m if d == 0 else s >= m)]
                    for s in keys:
                        x = 2 * d + s
                        last = pe.matmul(bank(NUM[2 * d + m], 0, 257), pt1[:, x * T + m * P:x * T + (m + 1) * P],
                                         v_one[:, s * 1028 + h * 257:s * 1028 + (h + 1) * 257],
                                         start=s == keys[0], stop=s == keys[-1])
            last.then_inc(S["num_made"], 1)
        pe.wait_ge(S["num_taken"], 4)
        at_out1 = plan["out1"][1]
        rows_half("out1", 8, 0, 0, at_out1, units=range(2), mixed=True)
        pe.wait_ge(S["h_done"], 1)
        for g in range(4):
            for k in range(2):
                for m in range(MT):
                    c = 2 * g + k
                    last = pe.transpose(bank(4 + g, k * T + m * P, P),
                                        h_nat[:, m * 1024 + c * P:m * 1024 + (c + 1) * P], ident[:, :])
            last.then_inc(S["ym_turned"], 1)
        rows_half("out1", 8, 0, 0, at_out1, units=range(2, 8), mixed=True)
        rows_half("out1", 8, 1, 8, at_out1 + 8)
        norm(1)
        ffn(0)
        norm(2)
        ffn(1)
        norm(3)
        def in2_tiles(i):
            for u in range(4):
                pe.wait_ge(S["tile_copied"], 4 * i + (u + 17))
                tile_unit("in2", 4, i, u, bank(u, 0, T), norm_index=None if u else 3)

        with pe.Fori(0, 3) as i:
            in2_tiles(i)
        pe.wait_ge(S["oh_in"], 64)
        pe.matmul(bank(6, 0, 384, 16), relb[:, :], oh_rev[:, :], start=True, stop=True).then_inc(S["rev_made"], 1)
        for m in range(MT):
            for i in range(NCMP):
                a = 255 + P * m - 16 * i - 31
                last = pe.matmul(bank(4, m * 240 + i * 16, 16), oh_fwd[:, a:a + P], relb[:, :],
                                 start=True, stop=True)
        last.then_inc(S["biasc_made"], 1)
        pe.wait_ge(S["small_in"], 16 * N_SMALL)
        pe.transpose(bank(5, 0, 32), pos2[:, :], ident[0:32, 0:32]).then_inc(S["pos_made"], 1)
        with pe.Fori(3, 7) as i:
            in2_tiles(i)
        pe.wait_ge(S["tile_copied"], 48)
        pe.wait_ge(S["wg_split"], 2)
        gates(pe, 48, 1)
        for br in range(2):
            for st in range(2):
                for c in range(2):
                    last = pe.transpose(bank(1 + br, st * T + c * P, P), chunk(pt2, 22 + 4 * br + c, st), ident[:, :])
        last.then_inc(S["vt_made"], 1)
        for x, raw in enumerate((raw_k, raw_v)):
            pe.wait_ge(S["raw_made"], x + 1)
            for u in range(2):
                pe.wait_ge(landed[2 * x + u], 16 * (plan["cmp"][0] // SLOTS + 1))
                for k in range(8):
                    kk = 8 * u + k
                    last = pe.matmul(bank(6 + x, 0, T, 60), raw[:, kk * 60:(kk + 1) * 60],
                                     stage[:, (2 * x + u) * UNIT + k * T:(2 * x + u) * UNIT + (k + 1) * T],
                                     start=kk == 0, stop=kk == 15)
                last.then_inc(direct_used, 1)
        pe.wait_ge(S["pos_copied"], 1)
        for x in range(2):
            pe.wait_ge(S["hn_gelu"], x + 1)
            for c in range(2):
                last = pe.transpose(bank(x, c * 60, 60), hid_n[:, x * T + c * P:x * T + (c + 1) * P], ident[0:60, 0:60])
            last.then_inc(S["ht_made"], 1)
        pe.wait_ge(S["ht_copied"], 2)
        for c in range(2):
            pe.matmul(bank(2, 0, 60), w2[:, c * P:(c + 1) * P], hid_t[:, c * 60:(c + 1) * 60], start=c == 0, stop=c == 1)
        for g in range(NKV):
            for c in range(2):
                last = pe.matmul(bank(3, g * DH, DH, 15), hid_t[:, 120 + c * 60 + g * 15:120 + c * 60 + (g + 1) * 15],
                                 w2[:, 2 * P + c * DH:2 * P + (c + 1) * DH], start=c == 0, stop=c == 1)
        last.then_inc(S["kv_made"], 1)
        pe.wait_ge(S["kv_copied"], 1)
        pe.wait_ge(S["q_scaled"], 1)
        for m in range(MT):
            for h in range(NH):
                half = slice(h % 2 * 64, h % 2 * 64 + 64)
                q = pt2[half, (8 + h // 2) * T + m * P:(8 + h // 2) * T + (m + 1) * P]
                last = pe.matmul(bank((4, 2)[h % 2] + m, h // 2 * 15, 15), q, kc_t[half, h // 4 * 15:(h // 4 + 1) * 15],
                                 start=True, stop=True)
            last.then_inc(S["cs_made"], 1)
        x = 0
        for m in range(MT):
            pe.wait_ge(S["cs_done"], m + 1)
            for q4 in range(4):
                if x >= 2:
                    pe.wait_ge(S["ct_copied"], x - 1)
                for j in range(4):
                    h = 4 * q4 + j
                    last = pe.transpose(bank(x % 2, j * P, P, 15), cmp_s[:, m * 240 + h * 15:m * 240 + (h + 1) * 15],
                                        ident[:, :])
                last.then_inc(S["ct_made"], 1)
                pe.wait_ge(S["ct_copied"], x + 1)
                if x % 2 == 0 and x >= 4:
                    pe.wait_ge(S["co_copied"], x // 2 - 1)
                for j in range(4):
                    h = 4 * q4 + j
                    last = pe.matmul(bank(6 + x // 2 % 2, (h % 8) * DH, DH), cmp_t[:, x % 2 * 512 + j * P:x % 2 * 512 + (j + 1) * P],
                                     vc_n[:, h // 4 * DH:(h // 4 + 1) * DH], start=True, stop=True)
                if q4 % 2:
                    last.then_inc(S["co_made"], 1)
                x += 1
        def key_tile(br, h):
            g = h // 4
            if g % 2 == h % 2:
                return pt2, 20 + 4 * br + g // 2
            return swp, 2 * br + g // 2

        pe.wait_ge(S["swapped"], 1)
        pe.wait_ge(S["vn_copied"], 2)
        for i in range(2 * NH + 2):
            if i < 2 * NH:
                br, h = i // NH, i % NH
                if i >= 2:
                    pe.wait_ge(S["sc_max"], i - 1)
                else:
                    pe.wait_ge(S["co_copied"], 4)
                half = slice(h % 2 * 64, h % 2 * 64 + 64)
                kt, kc = key_tile(br, h)
                for m in range(MT):
                    n = (m + 1) * P
                    last = pe.matmul(bank(i % 2, m * P, n), pt2[half, (8 + h // 2) * T + m * P:(8 + h // 2) * T + (m + 1) * P],
                                     kt[half, kc * T:kc * T + n], start=True, stop=True)
                last.then_inc(S["sc_made"], 1)
            if 1 <= i <= 2 * NH:
                j = i - 1
                pe.wait_ge(S["sc_exp"], j + 1)
                if j >= 2:
                    pe.wait_ge(S["pt_copied"], j - 1)
                for b in range(3):
                    last = pe.transpose(bank(2 + j % 2, b * P, P), soft[:, j % 2 * 384 + b * P:j % 2 * 384 + (b + 1) * P],
                                        ident[:, :])
                last.then_inc(S["pt_turned"], 1)
            if i >= 2:
                j = i - 2
                br, h = j // NH, j % NH
                pe.wait_ge(S["pt_copied"], j + 1)
                if j % 4 == 0 and j >= 8:
                    pe.wait_ge(S["av_taken"], j // 4 - 1)
                b, at = 4 + j // 4 % 2, j % 4 * P
                for m in range(MT):
                    for st in range(m + 1):
                        last = pe.matmul(bank(b, at + m * DH, DH), turned[:, j % 2 * 384 + (m + st) * P:j % 2 * 384 + (m + st + 1) * P],
                                         v_nat[:, br * 512 + st * T + h // 4 * DH:br * 512 + st * T + (h // 4 + 1) * DH],
                                         start=st == 0, stop=st == m)
                if j % 4 == 3:
                    last.then_inc(S["av_made"], 1)
        pe.wait_ge(S["o_added"], 8)
        for g in range(4):
            for k in range(2):
                for m in range(MT):
                    c = 2 * g + k
                    last = pe.transpose(bank(g, k * T + m * P, P), o_nat[:, m * 1024 + c * P:m * 1024 + (c + 1) * P],
                                        ident[:, :])
            last.then_inc(S["on_turned"], 1)
        def bring(c):
            pe.wait_ge(S["bn_made"], c + 1)
            if c:
                pe.wait_ge(S["bt_copied"], 2 * c)
                pe.wait_ge(S["cw_made"], c)
            else:
                pe.wait_ge(S["on_copied"], 4)
                pe.wait_ge(S["av_taken"], 8)
            for v in range(2):
                for jj in range(4):
                    last = pe.transpose(bank(4 + v, jj * P, P), bn[:, v * 512 + jj * P:v * 512 + (jj + 1) * P], ident[:, :])
            for v in range(2):
                last = pe.transpose(bank(6, v * P, P), cc[:, (v * 8 + c) * P:(v * 8 + c + 1) * P], ident[:, :])
            last.then_inc(S["bt_made"], 1)

        pe.wait_ge(S["s5_in"], 16 * N_S5)
        def drive(pr):
            c = pr // 2
            if pr % 2 == 0:
                pe.wait_ge(S["bt_copied"], 2 * c + 2)
            if pr >= 2:
                pe.wait_ge(S["scan_made"], pr - 1)
            for v in range(2):
                for e in range(2):
                    jj = 2 * (pr % 2) + e
                    last = pe.matmul(bank(2 * (pr % 2) + v, e * T, T), bt[:, v * 512 + jj * P:v * 512 + (jj + 1) * P],
                                     chunk(pt2, c), start=True, stop=True)
            last.then_inc(S["bu_made"], 1)

        def read(pr):
            c = pr // 2
            if pr % 2 == 0:
                pe.wait_ge(S["cw_made"], c + 1)
                if c:
                    pe.wait_ge(S["y_sum"], c)
            pe.wait_ge(S["back_made"], pr + 1)
            for e in range(2):
                jj = 2 * (pr % 2) + e
                for x, wsel in enumerate((0, 1, 2, 2)):
                    a = (c % 2) * 1536 + wsel * 512 + jj * P
                    last = pe.matmul(bank(7, 0, T), cw[:, a:a + P],
                                     backs[pr % 2][:, x * 512 + e * T:x * 512 + (e + 1) * T],
                                     start=pr % 2 + e + x == 0, stop=pr % 2 + e == 2 and x == 3)
            last.then_inc(S["y_made"], 1)

        bring(0)
        drive(0)
        drive(1)
        bring(1)
        for pr in range(16):
            if pr < 14:
                drive(pr + 2)
            read(pr)
            if pr % 2 and pr < 13:
                bring((pr + 3) // 2)
        pe.wait_ge(S["on_lo"], 4)
        pe.wait_ge(S["y_lo"], 8)

        def merge(i, fresh):
            for u in range(4):
                if u == 0:
                    pe.wait_ge(S["mg_half_lo"], i + 1)
                else:
                    pe.wait_ge(split_made, plan["merge"][1] + u + 1 + i * 4)
                if u == 0 and not fresh:
                    pe.wait_ge(S["mg_a"], i)
                if u == 1 and not fresh:
                    pe.wait_ge(S["mg_b"], i)
                if u == 2 and not fresh:
                    pe.wait_ge(S["mg_d"], i)
                if u == 3 and not fresh:
                    pe.wait_ge(S["mg_sum"], i)
                if u == 0:
                    tile_unit("merge", 4, i, u, bank(u, 0, T), n=8, waits=False, done=False, stop=False)
                    pe.wait_ge(split_made, plan["merge"][1] + 1 + i * 4)
                    tile_unit("merge", 4, i, u, bank(u, 0, T), k0=8, w0=HALF, n=8, waits=False, start=False)
                elif u == 1:
                    tile_unit("merge", 4, i, u, bank(u, 0, T), waits=False)
                elif u == 2:
                    tile_unit("merge", 4, i, u, bank(2, 0, T), ps_hi, ps_lo, n=8, waits=False, done=False)
                    tile_unit("merge", 4, i, u, bank(3, 0, T), ps_hi, ps_lo, n=8, w0=8 * P, waits=False)
                else:
                    tile_unit("merge", 4, i, u, bank(4, 0, T), po_hi, po_lo, n=8, waits=False)
        merge(0, True)
        with pe.Fori(1, 16) as i:
            merge(i, False)
        pe.wait_ge(S["mixed_made"], 16)
        rows_phase("out2", 8, hid_hi, hid_lo)
        norm(4)
        ffn(2)

    block_scope.__exit__(None, None, None)
    ctx.close()


def constants():
    t = np.arange(T)
    angle = 2 * np.pi * np.outer(t, t) / T
    cos, sin = np.cos(angle) / 16, np.sin(angle) / 16
    mask = np.zeros((P, 4, T), np.float32)
    for d in range(2):
        for s in range(2):
            src = s * P + np.arange(P)[:, None]
            dead = src > t[None] if d == 0 else src < t[None]
            mask[:, 2 * d + s][dead] = NEG
    sel = np.zeros((4, 4, P), np.float32)
    for h in range(4):
        sel[h, h] = 1
    def onehot(dist):
        d = np.maximum(dist, 0)
        far = 16 + (np.log(np.maximum(d, 1).astype(np.float32) / np.float32(16)) / np.float32(math.log(64))
                    * np.float32(16)).astype(np.int32)
        bucket = np.where(d < 16, d, np.minimum(far, 31))
        oh = np.zeros((33, dist.size), np.float32)
        oh[np.where(dist >= 0, bucket, 32), np.arange(dist.size)] = 1
        return oh
    rows = np.arange(P)
    return {
        "k_oh_rev": onehot(255 - np.arange(384)),
        "k_oh_fwd": onehot(np.arange(512) - 255),
        "k_live": (rows >= 31).astype(np.float32)[:, None],
        "k_trow": np.tile(np.arange(T, dtype=np.float32), (P, 1)),
        "k_cmask": (rows[:, None] // 64 == np.arange(32)[None] // 16).astype(np.float32),
        "k_ident": np.eye(P, dtype=np.float32),
        "k_dft1": np.concatenate([cos, sin], 1).astype(np.float32),
        "k_dft2": np.concatenate([cos, -sin], 1).astype(np.float32),
        "k_mask": mask,
        "k_sel": sel.reshape(4, 4 * P),
    }


_NAMES = [
    "x", "c", "w_ada", "b_ada", "norm1_w", "w_in", "b_gates", "mlstm_norm_w", "w_out", "norm2_w", "w_up",
    "w_conv", "b_conv", "w_down", "norm_f_w", "ffn1_pre_g_2", "ffn1_w_gate_2", "ffn1_w_up_2",
    "ffn1_w_down_2", "ffn1_post_g_2", "mix_pre_g_2", "w_in_2", "ssm_a_re_2", "ssm_a_im_2", "ssm_log_dt_2",
    "ssm_b_re_2", "ssm_b_im_2", "ssm_c_re_2", "ssm_c_im_2", "ssm_d_2", "ssm_glu_w1_2", "ssm_glu_w2_2",
    "cmp_pos_2", "cmp_k_w1_2", "cmp_k_w2_2", "cmp_v_w1_2", "cmp_v_w2_2", "nsa_w_o_2", "w_out_2",
    "mix_post_g_2", "ffn2_pre_g_2", "ffn2_w_gate_2", "ffn2_w_up_2", "ffn2_w_down_2", "ffn2_post_g_2",
    "rel_bias_2",
]
_LAYERED = {
    "ffn1_w_gate_2", "ffn1_w_up_2", "ffn1_w_down_2", "w_in_2", "ssm_glu_w1_2", "ssm_glu_w2_2",
    "cmp_pos_2", "cmp_k_w1_2", "cmp_k_w2_2", "cmp_v_w1_2", "cmp_v_w2_2", "nsa_w_o_2", "w_out_2",
    "ffn2_w_gate_2", "ffn2_w_up_2", "ffn2_w_down_2", "ssm_b_re_2", "ssm_b_im_2", "ssm_c_re_2", "ssm_c_im_2",
}


def declare(nc, arrays):
    I = {}
    for name, a in arrays.items():
        I[name] = nc.dram_tensor(f"in_{name}", a.shape, mybir.dt.from_np(a.dtype), kind="ExternalInput").ap()
        if name in _LAYERED:
            I[name] = I[name][0]
    return I, nc.dram_tensor("out_x", (1, T, D), F32, kind="ExternalOutput").ap()


def kernel(**inputs):
    import concourse.bacc as bacc
    from concourse.bass_utils import run_bass_kernel_spmd

    arrays = {n: np.ascontiguousarray(inputs[n]) for n in _NAMES}
    arrays.update(constants())
    nc = bacc.Bacc("TRN2", target_bir_lowering=False, num_devices=1)
    build(nc, *declare(nc, arrays))
    r = run_bass_kernel_spmd(nc, [{f"in_{n}": a for n, a in arrays.items()}], core_ids=[0])
    return r.results[0]["out_x"]
```
